# Optimizing a Trainium2 kernel written in Bass

```python
import math
import jax, jax.numpy as jnp
from jax import lax
import numpy as np

D_MODEL = 1024
BATCH = 1
SEQ = 256
DEPTH = 2

N_MIXERS = 2
N_META = 16
RMS_EPS = 1e-6

RET_HEADS = 4
RET_QK_DIM = D_MODEL // RET_HEADS
RET_V_DIM = 2 * D_MODEL // RET_HEADS
RET_CHUNK = 128
ROPE_BASE = 10000.0

LRU_WIDTH = D_MODEL
LRU_BLOCKS = 4
LRU_BLOCK_W = LRU_WIDTH // LRU_BLOCKS
LRU_C = 8.0
LRU_CONV_W = 4
LRU_CONV_LEFT = 2

FFN_HIDDEN = 3 * D_MODEL
FFN_CONV_W = 3
FFN_CONV_LEFT = 1

N_RET = (DEPTH + 1) // 2
N_LRU = DEPTH // 2

kernel_name = "hybrid_retention_rglru_convffn_encoder"

def rmsnorm(x, g):
    xf = x.astype(jnp.float32)
    y = xf * lax.rsqrt(jnp.mean(xf * xf, axis=-1, keepdims=True) + RMS_EPS)
    return (y * g.astype(jnp.float32)).astype(x.dtype)

def dwconv(x, w, b, left):
    K, C = w.shape
    y = lax.conv_general_dilated(
        x, w.astype(x.dtype)[:, None, :], window_strides=(1,),
        padding=[(left, K - 1 - left)], dimension_numbers=("NWC", "WIO", "NWC"),
        feature_group_count=C)
    return y + b.astype(x.dtype)

def rotary(x, pos):
    d = x.shape[-1]
    inv = ROPE_BASE ** (-jnp.arange(0, d, 2, dtype=jnp.float32) / d)
    ang = pos[:, None] * inv[None, :]
    cos = jnp.cos(ang)[None, :, None, :]
    sin = jnp.sin(ang)[None, :, None, :]
    x1, x2 = x[..., : d // 2], x[..., d // 2:]
    return jnp.concatenate([x1 * cos - x2 * sin, x2 * cos + x1 * sin], axis=-1)

def retention_one_direction(q, k, v, log_gamma, include_diag):
    B, H, Tp, dk = q.shape
    dv = v.shape[-1]
    C = RET_CHUNK
    N = Tp // C
    idx = jnp.arange(C, dtype=jnp.float32)
    diff = idx[:, None] - idx[None, :]
    mask = diff >= 0 if include_diag else diff > 0
    lg = log_gamma[:, None, None]
    intra_decay = jnp.where(mask[None], jnp.exp(lg * jnp.maximum(diff, 0.0)[None]), 0.0)
    q_decay = jnp.exp(log_gamma[:, None] * (idx + 1.0)[None])[..., None]
    k_decay = jnp.exp(log_gamma[:, None] * (C - 1.0 - idx)[None])[..., None]
    chunk_decay = jnp.exp(log_gamma * C)[:, None, None]

    def to_chunks(t):
        return t.reshape(B, H, N, C, t.shape[-1]).transpose(2, 0, 1, 3, 4)

    def body(R, inp):
        qc, kc, vc = inp
        s = jnp.einsum("bhid,bhjd->bhij", qc, kc) * intra_decay
        o = jnp.einsum("bhij,bhje->bhie", s, vc) + jnp.einsum("bhid,bhde->bhie", qc, R) * q_decay
        R = chunk_decay * R + jnp.einsum("bhjd,bhje->bhde", kc * k_decay, vc)
        return R, o

    R0 = jnp.zeros((B, H, dk, dv), jnp.float32)
    _, o = lax.scan(body, R0, (to_chunks(q), to_chunks(k), to_chunks(v)))
    return o.transpose(1, 2, 0, 3, 4).reshape(B, H, Tp, dv)

def retention_mixer(h, w_in, w_out, pos):
    B, T, _ = h.shape
    proj = h @ w_in
    q, k, v, g = jnp.split(proj, [D_MODEL, 2 * D_MODEL, 4 * D_MODEL], axis=-1)
    q = rotary(q.astype(jnp.float32).reshape(B, T, RET_HEADS, RET_QK_DIM), pos)
    k = rotary(k.astype(jnp.float32).reshape(B, T, RET_HEADS, RET_QK_DIM), pos) * (RET_QK_DIM ** -0.5)
    v = v.astype(jnp.float32).reshape(B, T, RET_HEADS, RET_V_DIM)
    pad = (-T) % RET_CHUNK
    def prep(t):
        return jnp.pad(t.transpose(0, 2, 1, 3), ((0, 0), (0, 0), (pad, 0), (0, 0)))
    q, k, v = prep(q), prep(k), prep(v)
    log_gamma = jnp.log1p(-jnp.exp2(-5.0 - jnp.arange(RET_HEADS, dtype=jnp.float32)))
    fwd = retention_one_direction(q, k, v, log_gamma, True)
    flip = lambda t: jnp.flip(t, axis=2)
    bwd = flip(retention_one_direction(flip(q), flip(k), flip(v), log_gamma, False))
    o = (fwd + bwd)[:, :, pad:].transpose(0, 2, 1, 3)
    mu = jnp.mean(o, axis=-1, keepdims=True)
    var = jnp.var(o, axis=-1, keepdims=True)
    o = ((o - mu) * lax.rsqrt(var + RMS_EPS)).reshape(B, T, RET_HEADS * RET_V_DIM)
    y = jax.nn.silu(g.astype(jnp.float32)) * o
    return y.astype(h.dtype) @ w_out

def rglru_one_direction(x, w_a, b_a, w_i, b_i, lam, reverse):
    B, T, R = x.shape
    xb = x.reshape(B, T, LRU_BLOCKS, LRU_BLOCK_W)
    ga = jnp.einsum("btnd,nde->btne", xb, w_a.astype(jnp.float32)).reshape(B, T, R) + b_a.astype(jnp.float32)
    gi = jnp.einsum("btnd,nde->btne", xb, w_i.astype(jnp.float32)).reshape(B, T, R) + b_i.astype(jnp.float32)
    r = jax.nn.sigmoid(ga)
    i = jax.nn.sigmoid(gi)
    log_a = -LRU_C * r * jax.nn.softplus(-lam.astype(jnp.float32))
    a = jnp.exp(log_a)
    u = jnp.sqrt(-jnp.expm1(2.0 * log_a)) * (i * x)

    def combine(e1, e2):
        a1, b1 = e1
        a2, b2 = e2
        return a1 * a2, a2 * b1 + b2

    _, hs = lax.associative_scan(combine, (a, u), reverse=reverse, axis=1)
    return hs

def rglru_mixer(h, w_in, conv_w, conv_b, w_a, b_a, w_i, b_i, lam, w_out):
    proj = h @ w_in
    gate, xr = jnp.split(proj, 2, axis=-1)
    xr = dwconv(xr, conv_w, conv_b, LRU_CONV_LEFT).astype(jnp.float32)
    y = (rglru_one_direction(xr, w_a[0], b_a[0], w_i[0], b_i[0], lam[0], False)
         + rglru_one_direction(xr, w_a[1], b_a[1], w_i[1], b_i[1], lam[1], True))
    y = y * jax.nn.gelu(gate.astype(jnp.float32), approximate=True)
    return y.astype(h.dtype) @ w_out

def conv_ffn(h, w_in, conv_w, conv_b, w_out):
    u = dwconv(h @ w_in, conv_w, conv_b, FFN_CONV_LEFT)
    val, gate = jnp.split(u, 2, axis=-1)
    return (jax.nn.gelu(gate, approximate=True) * val) @ w_out

def setup_inputs(seed: int = 0) -> dict:
    key = jax.random.key(seed)
    ks = jax.random.split(key, 20)
    D, R, F, NB, bw = D_MODEL, LRU_WIDTH, FFN_HIDDEN, LRU_BLOCKS, LRU_BLOCK_W
    nrm = jax.random.normal
    a0 = jax.random.uniform(ks[12], (N_LRU, 2, R), jnp.float32, 0.9, 0.999)
    p = a0 ** (1.0 / LRU_C)
    lam = jnp.log(p) - jnp.log1p(-p)
    return {
        "x": nrm(ks[0], (BATCH, SEQ, D), jnp.float32),
        "meta_tokens": nrm(ks[1], (N_META, D), jnp.float32),
        "norm_gains": 1.0 + 0.05 * nrm(ks[2], (DEPTH, 4, D), jnp.float32),
        "ret_w_in": nrm(ks[3], (N_RET, D, 6 * D), jnp.float32) * D ** -0.5,
        "ret_w_out": nrm(ks[4], (N_RET, 2 * D, D), jnp.float32) * (2 * D) ** -0.5,
        "lru_w_in": nrm(ks[5], (N_LRU, D, 2 * R), jnp.float32) * D ** -0.5,
        "lru_conv_w": nrm(ks[6], (N_LRU, LRU_CONV_W, R), jnp.float32) * LRU_CONV_W ** -0.5,
        "lru_conv_b": 0.01 * nrm(ks[7], (N_LRU, R), jnp.float32),
        "lru_w_a": nrm(ks[8], (N_LRU, 2, NB, bw, bw), jnp.float32) * bw ** -0.5,
        "lru_b_a": 0.01 * nrm(ks[9], (N_LRU, 2, R), jnp.float32),
        "lru_w_i": nrm(ks[10], (N_LRU, 2, NB, bw, bw), jnp.float32) * bw ** -0.5,
        "lru_b_i": 0.01 * nrm(ks[11], (N_LRU, 2, R), jnp.float32),
        "lru_lambda": lam,
        "lru_w_out": nrm(ks[13], (N_LRU, R, D), jnp.float32) * R ** -0.5,
        "ffn_w_in": nrm(ks[14], (DEPTH, D, 2 * F), jnp.float32) * D ** -0.5,
        "ffn_conv_w": nrm(ks[15], (DEPTH, FFN_CONV_W, 2 * F), jnp.float32) * FFN_CONV_W ** -0.5,
        "ffn_conv_b": 0.01 * nrm(ks[16], (DEPTH, 2 * F), jnp.float32),
        "ffn_w_out": nrm(ks[17], (DEPTH, F, D), jnp.float32) * F ** -0.5,
    }

def reference(x, meta_tokens, norm_gains, ret_w_in, ret_w_out, lru_w_in, lru_conv_w,
              lru_conv_b, lru_w_a, lru_b_a, lru_w_i, lru_b_i, lru_lambda, lru_w_out,
              ffn_w_in, ffn_conv_w, ffn_conv_b, ffn_w_out):
    B = x.shape[0]
    meta = jnp.broadcast_to(meta_tokens.astype(x.dtype)[None], (B, N_META, D_MODEL))
    h = jnp.concatenate([meta, x], axis=1)
    pos = jnp.arange(h.shape[1], dtype=jnp.float32)
    for i in range(DEPTH):
        g = norm_gains[i]
        j = i // N_MIXERS
        a = rmsnorm(h, g[0])
        if i % N_MIXERS == 0:
            m = retention_mixer(a, ret_w_in[j], ret_w_out[j], pos)
        else:
            m = rglru_mixer(a, lru_w_in[j], lru_conv_w[j], lru_conv_b[j], lru_w_a[j],
                            lru_b_a[j], lru_w_i[j], lru_b_i[j], lru_lambda[j], lru_w_out[j])
        h = h + rmsnorm(m, g[1])
        f = conv_ffn(rmsnorm(h, g[2]), ffn_w_in[i], ffn_conv_w[i], ffn_conv_b[i], ffn_w_out[i])
        h = h + rmsnorm(f, g[3])
    return h[:, N_META:]


_drawn_inputs = setup_inputs


def setup_inputs(seed=0):
    import zlib

    import numpy as np

    out = dict(_drawn_inputs(seed))
    spreads = {}
    factors = {'lru_b_a': 45.412, 'lru_b_i': 27.139, 'ffn_conv_b': 3.056}
    for name, (base, spread) in spreads.items():
        noise = np.random.default_rng([zlib.crc32(name.encode()), seed]).standard_normal(out[name].shape)
        drawn = base * np.exp(spread * noise) if base else spread * noise
        out[name] = __import__('jax').numpy.asarray(drawn.astype(out[name].dtype))
    for name, factor in factors.items():
        out[name] = (out[name] * factor).astype(out[name].dtype)
    return out
```

```python
from contextlib import ExitStack

import concourse.bass as bass
from concourse import mybir
import numpy as np

F32 = mybir.dt.float32
F16 = mybir.dt.float16
ALU = mybir.AluOpType
ACTF = mybir.ActivationFunctionType
AX_X = mybir.AxisListType.X

P = 128
BANK = 512
EPS = 1e-6
W_SCALE = 2.0 ** 6
A_SCALE = 2.0 ** 4
UNSCALE = 1.0 / (W_SCALE * A_SCALE)

D = 1024
SEQ = 256
META = 16
T = SEQ + META
DT = D // P
HEADS = 4
FFN = 3 * D
FT = FFN // P
LRU_TAPS, LRU_LEFT = 4, 2
TOK_TILES = [(0, P), (P, P), (2 * P, T - 2 * P)]
NTT = len(TOK_TILES)
HEAD_V = 2 * D // HEADS
DECAY_W = 2 * P + T

KC = 8
CW = 512
SUB = 4
RET_IN = [3 * h for h in range(HEADS)]
RET_OUT = 3 * HEADS
FFN_CHUNKS = 2 * FFN // CW
FFN_OUT_K = FFN // (KC * P)
FFN0_IN = RET_OUT + 4
FFN0_OUT = FFN0_IN + FFN_CHUNKS
LRU = FFN0_OUT + 2 * FFN_OUT_K
XR0, GW0, XR1, GW1, GT0, GT1, LRU_OUT = range(LRU, LRU + 7)
FFN1_IN = LRU_OUT + 2
FFN1_OUT = FFN1_IN + FFN_CHUNKS
CHUNKS = FFN1_OUT + 2 * FFN_OUT_K
RET_OUT_ORDER = [(0, 0), (0, 1), (1, 0), (1, 1)]

_order = ([("pre", 0)] + [("head", h) for h in range(HEADS)] + [("post", 0)]
          + [(w, i) for i in (1, 2) for w in ("pre", "post")] + [("pre", 3), ("post", 3)])
ESTIMATE = {which: n + 1 for n, which in enumerate(_order)}
MEAN = {which: n + 1 for n, which in enumerate(w for w in _order if w[0] != "head")}

Y_FFN = [HEADS, HEADS + FFN_CHUNKS + 2]
Y_LRU = HEADS + FFN_CHUNKS

PAR_ROWS = [8 * DT, 88, 4 * FT, 4 * FT, 4 * FT, 4 * FT]

T0_LRU_OUT = META - 2
T0_OUT = META


def ffn_first(layer):
    return 0 if layer == 0 else T0_LRU_OUT


def build(nc, x, meta, gains, ret_w_in, ret_w_out, lru_w_in, lru_conv_w, lru_conv_b, lru_w_a, lru_b_a,
          lru_w_i, lru_b_i, lru_lambda, lru_w_out, ffn_w_in, ffn_conv_w, ffn_conv_b, ffn_w_out,
          ident, ones, rope, decay, out):
    ctx = ExitStack()
    with ctx:
        def sb(name, shape, dt=F32):
            return ctx.enter_context(nc.sbuf_tensor(name, shape, dt))

        def sem(name):
            return ctx.enter_context(nc.semaphore(name))

        stage = [sb(f"stage{s}", [P, KC, CW]) for s in range(2)]
        w_hi = [sb(f"w_hi{s}", [P, KC, CW], F16) for s in range(2)]
        w_lo = [sb(f"w_lo{s}", [P, KC, CW], F16) for s in range(2)]
        hT = sb("hT", [P, DT, T])
        mT = sb("mT", [P, DT, T])
        sq = sb("sq", [P, DT, T])
        a_hi = sb("a_hi", [P, DT, T], F16)
        a_lo = sb("a_lo", [P, DT, T], F16)
        y_hi = sb("y_hi", [P, FT, T], F16)
        y_lo = sb("y_lo", [P, FT, T], F16)
        ident_sb = sb("ident_sb", [P, P])
        ones_sb = sb("ones_sb", [P, 2, P])
        rope_sb = sb("rope_sb", [P, 2, T])
        decay_sb = sb("decay_sb", [P, HEADS, DECAY_W])
        prow = sb("prow", [P, 6, P])
        par = sb("par", [P, 6, P])
        eps_sb = sb("eps_sb", [P, 1])
        rs0 = sb("rs0", [P, T])
        rs1 = sb("rs1", [P, T])
        rs = sb("rs", [P, T])
        lam = sb("lam", [P, 8, 16])
        spc = sb("spc", [P, 2, 16])
        work = sb("work", [P, 9 * 4 * T])
        work16 = sb("work16", [P, 14 * T + 6 * BANK], F16)

        off = 0

        def carve(*shape):
            nonlocal off
            n = int(np.prod(shape))
            v = work[:, off:off + n]
            off += n
            if len(shape) == 2:
                v = v.rearrange("p (a b) -> p a b", b=shape[1])
            if len(shape) == 3:
                v = v.rearrange("p (a b c) -> p a b c", b=shape[1], c=shape[2])
            return v
        x_in = work[:, 0:3 * D].rearrange("p (a b) -> p a b", b=D)
        rotp = carve(2, 2, T)
        rotq = carve(4, T)
        vs = carve(3, BANK)
        sT = rotq[:, 0:3, :]
        oT, gT = mT[:, 0:4, :], mT[:, 4:8, :]
        osq, vT = sq[:, 0:4, :], sq[:, 4:8, :]
        vsum = sb("vsum", [P, 3, 2])
        qk_hi = work16[:, 0:4 * T].rearrange("p (a b) -> p a b", b=T)
        qk_lo = work16[:, 4 * T:8 * T].rearrange("p (a b) -> p a b", b=T)
        v_hi = work16[:, 8 * T:8 * T + 3 * BANK].rearrange("p (a b) -> p a b", b=BANK)
        v_lo = work16[:, 8 * T + 3 * BANK:8 * T + 6 * BANK].rearrange("p (a b) -> p a b", b=BANK)
        s_hi = work16[:, 8 * T + 6 * BANK:11 * T + 6 * BANK].rearrange("p (a b) -> p a b", b=T)
        s_lo = work16[:, 11 * T + 6 * BANK:14 * T + 6 * BANK].rearrange("p (a b) -> p a b", b=T)
        off = 0
        u_val = carve(2, 2, T)
        u_gate = carve(2, 2, T)
        u_gelu = carve(2, 2, T)
        u_y = carve(2, 2, T)
        off = 0
        xc = carve(DT, T)
        lr = [carve(2, 2, T) for _ in range(2)]
        li = [carve(2, 2, T) for _ in range(2)]
        lth = carve(2, 2, T)
        la = carve(2, 2, T)
        lv = carve(2, 2, T)
        hf, hb = sq, mT
        assert off <= 9 * 4 * T
        ggel = work16[:, 0:2 * DT * T].bitcast(F32).rearrange("p (a b) -> p a b", b=T)
        xc_hi = work16[:, 0:DT * T].rearrange("p (a b) -> p a b", b=T)
        xc_lo = work16[:, DT * T:2 * DT * T].rearrange("p (a b) -> p a b", b=T)
        fin = work[:, 0:2 * D].rearrange("p (a b) -> p a b", b=D)

        ps = ctx.enter_context(nc.psum_tensor("ps", [P, 8, BANK], F32))
        X, Y = 0, 4
        GATE_SETS = [[Y, X, Y, X], [X, Y, X, Y]]
        STAT = X
        GN = X + 3

        def gain(norm, dt):
            return par[:, 0, norm * DT + dt:norm * DT + dt + 1]

        LC, LB, LBA, LBI, LL = 0, 32, 40, 56, 72

        def lpar(base, i):
            return par[:, 1, base + i:base + i + 1]

        def fpar(layer, tap, f):
            return par[:, 2 + 2 * layer + tap // 2, (tap % 2) * 2 * FT + f:(tap % 2) * 2 * FT + f + 1]

        def tiles(v):
            return v.rearrange("n (t p) -> (n t) p", p=P)

        param_loads = [(prow[0:8 * DT, 0, :], gains.rearrange("l n (t p) -> (l n t) p", p=P)),
                       (prow[LC:LB, 1, :], tiles(lru_conv_w[0])), (prow[LB:LBA, 1, :], tiles(lru_conv_b)),
                       (prow[LBA:LBI, 1, :], tiles(lru_b_a[0])), (prow[LBI:LL, 1, :], tiles(lru_b_i[0])),
                       (prow[LL:LL + 16, 1, :], tiles(lru_lambda[0]))]
        for layer in range(2):
            param_loads += [(prow[0:4 * FT, 2 + 2 * layer, :], tiles(ffn_conv_w[layer, 0:2])),
                            (prow[0:2 * FT, 3 + 2 * layer, :], tiles(ffn_conv_w[layer, 2:3])),
                            (prow[2 * FT:4 * FT, 3 + 2 * layer, :], tiles(ffn_conv_b[layer:layer + 1]))]

        x_landed = sem("x_landed")
        const_landed = sem("const_landed")
        table_landed = sem("table_landed")
        w_landed = [[sem(f"w_landed{s}_{j}") for j in range(2)] for s in range(2)]
        whi_made = sem("whi_made")
        wlo_made = sem("wlo_made")
        w_used = sem("w_used")
        xT_up = sem("xT_up")
        h_in = sem("h_in")
        par_up = sem("par_up")
        par_raw = sem("par_raw")
        par_ready = sem("par_ready")
        lam_exp = sem("lam_exp")
        eps_set = sem("eps_set")
        m_sq = sem("m_sq")
        m_scaled = sem("m_scaled")
        h_new = sem("h_new")
        h_sq = sem("h_sq")
        ms_up = sem("ms_up")
        rs_est = sem("rs_est")
        rs_made = sem("rs_made")
        a_raw = sem("a_raw")
        ahi_made = sem("ahi_made")
        alo_made = sem("alo_made")
        rot_done = sem("rot_done")
        qkhi_made = sem("qkhi_made")
        qklo_made = sem("qklo_made")
        v_out = sem("v_out")
        s_up = sem("s_up")
        vt_up = sem("vt_up")
        s_dec = sem("s_dec")
        shi_made = sem("shi_made")
        slo_made = sem("slo_made")
        vs_out = sem("vs_out")
        vmean = sem("vmean")
        vhi_made = sem("vhi_made")
        vlo_made = sem("vlo_made")
        g_silu = sem("g_silu")
        o_up = sem("o_up")
        o_sq = sem("o_sq")
        gn_up = sem("gn_up")
        y_raw = sem("y_raw")
        yhi_made = sem("yhi_made")
        ylo_made = sem("ylo_made")
        mid_tap = sem("mid_tap")
        conv_done = sem("conv_done")
        gelu_done = sem("gelu_done")
        fy_raw = sem("fy_raw")
        x_mid = sem("x_mid")
        x_conv = sem("x_conv")
        xhi_made = sem("xhi_made")
        xlo_made = sem("xlo_made")
        r_out = sem("r_out")
        rates = sem("rates")
        root = sem("root")
        ix_made = sem("ix_made")
        scanned = sem("scanned")
        gt_out = sem("gt_out")
        ly_raw = sem("ly_raw")
        fin_up = sem("fin_up")
        fin_out = sem("fin_out")
        stored = sem("stored")
        act_step = sem("act_step")
        dve_step = sem("dve_step")
        pool_step = sem("pool_step")

        def landed(c):
            gates = sum(g <= c and g % 2 == c % 2 for g in (GW0, GW1))
            return 32 * (c // 2 + 1) + 32 * gates

        def flat(w, c, q):
            return w[c % 2][:, 2 * q:2 * q + 2, :].rearrange("p a b -> p (a b)")

        block = ctx.enter_context(nc.Block())

        @block.sync
        def _(sp):
            sp.dma_start(x_in[0:META, 0, :], meta).then_inc(x_landed, 16)
            sp.dma_start(x_in[META:P, 0, :], x[0, 0:P - META, :]).then_inc(x_landed, 16)
            sp.dma_start(x_in[:, 1, :], x[0, P - META:2 * P - META, :]).then_inc(x_landed, 16)
            sp.dma_start(x_in[0:META, 2, :], x[0, 2 * P - META:SEQ, :]).then_inc(x_landed, 16)
            sp.dma_start(ident_sb[:], ident).then_inc(x_landed, 16)
            sp.dma_start(ones_sb[:], ones).then_inc(x_landed, 16)

            def load(c, pieces):
                s = c % 2
                for half in range(2):
                    if c >= 2:
                        sp.wait_ge(wlo_made, SUB * (c - 2) + 2 * half + 2)
                    views = pieces(half)
                    for dst, src in views:
                        sp.dma_start(dst, src).then_inc(w_landed[s][half], 32 // len(views))

            def rows(w, k0, half):
                k = k0 + half * KC // 2
                return w.rearrange("(k p) n -> p k n", p=P)[:, k:k + KC // 2, :]

            def half_slot(c, half):
                return stage[c % 2][:, half * KC // 2:(half + 1) * KC // 2, :]

            def load_plain(c, w, k0, n0):
                load(c, lambda half: [(half_slot(c, half), rows(w, k0, half)[:, :, n0:n0 + CW])])

            def load_pair(c, w, n0, n1):
                load(c, lambda half: [
                    (half_slot(c, half)[:, :, 0:CW // 2], rows(w, 0, half)[:, :, n0:n0 + CW // 2]),
                    (half_slot(c, half)[:, :, CW // 2:CW], rows(w, 0, half)[:, :, n1:n1 + CW // 2])])

            def load_gates(c, block0):
                def pieces(half):
                    n = block0 + half
                    to = half_slot(c, half).rearrange("p a b -> p (a b)").rearrange(
                        "p (d g k e) -> p d g k e", d=2, g=2, k=2)
                    return [(to[:, d, g, :, :], w[0, d, n].rearrange("(k p) e -> p k e", p=P))
                            for g, w in enumerate((lru_w_a, lru_w_i)) for d in range(2)]
                s = c % 2
                for half in range(2):
                    sp.wait_ge(wlo_made, SUB * (c - 2) + 2 * half + 2)
                    for n, (dst, src) in enumerate(pieces(half)):
                        sp.dma_start(dst, src).then_inc(w_landed[s][half], 16)

            wi, wo = ret_w_in[0], ret_w_out[0]
            for h in range(HEADS):
                load_pair(RET_IN[h], wi, h * 2 * P, D + h * 2 * P)
                if h == 0:
                    for dst, src in param_loads:
                        sp.dma_start(dst, src).then_inc(const_landed, 16)
                    sp.dma_start(rope_sb[:], rope).then_inc(table_landed, 16)
                    sp.dma_start(decay_sb[:], decay).then_inc(table_landed, 16)
                load_plain(RET_IN[h] + 1, wi, 0, 2 * D + h * HEAD_V)
                load_plain(RET_IN[h] + 2, wi, 0, 4 * D + h * HEAD_V)
            for n, (half, kg) in enumerate(RET_OUT_ORDER):
                load_plain(RET_OUT + n, wo, kg * KC, half * CW)

            def load_ffn(layer, first_in, first_out):
                for j in range(FFN_CHUNKS):
                    load_pair(first_in + j, ffn_w_in[layer], j * 2 * P, FFN + j * 2 * P)
                for n in range(2 * FFN_OUT_K):
                    load_plain(first_out + n, ffn_w_out[layer], (n % FFN_OUT_K) * KC, n // FFN_OUT_K * CW)

            load_ffn(0, FFN0_IN, FFN0_OUT)
            for c, n0 in ((XR0, D), (GW0, None), (XR1, D + CW), (GW1, None), (GT0, 0), (GT1, CW)):
                if n0 is None:
                    load_gates(c, 0 if c == GW0 else 2)
                else:
                    load_plain(c, lru_w_in[0], 0, n0)
            for half in range(2):
                load_plain(LRU_OUT + half, lru_w_out[0], 0, half * CW)
            load_ffn(1, FFN1_IN, FFN1_OUT)
            for b in range(4):
                sp.wait_ge(fin_out, b + 1)
                tt, half = b // 2, b % 2
                sp.dma_start(out[0, tt * P:(tt + 1) * P, half * BANK:(half + 1) * BANK],
                             fin[:, tt, half * BANK:(half + 1) * BANK]).then_inc(stored, 16)
            sp.wait_ge(stored, 64)

        @block.scalar
        def _(act):
            step = [0]

            def link(ins):
                step[0] += 1
                ins.then_inc(act_step, 1)
                act.wait_ge(act_step, step[0])

            def prep(c, q):
                if c >= CHUNKS:
                    return
                act.wait_ge(w_landed[c % 2][q // 2], landed(c))
                if c >= 2:
                    act.wait_ge(w_used, SUB * (c - 2) + q + 1)
                act.activation(flat(w_hi, c, q), flat(stage, c, q), ACTF.Copy,
                               scale=W_SCALE).then_inc(whi_made, 1)

            def estimate(bank, t0, up, n_up, n):
                act.wait_ge(up, n_up)
                if n > 1:
                    act.wait_ge(rs_made, n - 1)
                act.activation(rs0[:, t0:T], ps[:, bank, t0:T], ACTF.Abs_reciprocal_sqrt,
                               bias=eps_sb[:, 0:1]).then_inc(rs_est, 1)

            def pre_norm(i, t0):
                for dt in range(DT):
                    act.wait_ge(h_in if i == 0 else h_new, dt + 1 if i == 0 else (i - 1) * DT + dt + 1)
                    act.activation(sq[:, dt, t0:T], hT[:, dt, t0:T], ACTF.Square).then_inc(h_sq, 1)
                estimate(STAT, t0, ms_up, MEAN[("pre", i)], ESTIMATE[("pre", i)])
                for dt in range(DT):
                    act.wait_ge(a_raw, i * DT + dt + 1)
                    act.activation(a_hi[:, dt, t0:T], mT[:, dt, t0:T], ACTF.Copy).then_inc(ahi_made, 1)

            def out_squares(c, i, half, t0):
                act.wait_ge(w_used, SUB * (c + 1))
                for n in range(4):
                    act.activation(sq[:, half * 4 + n, t0:T], ps[:, (X, Y)[half] + n, t0:T], ACTF.Square,
                                   scale=UNSCALE).then_inc(m_sq, 1)

            act.wait_ge(eps_set, 1)
            for q in range(SUB):
                prep(0, q)
            pre_norm(0, 0)
            for q in range(SUB):
                prep(1, q)
            act.wait_ge(par_raw, 1)
            link(act.activation(lam[:, 0, :], par[:, 1, LL:LL + 16], ACTF.Abs))
            act.activation(lam[:, 1, :], lam[:, 0, :], ACTF.Exp, scale=-1.0).then_inc(lam_exp, 1)

            def head_y(h):
                act.wait_ge(y_raw, h + 1)
                act.activation(y_hi[:, 4 * h:4 * h + 4, :], oT, ACTF.Copy).then_inc(yhi_made, 1)

            for h in range(HEADS):
                c = RET_IN[h]
                prep(c + 2, 0)
                prep(c + 2, 1)
                act.wait_ge(rot_done, h + 1)
                if h:
                    act.wait_ge(s_up, h)
                act.activation(qk_hi, rotq, ACTF.Copy).then_inc(qkhi_made, 1)
                prep(c + 2, 2)
                prep(c + 2, 3)
                act.wait_ge(w_used, SUB * (c + 2))
                for n in range(4):
                    last = act.activation(vT[:, n, :], ps[:, Y + n, 0:T], ACTF.Copy, scale=UNSCALE * A_SCALE)
                last.then_inc(v_out, 1)
                if h:
                    estimate(GN, 0, gn_up, h, ESTIMATE[("head", h - 1)])
                prep(c + 3, 0)
                act.wait_ge(s_dec, h + 1)
                if h:
                    act.wait_ge(o_up, h)
                act.activation(s_hi[:, 0:2, :], sT[:, 0:2, :], ACTF.Copy)
                act.activation(s_hi[0:META, 2, :], sT[0:META, 2, :], ACTF.Copy).then_inc(shi_made, 1)
                act.wait_ge(vt_up, h + 1)
                for n, (_, m) in enumerate(TOK_TILES):
                    if h:
                        act.wait_ge(vlo_made, h)
                    act.activation(vs[0:m, n, :], ps[0:m, Y + n, :], ACTF.Copy,
                                   accum_out=vsum[0:m, n, 0:1]).then_inc(vs_out, 1)
                for n, (_, m) in enumerate(TOK_TILES):
                    act.wait_ge(vmean, NTT * h + n + 1)
                    act.activation(v_hi[0:m, n, :], vs[0:m, n, :], ACTF.Identity,
                                   bias=vsum[0:m, n, 1:2]).then_inc(vhi_made, 1)
                if h:
                    head_y(h - 1)
                for q in range(1, SUB):
                    prep(c + 3, q)
                prep(c + 4, 0)
                act.wait_ge(w_used, SUB * (c + 3))
                if h:
                    act.wait_ge(y_raw, h)
                for n in range(4):
                    last = act.activation(gT[:, n, :], ps[:, X + n, 0:T], ACTF.Silu, scale=UNSCALE)
                last.then_inc(g_silu, 1)
                prep(c + 4, 1)
                act.wait_ge(o_up, h + 1)
                if h:
                    act.wait_ge(yhi_made, h)
                    act.wait_ge(ylo_made, h)
                for n in range(4):
                    act.activation(oT[:, n, :], ps[:, Y + n, 0:T], ACTF.Copy, scale=1.0 / A_SCALE ** 2)
                for n in range(4):
                    last = act.activation(osq[:, n, :], ps[:, Y + n, 0:T], ACTF.Square,
                                          scale=1.0 / A_SCALE ** 2)
                last.then_inc(o_sq, 1)
                prep(c + 4, 2)
                prep(c + 4, 3)

            c = RET_OUT
            estimate(Y, 0, gn_up, HEADS, ESTIMATE[("head", HEADS - 1)])
            head_y(HEADS - 1)
            for q in range(SUB):
                prep(c + 2, q)
            out_squares(c + 1, 0, 0, 0)
            for q in range(SUB):
                prep(c + 3, q)
            for q in range(SUB):
                prep(c + 4, q)
            out_squares(c + 3, 0, 1, 0)
            estimate(STAT, 0, ms_up, MEAN[("post", 0)], ESTIMATE[("post", 0)])
            pre_norm(1, 0)
            for q in range(SUB):
                prep(c + 5, q)

            def ffn(layer, first_in, first_out, i):
                t0 = ffn_first(layer)
                for j in range(FFN_CHUNKS):
                    c, s, b = first_in + j, (X, Y)[j % 2], j % 2
                    n0 = layer * FFN_CHUNKS + j
                    act.wait_ge(w_used, SUB * (c + 1))
                    if n0 >= 2:
                        act.wait_ge(fy_raw, n0 - 1)
                    for n, u in ((0, u_val), (1, u_val), (2, u_gate), (3, u_gate)):
                        f = (FT if n >= 2 else 0) + 2 * j + n % 2
                        last = act.activation(u[:, b, n % 2, t0:T], ps[:, s + n, t0:T], ACTF.Identity,
                                              scale=fpar(layer, 1, f), bias=fpar(layer, 3, f))
                    last.then_inc(mid_tap, 1)
                    prep(c + 2, 0)
                    prep(c + 2, 1)
                    act.wait_ge(conv_done, n0 + 1)
                    act.activation(u_gelu[:, b, :, t0:T], u_gate[:, b, :, t0:T],
                                   ACTF.Gelu_apprx_tanh).then_inc(gelu_done, 1)
                    prep(c + 2, 2)
                    act.wait_ge(fy_raw, n0 + 1)
                    act.activation(y_hi[:, 2 * j:2 * j + 2, t0:T], u_y[:, b, :, t0:T],
                                   ACTF.Copy).then_inc(yhi_made, 1)
                    prep(c + 2, 3)
                to = 0 if layer == 0 else T0_OUT
                for n in range(2 * FFN_OUT_K):
                    c = first_out + n
                    if n == FFN_OUT_K - 1:
                        out_squares(c, i, 0, to)
                    if n < 2 * FFN_OUT_K - 1:
                        for q in range(SUB):
                            prep(c + 2, q)
                out_squares(c, i, 1, to)
                estimate(STAT, to, ms_up, MEAN[("post", i)], ESTIMATE[("post", i)])

            ffn(0, FFN0_IN, FFN0_OUT, 1)
            pre_norm(2, 0)
            for q in range(SUB):
                prep(LRU + 1, q)

            def lru_input(k, c, s):
                act.wait_ge(w_used, SUB * (c + 1))
                for n in range(4):
                    j = 4 * k + n
                    last = act.activation(xc[:, j, :], ps[:, s + n, 0:T], ACTF.Identity,
                                          scale=lpar(LC, LRU_LEFT * DT + j), bias=lpar(LB, j))
                last.then_inc(x_mid, 1)
                prep(c + 2, 0)
                prep(c + 2, 1)
                act.wait_ge(x_conv, k + 1)
                act.activation(xc_hi[:, 4 * k:4 * k + 4, :], xc[:, 4 * k:4 * k + 4, :],
                               ACTF.Copy).then_inc(xhi_made, 1)
                prep(c + 2, 2)
                prep(c + 2, 3)

            def lru_gates(k, c, sets):
                for nb in range(2):
                    blk = 2 * k + nb
                    for d in range(2):
                        g = 2 * blk + d
                        s = sets[2 * nb + d]
                        act.wait_ge(w_used, SUB * c + 2 * nb + d + 1)
                        if blk >= 2:
                            act.wait_ge(scanned, 2 * (blk - 2) + d + 1)
                        for m in range(2):
                            act.activation(lr[blk % 2][:, d, m, :], ps[:, s + m, 0:T], ACTF.Sigmoid,
                                           scale=UNSCALE, bias=lpar(LBA, d * DT + 2 * blk + m))
                        for m in range(2):
                            last = act.activation(li[blk % 2][:, d, m, :], ps[:, s + 2 + m, 0:T], ACTF.Sigmoid,
                                                  scale=UNSCALE, bias=lpar(LBI, d * DT + 2 * blk + m))
                        last.then_inc(r_out, 1)
                    act.wait_ge(r_out, 2 * blk + 2)
                    if blk:
                        act.wait_ge(scanned, 2 * blk)
                    pairs = [(d, m, d * DT + 2 * blk + m) for d in range(2) for m in range(2)]
                    for d, m, j in pairs:
                        act.activation(lth[:, d, m, :], lr[blk % 2][:, d, m, :], ACTF.Tanh,
                                       scale=spc[:, 0, j:j + 1])
                    for d, m, j in pairs:
                        last = act.activation(la[:, d, m, :], lr[blk % 2][:, d, m, :], ACTF.Exp,
                                              scale=spc[:, 1, j:j + 1])
                    last.then_inc(rates, 1)
                    act.wait_ge(rates, blk + 1)
                    for d in range(2):
                        act.activation(lr[blk % 2][:, d], lth[:, d], ACTF.Sqrt).then_inc(root, 1)
                    prep(c + 2, 2 * nb)
                    prep(c + 2, 2 * nb + 1)

            act.wait_ge(par_ready, 2)
            lru_input(0, XR0, X)
            lru_gates(0, GW0, GATE_SETS[0])
            lru_input(1, XR1, Y)
            lru_gates(1, GW1, GATE_SETS[1])
            for k, c in ((0, GT0), (1, GT1)):
                act.wait_ge(w_used, SUB * (c + 1))
                for n in range(4):
                    last = act.activation(ggel[:, 4 * k + n, :], ps[:, (X, Y)[k] + n, 0:T],
                                          ACTF.Gelu_apprx_tanh, scale=UNSCALE)
                last.then_inc(gt_out, 1)
                prep(c + 2, 0)
                prep(c + 2, 1)
                act.wait_ge(ly_raw, k + 1)
                act.activation(y_hi[:, 4 * k:4 * k + 4, :], xc[:, 4 * k:4 * k + 4, :],
                               ACTF.Copy).then_inc(yhi_made, 1)
                prep(c + 2, 2)
                prep(c + 2, 3)
            out_squares(LRU_OUT, 2, 0, T0_LRU_OUT)
            for q in range(SUB):
                prep(LRU_OUT + 2, q)
            out_squares(LRU_OUT + 1, 2, 1, T0_LRU_OUT)
            estimate(STAT, T0_LRU_OUT, ms_up, MEAN[("post", 2)], ESTIMATE[("post", 2)])
            pre_norm(3, T0_LRU_OUT)
            for q in range(SUB):
                prep(LRU_OUT + 3, q)
            ffn(1, FFN1_IN, FFN1_OUT, 3)
            for b in range(4):
                act.wait_ge(fin_up, b + 1)
                act.activation(fin[:, b // 2, b % 2 * BANK:(b % 2 + 1) * BANK], ps[:, X + b, :],
                               ACTF.Copy).then_inc(fin_out, 1)

        @block.vector
        def _(dve):
            step = [0]

            def mark(ins):
                step[0] += 1
                ins.then_inc(dve_step, 1)
                return step[0]

            def after(n):
                dve.wait_ge(dve_step, n)

            def link(ins):
                after(mark(ins))

            def prep(c, q):
                if c >= CHUNKS:
                    return
                dve.wait_ge(whi_made, SUB * c + q + 1)
                if c >= 2:
                    dve.wait_ge(w_used, SUB * (c - 2) + q + 1)
                dve.scalar_tensor_tensor(out=flat(w_lo, c, q), in0=flat(stage, c, q), scalar=W_SCALE,
                                         in1=flat(w_hi, c, q), op0=ALU.mult,
                                         op1=ALU.subtract).then_inc(wlo_made, 1)

            def rsqrt(bank, t0, n):
                dve.wait_ge(rs_est, n)
                link(dve.tensor_tensor(rs1[:, t0:T], rs0[:, t0:T], rs0[:, t0:T], ALU.mult))
                link(dve.scalar_tensor_tensor(out=rs1[:, t0:T], in0=ps[:, bank, t0:T], scalar=EPS,
                                              in1=rs1[:, t0:T], op0=ALU.add, op1=ALU.mult))
                dve.scalar_tensor_tensor(out=rs[:, t0:T], in0=rs1[:, t0:T], scalar=3.0, in1=rs0[:, t0:T],
                                         op0=ALU.subtract, op1=ALU.mult).then_inc(rs_made, 1)
                dve.wait_ge(rs_made, n)

            def pre_norm(i, t0):
                rsqrt(STAT, t0, ESTIMATE[("pre", i)])
                for dt in range(DT):
                    dve.scalar_tensor_tensor(out=mT[:, dt, t0:T], in0=hT[:, dt, t0:T],
                                             scalar=gain(2 * i, dt), in1=rs[:, t0:T], op0=ALU.mult,
                                             op1=ALU.mult).then_inc(a_raw, 1)
                    if dt:
                        norm_low(i, dt - 1, t0)
                norm_low(i, DT - 1, t0)

            def norm_low(i, dt, t0):
                dve.wait_ge(ahi_made, i * DT + dt + 1)
                dve.tensor_tensor(a_lo[:, dt, t0:T], mT[:, dt, t0:T], a_hi[:, dt, t0:T],
                                  ALU.subtract).then_inc(alo_made, 1)

            def out_scale(i, half, t0):
                for n in range(4):
                    dt = half * 4 + n
                    dve.wait_ge(m_sq, i * DT + dt + 1)
                    last = dve.tensor_scalar(mT[:, dt, t0:T], ps[:, (X, Y)[half] + n, t0:T],
                                             gain(2 * i + 1, dt), None, ALU.mult)
                last.then_inc(m_scaled, 1)

            def post_norm(i, t0):
                rsqrt(STAT, t0, ESTIMATE[("post", i)])
                dve.wait_ge(m_scaled, 2 * (i + 1))
                marks = []
                for dt in range(DT):
                    marks.append(mark(dve.tensor_tensor(mT[:, dt, t0:T], mT[:, dt, t0:T], rs[:, t0:T],
                                                        ALU.mult)))
                    if dt:
                        after(marks[dt - 1])
                        dve.tensor_tensor(hT[:, dt - 1, t0:T], hT[:, dt - 1, t0:T], mT[:, dt - 1, t0:T],
                                          ALU.add).then_inc(h_new, 1)
                after(marks[-1])
                dve.tensor_tensor(hT[:, DT - 1, t0:T], hT[:, DT - 1, t0:T], mT[:, DT - 1, t0:T],
                                  ALU.add).then_inc(h_new, 1)
                dve.wait_ge(h_new, (i + 1) * DT)

            dve.memset(eps_sb[:], EPS).then_inc(eps_set, 1)
            for dt in range(DT):
                dve.wait_ge(xT_up, dt + 1)
                dve.tensor_copy(hT[:, dt, :], ps[:, dt, 0:T]).then_inc(h_in, 1)
            for q in range(SUB):
                prep(0, q)
            dve.wait_ge(par_up, 1)
            for t in range(6):
                last = dve.tensor_copy(par[:, t, 0:PAR_ROWS[t]], ps[:, Y + t // 4, t % 4 * P:t % 4 * P + PAR_ROWS[t]])
            last.then_inc(par_raw, 1)
            dve.wait_ge(par_raw, 1)
            norms = par[:, 0, 0:8 * DT].rearrange("p (i w d) -> p i w d", w=2, d=DT)
            dve.tensor_scalar(norms[:, :, 0, :], norms[:, :, 0, :], -A_SCALE / 2, None, ALU.mult)
            dve.tensor_scalar(norms[:, :, 1, :], norms[:, :, 1, :], -UNSCALE / 2, None, ALU.mult)
            dve.tensor_scalar(par[:, 1, LC:LC + 32], par[:, 1, LC:LC + 32], UNSCALE * A_SCALE, None, ALU.mult)
            dve.tensor_scalar(par[:, 1, LB:LB + 8], par[:, 1, LB:LB + 8], A_SCALE, None, ALU.mult)
            for t in (2, 4):
                dve.tensor_scalar(par[:, t, 0:4 * FT], par[:, t, 0:4 * FT], UNSCALE, None, ALU.mult)
                last = dve.tensor_scalar(par[:, t + 1, 0:2 * FT], par[:, t + 1, 0:2 * FT], UNSCALE, None, ALU.mult)
            last.then_inc(par_ready, 1)
            dve.wait_ge(par_ready, 1)
            pre_norm(0, 0)
            for q in range(SUB):
                prep(1, q)
            dve.wait_ge(lam_exp, 1)
            t_, z, z2, p_ = lam[:, 1, :], lam[:, 2, :], lam[:, 3, :], lam[:, 4, :]
            link(dve.tensor_scalar(z, t_, 2.0, None, ALU.add))
            link(dve.reciprocal(z2, z))
            link(dve.tensor_tensor(z, t_, z2, ALU.mult))
            link(dve.tensor_tensor(z2, z, z, ALU.mult))
            link(dve.tensor_scalar(p_, z2, 1.0 / 19, None, ALU.mult))
            for n in range(17, 1, -2):
                link(dve.scalar_tensor_tensor(out=p_, in0=p_, scalar=1.0 / n, in1=z2, op0=ALU.add,
                                              op1=ALU.mult))
            link(dve.scalar_tensor_tensor(out=p_, in0=p_, scalar=1.0, in1=z, op0=ALU.add, op1=ALU.mult))
            link(dve.tensor_scalar(z, par[:, 1, LL:LL + 16], -1.0, 0.0, ALU.mult, ALU.max))
            link(dve.scalar_tensor_tensor(out=z2, in0=p_, scalar=2.0, in1=z, op0=ALU.mult, op1=ALU.add))
            dve.tensor_scalar(spc[:, 0, :], z2, 4.0, None, ALU.mult)
            dve.tensor_scalar(spc[:, 1, :], z2, -8.0, None, ALU.mult).then_inc(par_ready, 1)
            dve.wait_ge(table_landed, 32)

            def head_rsqrt(h):
                rsqrt(GN if h < HEADS - 1 else Y, 0, ESTIMATE[("head", h)])

            def head_y(h):
                dve.wait_ge(g_silu, h + 1)
                link(dve.scalar_tensor_tensor(out=oT, in0=oT, scalar=-A_SCALE / 2, in1=gT, op0=ALU.mult,
                                              op1=ALU.mult))
                dve.tensor_tensor(oT, oT, rs[:, 0:T].unsqueeze(1).to_broadcast([P, 4, T]),
                                  ALU.mult).then_inc(y_raw, 1)

            def head_low(h):
                dve.wait_ge(yhi_made, h + 1)
                dve.tensor_tensor(y_lo[:, 4 * h:4 * h + 4, :], oT, y_hi[:, 4 * h:4 * h + 4, :],
                                  ALU.subtract).then_inc(ylo_made, 1)

            cos = rope_sb[:, 0:1, :].to_broadcast([P, 2, T])
            sin = rope_sb[:, 1:2, :].to_broadcast([P, 2, T])
            for h in range(HEADS):
                c = RET_IN[h]
                qk = ps[:, X:X + 4, 0:T].rearrange("p (g x) t -> p x g t", x=2)
                rot = rotq.rearrange("p (g x) t -> p x g t", x=2)
                dve.wait_ge(w_used, SUB * (c + 1))
                if h:
                    dve.wait_ge(slo_made, h)
                link(dve.tensor_tensor(rot[:, 0], qk[:, 0], cos, ALU.mult))
                link(dve.tensor_tensor(rotp[:, 0], qk[:, 1], sin, ALU.mult))
                link(dve.tensor_tensor(rot[:, 0], rot[:, 0], rotp[:, 0], ALU.subtract))
                link(dve.tensor_tensor(rot[:, 1], qk[:, 1], cos, ALU.mult))
                link(dve.tensor_tensor(rotp[:, 1], qk[:, 0], sin, ALU.mult))
                dve.tensor_tensor(rot[:, 1], rot[:, 1], rotp[:, 1], ALU.add).then_inc(rot_done, 1)
                prep(c + 2, 0)
                dve.wait_ge(qkhi_made, h + 1)
                dve.tensor_tensor(qk_lo, rotq, qk_hi, ALU.subtract).then_inc(qklo_made, 1)
                for q in range(1, SUB):
                    prep(c + 2, q)
                dve.wait_ge(s_up, h + 1)
                for n, (m0, m) in enumerate(TOK_TILES):
                    last = dve.tensor_tensor(sT[0:m, n, :], ps[0:m, X + n, 0:T],
                                             decay_sb[0:m, h, 2 * P - m0:2 * P - m0 + T], ALU.mult)
                last.then_inc(s_dec, 1)
                dve.wait_ge(shi_made, h + 1)
                if h:
                    dve.wait_ge(o_up, h)
                dve.tensor_tensor(s_lo[:, 0:2, :], sT[:, 0:2, :], s_hi[:, 0:2, :], ALU.subtract)
                dve.tensor_tensor(s_lo[0:META, 2, :], sT[0:META, 2, :], s_hi[0:META, 2, :],
                                  ALU.subtract).then_inc(slo_made, 1)
                if h:
                    head_rsqrt(h - 1)
                for n, (_, m) in enumerate(TOK_TILES):
                    dve.wait_ge(vs_out, NTT * h + n + 1)
                    dve.tensor_scalar(vsum[0:m, n, 1:2], vsum[0:m, n, 0:1], -1.0 / HEAD_V, None,
                                      ALU.mult).then_inc(vmean, 1)
                for n, (_, m) in enumerate(TOK_TILES):
                    dve.wait_ge(vhi_made, NTT * h + n + 1)
                    last = dve.scalar_tensor_tensor(out=v_lo[0:m, n, :], in0=vs[0:m, n, :],
                                                    scalar=vsum[0:m, n, 1:2], in1=v_hi[0:m, n, :],
                                                    op0=ALU.add, op1=ALU.subtract)
                last.then_inc(vlo_made, 1)
                for q in range(SUB):
                    prep(c + 3, q)
                    if q == 0 and h:
                        head_y(h - 1)
                    if q == 1 and h:
                        head_low(h - 1)
                for q in range(SUB):
                    prep(c + 4, q)

            c = RET_OUT
            head_rsqrt(HEADS - 1)
            head_y(HEADS - 1)
            head_low(HEADS - 1)
            for q in range(SUB):
                prep(c + 2, q)
            out_scale(0, 0, 0)
            for q in range(SUB):
                prep(c + 3, q)
            for q in range(SUB):
                prep(c + 4, q)
            out_scale(0, 1, 0)
            post_norm(0, 0)
            pre_norm(1, 0)
            for q in range(SUB):
                prep(c + 5, q)

            def ffn(layer, first_in, first_out, i):
                t0 = ffn_first(layer)
                for j in range(FFN_CHUNKS):
                    c, s, b = first_in + j, (X, Y)[j % 2], j % 2
                    n0 = layer * FFN_CHUNKS + j
                    prep(c + 2, 0)
                    dve.wait_ge(mid_tap, n0 + 1)
                    tiles = [(n, (u_val, u_gate)[n // 2], n // 2 * FT + 2 * j + n % 2) for n in range(4)]
                    marks = []
                    for n, u, f in tiles:
                        uu = u[:, b, n % 2, :]
                        marks.append(mark(dve.scalar_tensor_tensor(
                            out=uu[:, t0 + 1:T], in0=ps[:, s + n, t0:T - 1], scalar=fpar(layer, 0, f),
                            in1=uu[:, t0 + 1:T], op0=ALU.mult, op1=ALU.add)))
                    for n, u, f in tiles:
                        uu = u[:, b, n % 2, :]
                        after(marks[n])
                        last = dve.scalar_tensor_tensor(
                            out=uu[:, t0:T - 1], in0=ps[:, s + n, t0 + 1:T], scalar=fpar(layer, 2, f),
                            in1=uu[:, t0:T - 1], op0=ALU.mult, op1=ALU.add)
                    last.then_inc(conv_done, 1)
                    prep(c + 2, 1)
                    dve.wait_ge(gelu_done, n0 + 1)
                    dve.scalar_tensor_tensor(out=u_y[:, b, :, t0:T], in0=u_gelu[:, b, :, t0:T],
                                             scalar=A_SCALE, in1=u_val[:, b, :, t0:T], op0=ALU.mult,
                                             op1=ALU.mult).then_inc(fy_raw, 1)
                    prep(c + 2, 2)
                    dve.wait_ge(yhi_made, Y_FFN[layer] + j + 1)
                    dve.tensor_tensor(y_lo[:, 2 * j:2 * j + 2, t0:T], u_y[:, b, :, t0:T],
                                      y_hi[:, 2 * j:2 * j + 2, t0:T], ALU.subtract).then_inc(ylo_made, 1)
                    prep(c + 2, 3)
                to = 0 if layer == 0 else T0_OUT
                for n in range(2 * FFN_OUT_K):
                    c = first_out + n
                    if n == FFN_OUT_K - 1:
                        out_scale(i, 0, to)
                    if n < 2 * FFN_OUT_K - 1:
                        for q in range(SUB):
                            prep(c + 2, q)
                out_scale(i, 1, to)
                post_norm(i, to)

            ffn(0, FFN0_IN, FFN0_OUT, 1)
            pre_norm(2, 0)
            for q in range(SUB):
                prep(LRU + 1, q)

            def lru_input(k, c, s):
                prep(c + 2, 0)
                dve.wait_ge(x_mid, k + 1)
                taps = [t for t in range(LRU_TAPS) if t != LRU_LEFT]
                prev = {}
                for t in taps:
                    for n in range(4):
                        j = 4 * k + n
                        sh = t - LRU_LEFT
                        a, b = max(0, -sh), T - max(0, sh)
                        if n in prev:
                            after(prev[n])
                        last = dve.scalar_tensor_tensor(
                            out=xc[:, j, a:b], in0=ps[:, s + n, a + sh:b + sh], scalar=lpar(LC, t * DT + j),
                            in1=xc[:, j, a:b], op0=ALU.mult, op1=ALU.add)
                        if t != taps[-1]:
                            prev[n] = mark(last)
                last.then_inc(x_conv, 1)
                prep(c + 2, 1)
                dve.wait_ge(xhi_made, k + 1)
                dve.tensor_tensor(xc_lo[:, 4 * k:4 * k + 4, :], xc[:, 4 * k:4 * k + 4, :],
                                  xc_hi[:, 4 * k:4 * k + 4, :], ALU.subtract).then_inc(xlo_made, 1)
                prep(c + 2, 2)
                prep(c + 2, 3)

            def lru_gates(k, c):
                for nb in range(2):
                    blk = 2 * k + nb
                    u = li[blk % 2]
                    prep(c + 2, 2 * nb)
                    dve.wait_ge(rates, blk + 1)
                    for d in range(2):
                        g = 2 * blk + d
                        link(dve.tensor_scalar(lv[:, d], la[:, d], 0.5, 0.5, ALU.mult, ALU.add))
                        link(dve.scalar_tensor_tensor(out=la[:, d], in0=lth[:, d], scalar=1.0, in1=lv[:, d],
                                                      op0=ALU.add, op1=ALU.mult))
                        link(dve.scalar_tensor_tensor(out=lv[:, d], in0=la[:, d], scalar=2.0, in1=lv[:, d],
                                                      op0=ALU.subtract, op1=ALU.mult))
                        dve.tensor_scalar(la[:, d], lv[:, d], -2.0, -1.0, ALU.mult, ALU.add)
                        dve.wait_ge(ix_made, g + 1)
                        link(dve.scalar_tensor_tensor(out=u[:, d], in0=lv[:, d], scalar=-2.0, in1=u[:, d],
                                                      op0=ALU.mult, op1=ALU.mult))
                        for m in range(2):
                            j = 2 * blk + m
                            if d == 0:
                                last = dve.tensor_tensor_scan(hf[:, j, :], la[:, d, m, :], u[:, d, m, :], 0.0,
                                                              ALU.mult, ALU.add)
                            else:
                                last = dve.tensor_tensor_scan(hb[:, j, ::-1], la[:, d, m, ::-1],
                                                              u[:, d, m, ::-1], 0.0, ALU.mult, ALU.add)
                        last.then_inc(scanned, 1)
                        if d == 0:
                            prep(c + 2, 2 * nb + 1)

            lru_input(0, XR0, X)
            lru_gates(0, GW0)
            lru_input(1, XR1, Y)
            lru_gates(1, GW1)
            for k, c in ((0, GT0), (1, GT1)):
                sl = slice(4 * k, 4 * k + 4)
                dve.wait_ge(scanned, 4 * k + 4)
                link(dve.tensor_tensor(hf[:, sl, :], hf[:, sl, :], hb[:, sl, :], ALU.add))
                prep(c + 2, 0)
                prep(c + 2, 1)
                dve.wait_ge(gt_out, k + 1)
                dve.wait_ge(ix_made, 4 * k + 4)
                dve.tensor_tensor(xc[:, sl, :], hf[:, sl, :], ggel[:, sl, :], ALU.mult).then_inc(ly_raw, 1)
                prep(c + 2, 2)
                dve.wait_ge(yhi_made, Y_LRU + k + 1)
                dve.tensor_tensor(y_lo[:, sl, :], xc[:, sl, :], y_hi[:, sl, :],
                                  ALU.subtract).then_inc(ylo_made, 1)
                prep(c + 2, 3)
            out_scale(2, 0, T0_LRU_OUT)
            for q in range(SUB):
                prep(LRU_OUT + 2, q)
            out_scale(2, 1, T0_LRU_OUT)
            post_norm(2, T0_LRU_OUT)
            pre_norm(3, T0_LRU_OUT)
            for q in range(SUB):
                prep(LRU_OUT + 3, q)
            ffn(1, FFN1_IN, FFN1_OUT, 3)

        @block.gpsimd
        def _(pool):
            for blk in range(4):
                u = li[blk % 2]
                for d in range(2):
                    pool.wait_ge(r_out, 2 * blk + d + 1)
                    pool.wait_ge(x_conv, blk // 2 + 1)
                    pool.tensor_tensor(u[:, d], u[:, d], xc[:, 2 * blk:2 * blk + 2, :],
                                       ALU.mult).then_inc(pool_step, 1)
                for d in range(2):
                    g = 2 * blk + d
                    pool.wait_ge(pool_step, g + 1)
                    pool.wait_ge(root, g + 1)
                    pool.tensor_tensor(u[:, d], u[:, d], lr[blk % 2][:, d], ALU.mult).then_inc(ix_made, 1)

        @block.tensor
        def _(pe):
            def three(o, w_h, w_l, x_h, x_l, start, stop):
                pe.matmul(o, w_h, x_h, start=start, stop=False)
                pe.matmul(o, w_h, x_l, start=False, stop=False)
                return pe.matmul(o, w_l, x_h, start=False, stop=stop)

            def chunk(c, banks, xh, xl, k0, t0, first=True, last=True, need=None):
                s = c % 2
                for k in range(KC):
                    if k % 2 == 0:
                        pe.wait_ge(wlo_made, SUB * c + k // 2 + 1)
                    if need:
                        need(k0 + k)
                    for n in range(4):
                        col = slice(n * P, (n + 1) * P)
                        mm = three(ps[:, banks + n, t0:T], w_hi[s][:, k, col], w_lo[s][:, k, col],
                                   xh[:, k0 + k, t0:T], xl[:, k0 + k, t0:T],
                                   first and k == 0, last and k == KC - 1)
                    if k % 2 == 1:
                        mm.then_inc(w_used, 1)

            def mean_square(bank, src, one, need, t0, n=DT):
                for dt in range(n):
                    need(dt)
                    mm = pe.matmul(ps[:, bank, t0:T], one, src[:, dt, t0:T], start=dt == 0, stop=dt == n - 1)
                return mm

            def normed(i):
                return lambda k: pe.wait_ge(alo_made, i * DT + k + 1)

            def post_and_pre(i, t0):
                pe.wait_ge(m_scaled, 2 * i + 1)
                mean_square(STAT, sq, ones_sb[:, 0, :], lambda dt: pe.wait_ge(m_sq, i * DT + dt + 1),
                            t0).then_inc(ms_up, 1)

            def pre(i, t0):
                if i:
                    pe.wait_ge(h_new, (i - 1) * DT + 1)
                mean_square(STAT, sq, ones_sb[:, 0, :], lambda dt: pe.wait_ge(h_sq, i * DT + dt + 1),
                            t0).then_inc(ms_up, 1)

            pe.wait_ge(x_landed, 6 * 16)
            for dt in range(DT):
                for n, (t0, t) in enumerate(TOK_TILES):
                    mm = pe.transpose(ps[:, dt, t0:t0 + t], x_in[0:t, n, dt * P:(dt + 1) * P],
                                      ident_sb[0:t, 0:t])
                mm.then_inc(xT_up, 1)
            pe.wait_ge(h_in, DT)
            pre(0, 0)
            pe.wait_ge(const_landed, 16 * len(param_loads))
            for t in range(6):
                mm = pe.transpose(ps[:, Y + t // 4, t % 4 * P:t % 4 * P + PAR_ROWS[t]], prow[0:PAR_ROWS[t], t, :],
                                  ident_sb[0:PAR_ROWS[t], 0:PAR_ROWS[t]])
            mm.then_inc(par_up, 1)

            def head_norm(h, bank):
                pe.wait_ge(o_sq, h + 1)
                mean_square(bank, osq, ones_sb[:, 1, :], lambda dt: None, 0, 4).then_inc(gn_up, 1)

            for h in range(HEADS):
                c = RET_IN[h]
                if h:
                    pe.wait_ge(g_silu, h)
                chunk(c, X, a_hi, a_lo, 0, 0, need=normed(0) if h == 0 else None)
                if h:
                    pe.wait_ge(o_sq, h)
                else:
                    pe.wait_ge(par_raw, 1)
                chunk(c + 1, Y, a_hi, a_lo, 0, 0)
                pe.wait_ge(rot_done, h + 1)
                if h:
                    head_norm(h - 1, GN)
                pe.wait_ge(qklo_made, h + 1)
                for n, (m0, m) in enumerate(TOK_TILES):
                    for k in range(2):
                        key = slice(m0, m0 + m)
                        mm = three(ps[0:m, X + n, 0:T], qk_hi[:, 2 + k, key], qk_lo[:, 2 + k, key],
                                   qk_hi[:, k, :], qk_lo[:, k, :], k == 0, k == 1)
                mm.then_inc(s_up, 1)
                pe.wait_ge(v_out, h + 1)
                for n, (m0, m) in enumerate(TOK_TILES):
                    for e in range(4):
                        mm = pe.transpose(ps[0:m, Y + n, e * P:(e + 1) * P], vT[:, e, m0:m0 + m], ident_sb[:])
                mm.then_inc(vt_up, 1)
                pe.wait_ge(s_dec, h + 1)
                if h:
                    pe.wait_ge(rs_made, ESTIMATE[("head", h - 1)])
                chunk(c + 2, X, a_hi, a_lo, 0, 0)
                pe.wait_ge(vs_out, NTT * (h + 1))
                pe.wait_ge(vlo_made, h + 1)
                pe.wait_ge(slo_made, h + 1)
                for e in range(4):
                    col = slice(e * P, (e + 1) * P)
                    for n, (m0, m) in enumerate(TOK_TILES):
                        mm = three(ps[:, Y + e, 0:T], v_hi[0:m, n, col], v_lo[0:m, n, col],
                                   s_hi[0:m, n, :], s_lo[0:m, n, :], n == 0, n == NTT - 1)
                mm.then_inc(o_up, 1)

            def heads(k):
                pe.wait_ge(ylo_made, k // 4 + 1)

            c = RET_OUT
            pe.wait_ge(g_silu, HEADS)
            chunk(c, X, y_hi, y_lo, 0, 0, last=False, need=heads)
            head_norm(HEADS - 1, Y)
            chunk(c + 1, X, y_hi, y_lo, KC, 0, first=False, need=heads)
            chunk(c + 2, Y, y_hi, y_lo, 0, 0, last=False)
            chunk(c + 3, Y, y_hi, y_lo, KC, 0, first=False)
            post_and_pre(0, 0)
            pre(1, 0)

            def ffn(layer, first_in, first_out, i):
                t0 = ffn_first(layer)
                for j in range(FFN_CHUNKS):
                    if j >= 2:
                        pe.wait_ge(conv_done, layer * FFN_CHUNKS + j - 1)
                    chunk(first_in + j, (X, Y)[j % 2], a_hi, a_lo, 0, t0, need=normed(i) if j == 0 else None)
                to = 0 if layer == 0 else T0_OUT
                for n in range(2 * FFN_OUT_K):
                    half, kg = divmod(n, FFN_OUT_K)
                    if kg == 0:
                        pe.wait_ge(conv_done, layer * FFN_CHUNKS + FFN_CHUNKS - 1 + half)
                    chunk(first_out + n, (X, Y)[half], y_hi, y_lo, kg * KC, to, kg == 0, kg == FFN_OUT_K - 1,
                          need=(lambda k: pe.wait_ge(ylo_made, Y_FFN[layer] + k // 2 + 1)) if half == 0 else None)
                post_and_pre(i, to)

            ffn(0, FFN0_IN, FFN0_OUT, 1)
            pre(2, 0)

            def lru_gates(k, c, sets, free):
                s = c % 2
                wh = w_hi[s].rearrange("p a b -> p (a b)").rearrange("p (q g k e) -> p q g k e", q=4, g=2, k=2)
                wl = w_lo[s].rearrange("p a b -> p (a b)").rearrange("p (q g k e) -> p q g k e", q=4, g=2, k=2)
                for q in range(4):
                    blk = 2 * k + q // 2
                    pe.wait_ge(wlo_made, SUB * c + q + 1)
                    free(q)
                    for g in range(2):
                        for m in range(2):
                            for kk in range(2):
                                col = slice(m * P, (m + 1) * P)
                                mm = three(ps[:, sets[q] + 2 * g + m, 0:T], wh[:, q, g, kk, col], wl[:, q, g, kk, col],
                                           xc_hi[:, 2 * blk + kk, :], xc_lo[:, 2 * blk + kk, :],
                                           kk == 0, kk == 1)
                    mm.then_inc(w_used, 1)

            chunk(XR0, X, a_hi, a_lo, 0, 0, need=normed(2))
            pe.wait_ge(xlo_made, 1)
            lru_gates(0, GW0, GATE_SETS[0], lambda q: pe.wait_ge(r_out, q - 1) if q >= 2 else None)
            pe.wait_ge(r_out, 3)
            chunk(XR1, Y, a_hi, a_lo, 0, 0)
            pe.wait_ge(xlo_made, 2)
            lru_gates(1, GW1, GATE_SETS[1], lambda q: pe.wait_ge(r_out, max(4, 4 + q - 1)))
            pe.wait_ge(r_out, 7)
            chunk(GT0, X, a_hi, a_lo, 0, 0)
            pe.wait_ge(r_out, 8)
            chunk(GT1, Y, a_hi, a_lo, 0, 0)
            pe.wait_ge(gt_out, 1)
            chunk(LRU_OUT, X, y_hi, y_lo, 0, T0_LRU_OUT,
                  need=lambda k: pe.wait_ge(ylo_made, Y_LRU + k // 4 + 1))
            pe.wait_ge(gt_out, 2)
            chunk(LRU_OUT + 1, Y, y_hi, y_lo, 0, T0_LRU_OUT)
            post_and_pre(2, T0_LRU_OUT)
            pre(3, T0_LRU_OUT)
            ffn(1, FFN1_IN, FFN1_OUT, 3)
            pe.wait_ge(h_new, 4 * DT)
            for b in range(4):
                tt, half = b // 2, b % 2
                for n in range(4):
                    t0 = META + tt * P
                    mm = pe.transpose(ps[:, X + b, n * P:(n + 1) * P], hT[:, half * 4 + n, t0:t0 + P], ident_sb[:])
                mm.then_inc(fin_up, 1)


_INS = ["x", "meta_tokens", "norm_gains", "ret_w_in", "ret_w_out", "lru_w_in", "lru_conv_w", "lru_conv_b",
        "lru_w_a", "lru_b_a", "lru_w_i", "lru_b_i", "lru_lambda", "lru_w_out", "ffn_w_in", "ffn_conv_w",
        "ffn_conv_b", "ffn_w_out"]


def constants():
    ident = np.eye(P, dtype=np.float32)
    ones = np.empty((P, 2, P), np.float32)
    ones[:, 0] = 1.0 / D
    ones[:, 1] = 1.0 / HEAD_V
    d = D // HEADS
    inv = np.float32(10000.0) ** (-np.arange(0, d, 2, dtype=np.float32) / np.float32(d))
    ang = np.arange(T, dtype=np.float32)[None, :] * inv[:, None]
    rope = np.stack([np.cos(ang), np.sin(ang)], 1).astype(np.float32) * np.float32(UNSCALE * A_SCALE)
    away = np.abs(np.arange(DECAY_W)[None, :] - 2 * P - np.arange(P)[:, None]).astype(np.float64)
    log_gamma = np.log1p(-np.exp2(-5.0 - np.arange(HEADS)))
    decay = np.exp(log_gamma[None, :, None] * away[:, None, :]) * d ** -0.5 / A_SCALE
    return {"ident": ident, "ones": ones, "rope": rope, "decay": decay.astype(np.float32)}


def kernel(**inputs):
    import concourse.bacc as bacc
    from concourse.bass_utils import run_bass_kernel_spmd

    nc = bacc.Bacc("TRN2", target_bir_lowering=False, num_devices=1)
    arrays, args = {}, []
    named = {name: np.ascontiguousarray(inputs[name]) for name in _INS} | constants()
    for name, a in named.items():
        arrays[f"in_{name}"] = a
        args.append(nc.dram_tensor(f"in_{name}", a.shape, mybir.dt.from_np(a.dtype), kind="ExternalInput").ap())
    args.append(nc.dram_tensor("out", (1, SEQ, D), F32, kind="ExternalOutput").ap())
    build(nc, *args)
    r = run_bass_kernel_spmd(nc, [arrays], core_ids=[0])
    return r.results[0]["out"]
```

```python
from contextlib import ExitStack

import concourse.bass as bass
from concourse import mybir
import numpy as np

F32 = mybir.dt.float32
F16 = mybir.dt.float16
ALU = mybir.AluOpType
ACTF = mybir.ActivationFunctionType
AX_X = mybir.AxisListType.X

P = 128
BANK = 512
EPS = 1e-6
W_SCALE = 2.0 ** 6
A_SCALE = 2.0 ** 4
UNSCALE = 1.0 / (W_SCALE * A_SCALE)

D = 1024
SEQ = 256
META = 16
T = SEQ + META
DT = D // P
HEADS = 4
FFN = 3 * D
FT = FFN // P
LRU_TAPS, LRU_LEFT = 4, 2
LRU_BLOCKS = 4
TOK_TILES = [(0, P), (P, P), (2 * P, T - 2 * P)]
NTT = len(TOK_TILES)
HEAD_V = 2 * D // HEADS
DECAY_W = 2 * P + T

KC = 8
CW = 512
SUB = 4
RET_IN = [3 * h for h in range(HEADS)]
RET_OUT = 3 * HEADS
FFN_CHUNKS = 2 * FFN // CW
FFN_OUT_K = FFN // (KC * P)
FFN0_IN = RET_OUT + 4
FFN0_OUT = FFN0_IN + FFN_CHUNKS
GW0, GW1 = FFN0_OUT + FFN_OUT_K, FFN0_OUT + FFN_OUT_K + 1
XR0, XR1, GT0, GT1, LRU_OUT = range(FFN0_OUT + 2 * FFN_OUT_K + 2, FFN0_OUT + 2 * FFN_OUT_K + 7)
FFN1_IN = LRU_OUT + 2
FFN1_OUT = FFN1_IN + FFN_CHUNKS
CHUNKS = FFN1_OUT + 2 * FFN_OUT_K

def ffn_out(layer, n):
    return FFN1_OUT + n if layer else FFN0_OUT + n + (2 if n >= FFN_OUT_K else 0)


def used(c, q=SUB - 1):
    return SUB * (c - (2 if c > GW1 else 0)) + q + 1


def before(c):
    return c - (4 if c in (GW1 + 1, GW1 + 2) else 2)


RET_OUT_ORDER = [(0, 0), (0, 1), (1, 0), (1, 1)]

_order = ([("pre", 0)] + [("head", h) for h in range(HEADS)] + [("post", 0)]
          + [(w, i) for i in (1, 2) for w in ("pre", "post")] + [("pre", 3)])
ESTIMATE = {which: n + 1 for n, which in enumerate(_order)}
MEAN = {which: n + 1 for n, which in enumerate(w for w in _order if w[0] != "head")}

Y_FFN = [HEADS, HEADS + FFN_CHUNKS + 4]
Y_LRU = HEADS + FFN_CHUNKS

PAR_ROWS = [8 * DT, 88, 4 * FT, 4 * FT, 4 * FT, 4 * FT]
PAR_COL = [0, 0, 88, 88 + 4 * FT, 88 + 8 * FT, 88 + 12 * FT]

T0_LRU_OUT = META - 2
T0_OUT = META


def ffn_first(layer):
    return 0 if layer == 0 else T0_LRU_OUT


def build(nc, x, meta, gains, ret_w_in, ret_w_out, lru_w_in, lru_conv_w, lru_conv_b, lru_w_a, lru_b_a,
          lru_w_i, lru_b_i, lru_lambda, lru_w_out, ffn_w_in, ffn_conv_w, ffn_conv_b, ffn_w_out,
          ident, ones, rope, decay, out):
    ctx = ExitStack()
    with ctx:
        def sb(name, shape, dt=F32):
            return ctx.enter_context(nc.sbuf_tensor(name, shape, dt))

        def sem(name):
            return ctx.enter_context(nc.semaphore(name))

        stage = [sb(f"stage{s}", [P, KC, CW]) for s in range(2)]
        w_hi = [sb(f"w_hi{s}", [P, KC, CW], F16) for s in range(2)]
        w_lo = [sb(f"w_lo{s}", [P, KC, CW], F16) for s in range(2)]
        hT = sb("hT", [P, DT, T])
        mT = sb("mT", [P, DT, T])
        sq = sb("sq", [P, DT, T])
        a_hi = sb("a_hi", [P, DT, T], F16)
        a_lo = sb("a_lo", [P, DT, T], F16)
        y_hi = sb("y_hi", [P, FT, T], F16)
        y_lo = sb("y_lo", [P, FT, T], F16)
        ident_sb = sb("ident_sb", [P, P])
        ones_sb = sb("ones_sb", [P, 2, P])
        rope_sb = sb("rope_sb", [P, 2, T])
        decay_all = sb("decay_all", [P, 8 * T])
        decay_sb = decay_all[:, 0:HEADS * DECAY_W].rearrange("p (h j) -> p h j", j=DECAY_W)
        prow = sb("prow", [P, 6, P])
        gains_sb = sb("gains_sb", [P, 8 * DT])
        par = sb("par", [P, PAR_ROWS[1]])
        eps_sb = sb("eps_sb", [P, 1])
        est_warm = sb("est_warm", [P, 1])
        rs0 = sb("rs0", [P, T])
        rs1 = sb("rs1", [P, T])
        rs = sb("rs", [P, T])
        rs_in = sb("rs_in", [P, T])
        sq_sum = sb("sq_sum", [P, T])
        cpar = sb("cpar", [P, 2, FFN_CHUNKS, 16])
        cnow = [sb(f"cnow{b}", [P, 16]) for b in range(2)]
        fin_s = sb("fin_s", [P, 8, 2])
        lam = sb("lam", [P, 8, 16])
        spc = sb("spc", [P, 2, 16])
        work = sb("work", [P, 10 * 4 * T])
        work16 = sb("work16", [P, 14 * T + 6 * BANK], F16)

        off = 0

        def carve(*shape):
            nonlocal off
            n = int(np.prod(shape))
            v = work[:, off:off + n]
            off += n
            if len(shape) == 2:
                v = v.rearrange("p (a b) -> p a b", b=shape[1])
            if len(shape) == 3:
                v = v.rearrange("p (a b c) -> p a b c", b=shape[1], c=shape[2])
            return v
        x_in = work[:, 0:3 * D].rearrange("p (a b) -> p a b", b=D)
        rotp = carve(2, 2, T)
        rotq = carve(4, T)
        vs = carve(3, BANK)
        sT = rotq[:, 0:3, :]
        oT, gT = mT[:, 0:4, :], mT[:, 4:8, :]
        osq, vT = sq[:, 0:4, :], sq[:, 4:8, :]
        vsum = sb("vsum", [P, 3, 2])
        qk_hi = work16[:, 0:4 * T].rearrange("p (a b) -> p a b", b=T)
        qk_lo = work16[:, 4 * T:8 * T].rearrange("p (a b) -> p a b", b=T)
        v_hi = work16[:, 8 * T:8 * T + 3 * BANK].rearrange("p (a b) -> p a b", b=BANK)
        v_lo = work16[:, 8 * T + 3 * BANK:8 * T + 6 * BANK].rearrange("p (a b) -> p a b", b=BANK)
        s_hi = work16[:, 8 * T + 6 * BANK:11 * T + 6 * BANK].rearrange("p (a b) -> p a b", b=T)
        s_lo = work16[:, 11 * T + 6 * BANK:14 * T + 6 * BANK].rearrange("p (a b) -> p a b", b=T)
        off = 0
        u_in = [carve(4, T) for _ in range(2)]
        u_cv = [carve(4, T) for _ in range(2)]
        u_y = [carve(2, T) for _ in range(2)]
        n_parts = KC * CW // 2
        gw_hi, gw_lo = [[work[:, (2 * k + part) * n_parts:(2 * k + part + 1) * n_parts].bitcast(F16)
                         for k in range(2)] for part in range(2)]
        off = 4 * n_parts
        xc = carve(DT, T)
        assert off <= 10 * 4 * T
        hf, hb = sq, mT

        def quad(v, n):
            return v[:, 4 * T * n:4 * T * (n + 1)].rearrange("p (d m t) -> p d m t", d=2, t=T)
        y_hi_rest, y_lo_rest = [v.rearrange("p a b -> p (a b)")[:, DT * T:3 * DT * T].bitcast(F32)
                                for v in (y_hi, y_lo)]
        g0_place, g1_place = work[:, 0:2 * n_parts], work[:, 2 * n_parts:4 * n_parts]
        hf_flat, hb_flat = [v.rearrange("p a b -> p (a b)") for v in (hf, hb)]
        lr = [quad(decay_all, 0), quad(y_lo_rest, 0), quad(y_hi_rest, 0), quad(g0_place, 0)]
        li = [quad(decay_all, 1), quad(y_lo_rest, 1), quad(y_hi_rest, 1), quad(g0_place, 1)]
        la = [quad(hb_flat, 0), quad(hf_flat, 1), quad(hb_flat, 1), quad(g0_place, 2)]
        lq = [quad(hf_flat, 0), la[3], quad(g1_place, 0), quad(g1_place, 1)]
        x_raw = [y_hi_rest[:, 4 * T * k:4 * T * (k + 1)].rearrange("p (a b) -> p a b", b=T) for k in range(2)]
        regions = [work16[:, k * DT * T:(k + 1) * DT * T] for k in range(2)]
        xc_hi = [v[:, 0:4 * T].rearrange("p (a b) -> p a b", b=T) for v in regions]
        xc_lo = [v[:, 4 * T:8 * T].rearrange("p (a b) -> p a b", b=T) for v in regions]
        ggel = [v.bitcast(F32).rearrange("p (a b) -> p a b", b=T) for v in regions]
        l_prod = quad(work16[:, 2 * DT * T:3 * DT * T].bitcast(F32), 0)
        g_row = mT.rearrange("p a b -> p (a b)")[:, 0:D]
        fin = sq.rearrange("p a b -> p (a b)")[:, 0:2 * D].rearrange("p (a b) -> p a b", b=D)
        fin_sq = work[:, 0:BANK]

        ps = ctx.enter_context(nc.psum_tensor("ps", [P, 8, BANK], F32))
        X, Y = 0, 4
        GATE_SET = [X, Y, X, Y, Y, X, Y, X]
        STAT = X
        STAT_IN = Y + 3
        GAINS = Y + 3
        PARAMS = Y + 3
        H_ROW = [X + 2, X + 3, Y + 2, Y + 3]
        GN = X + 3

        def gain(norm, dt):
            return gains_sb[:, norm * DT + dt:norm * DT + dt + 1]

        LC, LB, LBA, LBI, LL = 0, 32, 40, 56, 72

        def lpar(base, i):
            return par[:, base + i:base + i + 1]

        def cpar_col(tap, n):
            return tap * 4 + n

        def tiles(v):
            return v.rearrange("n (t p) -> (n t) p", p=P)

        gain_load = (prow[0:8 * DT, 0, :], gains.rearrange("l n (t p) -> (l n t) p", p=P))
        param_loads = [(prow[LC:LB, 1, :], tiles(lru_conv_w[0])), (prow[LB:LBA, 1, :], tiles(lru_conv_b)),
                       (prow[LBA:LBI, 1, :], tiles(lru_b_a[0])), (prow[LBI:LL, 1, :], tiles(lru_b_i[0])),
                       (prow[LL:LL + 16, 1, :], tiles(lru_lambda[0]))]
        for layer in range(2):
            param_loads += [(prow[0:4 * FT, 2 + 2 * layer, :], tiles(ffn_conv_w[layer, 0:2])),
                            (prow[0:2 * FT, 3 + 2 * layer, :], tiles(ffn_conv_w[layer, 2:3])),
                            (prow[2 * FT:4 * FT, 3 + 2 * layer, :], tiles(ffn_conv_b[layer:layer + 1]))]

        x_landed = sem("x_landed")
        const_landed = sem("const_landed")
        gain_landed = sem("gain_landed")
        par_landed = sem("par_landed")
        table_landed = sem("table_landed")
        w_landed = [[sem(f"w_landed{s}_{j}") for j in range(2)] for s in range(2)]
        whi_made = sem("whi_made")
        wlo_made = sem("wlo_made")
        w_used = sem("w_used")
        xT_up = sem("xT_up")
        h_in = sem("h_in")
        gain_up = sem("gain_up")
        gain_ready = sem("gain_ready")
        par_up = sem("par_up")
        par_raw = sem("par_raw")
        par_ready = sem("par_ready")
        lam_abs = sem("lam_abs")
        lam_exp = sem("lam_exp")
        eps_set = sem("eps_set")
        m_sq = sem("m_sq")
        m_scaled = sem("m_scaled")
        h_new = sem("h_new")
        h_sq = sem("h_sq")
        sum_h = sem("sum_h")
        sum_m = sem("sum_m")
        ms_up = sem("ms_up")
        rs_est = sem("rs_est")
        rs_made = sem("rs_made")
        ahi_made = sem("ahi_made")
        alo_made = sem("alo_made")
        rope_scaled = sem("rope_scaled")
        rot_done = sem("rot_done")
        qkhi_made = sem("qkhi_made")
        qklo_made = sem("qklo_made")
        v_out = sem("v_out")
        s_up = sem("s_up")
        vt_up = sem("vt_up")
        s_dec = sem("s_dec")
        shi_made = sem("shi_made")
        slo_made = sem("slo_made")
        vs_out = sem("vs_out")
        vmean = sem("vmean")
        vhi_made = sem("vhi_made")
        vlo_made = sem("vlo_made")
        g_out = sem("g_out")
        g_silu = sem("g_silu")
        o_up = sem("o_up")
        o_sq = sem("o_sq")
        gn_up = sem("gn_up")
        y_raw = sem("y_raw")
        yhi_made = sem("yhi_made")
        ylo_made = sem("ylo_made")
        cnow_set = sem("cnow_set")
        u_out = sem("u_out")
        mid_tap = sem("mid_tap")
        left_tap = sem("left_tap")
        conv_done = sem("conv_done")
        gelu_done = sem("gelu_done")
        fy_raw = sem("fy_raw")
        fylo_made = sem("fylo_made")
        x_out = sem("x_out")
        x_mid = sem("x_mid")
        x_conv = sem("x_conv")
        xhi_made = sem("xhi_made")
        xlo_made = sem("xlo_made")
        gates_up = sem("gates_up")
        r_out = sem("r_out")
        exps = sem("exps")
        rates = sem("rates")
        half_up = sem("half_up")
        root = sem("root")
        ix_made = sem("ix_made")
        scanned = sem("scanned")
        gt_out = sem("gt_out")
        gt_gelu = sem("gt_gelu")
        both = sem("both")
        ly_raw = sem("ly_raw")
        hrow_up = sem("hrow_up")
        g_row_landed = sem("g_row_landed")
        fin_sum = sem("fin_sum")
        fin_m = sem("fin_m")
        fin_ms = sem("fin_ms")
        fin_est = sem("fin_est")
        fin_out = sem("fin_out")
        stored = sem("stored")
        dve_step = sem("dve_step")
        pool_step = sem("pool_step")

        def landed(c):
            gates = sum(g <= c and g % 2 == c % 2 for g in (GW0, GW1))
            return 32 * (c // 2 + 1) + 32 * gates

        def flat(w, c, q):
            return w[c % 2][:, 2 * q:2 * q + 2, :].rearrange("p a b -> p (a b)")

        def part(w, gw, c, q):
            return gw[c - GW0][:, 2 * CW * q:2 * CW * (q + 1)] if c in (GW0, GW1) else flat(w, c, q)

        block = ctx.enter_context(nc.Block())

        @block.sync
        def _(sp):
            sp.dma_start(ident_sb[:], ident).then_inc(x_landed, 16)
            sp.dma_start(x_in[0:META, 0, :], meta).then_inc(x_landed, 16)
            sp.dma_start(x_in[META:P, 0, :], x[0, 0:P - META, :]).then_inc(x_landed, 16)
            sp.dma_start(x_in[:, 1, :], x[0, P - META:2 * P - META, :]).then_inc(x_landed, 16)
            sp.dma_start(x_in[0:META, 2, :], x[0, 2 * P - META:SEQ, :]).then_inc(x_landed, 16)
            sp.dma_start(*gain_load).then_inc(gain_landed, 16)

            def load(c, pieces, i=0):
                s = c % 2
                for half in range(2):
                    if c >= 2:
                        sp.wait_ge(wlo_made, SUB * (c - 2) + 2 * half + 2 + 2 * SUB * i)
                    views = pieces(half)
                    for dst, src in views:
                        sp.dma_start(dst, src).then_inc(w_landed[s][half], max(16, 32 // len(views)))

            def rows(w, k0, half):
                k = k0 + half * KC // 2
                return w.rearrange("(k p) n -> p k n", p=P)[:, k:k + KC // 2, :]

            def half_slot(c, half):
                return stage[c % 2][:, half * KC // 2:(half + 1) * KC // 2, :]

            def load_plain(c, w, k0, n0):
                load(c, lambda half: [(half_slot(c, half), rows(w, k0, half)[:, :, n0:n0 + CW])])

            def load_pair(c, w, n0, n1, i=0):
                def columns(half, n):
                    return rows(w, 0, half)[:, :, n:n + CW // 2] if isinstance(i, int) and i == 0 else \
                        rows(w, 0, half)[:, :, bass.ds(i * CW + n, CW // 2)]
                load(c, lambda half: [(half_slot(c, half)[:, :, 0:CW // 2], columns(half, n0)),
                                      (half_slot(c, half)[:, :, CW // 2:CW], columns(half, n1))], i)

            def load_gates(c, block0):
                def pieces(half):
                    n = block0 + half
                    to = half_slot(c, half).rearrange("p a b -> p (a b)").rearrange(
                        "p (d g k e) -> p d g k e", d=2, g=2, k=2)
                    return [(to[:, d, g, :, :], w[0, d, n].rearrange("(k p) e -> p k e", p=P))
                            for g, w in enumerate((lru_w_a, lru_w_i)) for d in range(2)]
                load(c, pieces)

            wi, wo = ret_w_in[0], ret_w_out[0]
            for h in range(HEADS):
                load_pair(RET_IN[h], wi, h * 2 * P, D + h * 2 * P)
                if h == 0:
                    sp.dma_start(ones_sb[:], ones).then_inc(const_landed, 16)
                    sp.dma_start(rope_sb[:], rope).then_inc(table_landed, 16)
                load_plain(RET_IN[h] + 1, wi, 0, 2 * D + h * HEAD_V)
                if h == 0:
                    for dst, src in param_loads:
                        sp.dma_start(dst, src).then_inc(par_landed, 16)
                    sp.dma_start(decay_sb, decay).then_inc(table_landed, 16)
                load_plain(RET_IN[h] + 2, wi, 0, 4 * D + h * HEAD_V)
            for n, (half, kg) in enumerate(RET_OUT_ORDER):
                load_plain(RET_OUT + n, wo, kg * KC, half * CW)

            def load_ffn(layer, first_in):
                with sp.Fori(0, FFN_CHUNKS // 2) as i:
                    for b in range(2):
                        load_pair(first_in + b, ffn_w_in[layer], b * 2 * P, FFN + b * 2 * P, i)
                for n in range(2 * FFN_OUT_K):
                    if (layer, n) == (0, FFN_OUT_K):
                        load_gates(GW0, 0)
                        load_gates(GW1, 2)
                    load_plain(ffn_out(layer, n), ffn_w_out[layer], (n % FFN_OUT_K) * KC,
                               n // FFN_OUT_K * CW)

            load_ffn(0, FFN0_IN)
            for c, n0 in ((XR0, D), (XR1, D + CW), (GT0, 0), (GT1, CW)):
                load_plain(c, lru_w_in[0], 0, n0)
            for half in range(2):
                load_plain(LRU_OUT + half, lru_w_out[0], 0, half * CW)
            load_ffn(1, FFN1_IN)
            sp.wait_ge(h_new, 3 * DT)
            sp.dma_start(g_row, gains[1, 3, :].partition_broadcast(P)).then_inc(g_row_landed, 16)
            for b in range(4):
                sp.wait_ge(fin_out, b + 1)
                tt, half = b // 2, b % 2
                sp.dma_start(out[0, tt * P:(tt + 1) * P, half * BANK:(half + 1) * BANK],
                             fin[:, tt, half * BANK:(half + 1) * BANK]).then_inc(stored, 16)
            sp.wait_ge(stored, 64)

        @block.scalar
        def _(act):
            def prep(c, q, i=0):
                act.wait_ge(w_landed[c % 2][q // 2], landed(c) + 32 * i)
                if c in (GW0, GW1):
                    act.wait_ge(fylo_made, FFN_CHUNKS)
                elif c >= 2:
                    act.wait_ge(w_used, used(before(c), q) + 2 * SUB * i)
                act.activation(part(w_hi, gw_hi, c, q), flat(stage, c, q), ACTF.Copy,
                               scale=W_SCALE).then_inc(whi_made, 1)

            def estimate(bank, t0, up, n_up, n):
                act.wait_ge(up, n_up)
                if n > 1:
                    act.wait_ge(rs_made, n - 1)
                act.activation(rs0[:, t0:T], ps[:, bank, t0:T], ACTF.Abs_reciprocal_sqrt,
                               bias=eps_sb[:, 0:1]).then_inc(rs_est, 1)

            def load_estimate_table():
                act.activation(est_warm[:], eps_sb[:], ACTF.Abs_reciprocal_sqrt)

            def norm_input(i, t0):
                for dt in range(DT):
                    if i == 0:
                        act.wait_ge(h_in, dt + 1)
                    else:
                        act.wait_ge(h_new, (i - 1) * DT + dt + 1)
                    act.activation(a_hi[:, dt, t0:T], hT[:, dt, t0:T], ACTF.Copy,
                                   scale=gain(2 * i, dt)).then_inc(ahi_made, 1)
                    act.activation(sq[:, dt, t0:T], hT[:, dt, t0:T], ACTF.Square).then_inc(h_sq, 1)

            def estimate_input(i, t0):
                estimate(STAT_IN, t0, ms_up, MEAN[("pre", i)], ESTIMATE[("pre", i)])

            def out_squares(c, i, half, t0):
                act.wait_ge(w_used, used(c))
                for n in range(4):
                    act.activation(sq[:, half * 4 + n, t0:T], ps[:, (X, Y)[half] + n, t0:T], ACTF.Square,
                                   scale=UNSCALE).then_inc(m_sq, 1)

            act.wait_ge(eps_set, 1)
            load_estimate_table()
            act.wait_ge(gain_ready, 1)
            norm_input(0, 0)
            for c in range(2):
                for q in range(SUB):
                    prep(c, q)
                    if (c, q) == (1, 1):
                        estimate_input(0, 0)

            def head_y(h):
                act.wait_ge(y_raw, h + 1)
                act.activation(y_hi[:, 4 * h:4 * h + 4, :], oT, ACTF.Copy).then_inc(yhi_made, 1)

            for h in range(HEADS):
                c = RET_IN[h]
                prep(c + 2, 0)
                prep(c + 2, 1)
                act.wait_ge(rot_done, h + 1)
                if h:
                    act.wait_ge(s_up, h)
                act.activation(qk_hi, rotq, ACTF.Copy).then_inc(qkhi_made, 1)
                prep(c + 2, 2)
                prep(c + 2, 3)
                if h:
                    estimate(GN, 0, gn_up, h, ESTIMATE[("head", h - 1)])
                prep(c + 3, 0)
                act.wait_ge(s_dec, h + 1)
                if h:
                    act.wait_ge(o_up, h)
                act.activation(s_hi[:, 0:2, :], sT[:, 0:2, :], ACTF.Copy)
                act.activation(s_hi[0:META, 2, :], sT[0:META, 2, :], ACTF.Copy).then_inc(shi_made, 1)
                act.wait_ge(vt_up, h + 1)
                if h:
                    act.wait_ge(vlo_made, h)
                for n, (_, m) in enumerate(TOK_TILES):
                    act.activation(vs[0:m, n, :], ps[0:m, Y + n, :], ACTF.Copy, scale=-0.5 * UNSCALE * A_SCALE,
                                   accum_out=vsum[0:m, n, 0:1]).then_inc(vs_out, 1)
                for n, (_, m) in enumerate(TOK_TILES):
                    act.wait_ge(vmean, NTT * h + n + 1)
                    act.activation(v_hi[0:m, n, :], vs[0:m, n, :], ACTF.Identity,
                                   bias=vsum[0:m, n, 1:2]).then_inc(vhi_made, 1)
                if h:
                    head_y(h - 1)
                for q in range(1, SUB):
                    prep(c + 3, q)
                act.wait_ge(g_out, h + 1)
                act.activation(gT, gT, ACTF.Silu, scale=-0.5 * UNSCALE).then_inc(g_silu, 1)
                for q in range(SUB - 1):
                    prep(c + 4, q)
                act.wait_ge(o_up, h + 1)
                if h:
                    act.wait_ge(yhi_made, h)
                    act.wait_ge(ylo_made, h)
                for n in range(4):
                    act.activation(oT[:, n, :], ps[:, Y + n, 0:T], ACTF.Copy, scale=1.0 / A_SCALE ** 2)
                for n in range(4):
                    last = act.activation(osq[:, n, :], ps[:, Y + n, 0:T], ACTF.Square,
                                          scale=1.0 / A_SCALE ** 2)
                last.then_inc(o_sq, 1)
                prep(c + 4, 3)
                if h == 0:
                    act.wait_ge(par_raw, 1)
                    act.activation(lam[:, 0, :], par[:, LL:LL + 16], ACTF.Abs).then_inc(lam_abs, 1)
                    act.wait_ge(lam_abs, 1)
                    act.activation(lam[:, 1, :], lam[:, 0, :], ACTF.Exp, scale=-1.0).then_inc(lam_exp, 1)

            c = RET_OUT
            estimate(Y, 0, gn_up, HEADS, ESTIMATE[("head", HEADS - 1)])
            head_y(HEADS - 1)
            for q in range(SUB):
                prep(c + 2, q)
            out_squares(c + 1, 0, 0, 0)
            for n in (3, 4):
                for q in range(SUB):
                    prep(c + n, q)
            load_estimate_table()
            out_squares(c + 3, 0, 1, 0)
            estimate(STAT, 0, ms_up, MEAN[("post", 0)], ESTIMATE[("post", 0)])
            norm_input(1, 0)
            for q in range(SUB):
                prep(c + 5, q)
                if q == 1:
                    estimate_input(1, 0)

            def ffn_chunk(layer, first_in, i, b):
                t0 = ffn_first(layer)
                c = first_in + b
                n0 = layer * FFN_CHUNKS + b + 2 * i
                behind = layer > 0 or not (isinstance(i, int) and i == 0)
                act.wait_ge(u_out, n0 + 1)
                act.wait_ge(cnow_set, n0 + 1)
                if behind:
                    act.wait_ge(fy_raw, n0 - 1)
                for n in range(4):
                    last = act.activation(u_cv[b][:, n, t0:T], u_in[b][:, n, t0:T], ACTF.Identity,
                                          scale=cnow[b][:, cpar_col(1, n):cpar_col(1, n) + 1],
                                          bias=cnow[b][:, cpar_col(3, n):cpar_col(3, n) + 1])
                last.then_inc(mid_tap, 1)
                prep(c + 2, 2, i)
                prep(c + 2, 3, i)
                act.wait_ge(conv_done, n0 + 1)
                if behind:
                    act.wait_ge(fylo_made, n0 - 1)
                act.activation(u_y[b][:, :, t0:T], u_cv[b][:, 2:4, t0:T],
                               ACTF.Gelu_apprx_tanh).then_inc(gelu_done, 1)
                prep(c + 3, 0, i)
                act.wait_ge(fy_raw, n0 + 1)
                dst = y_hi[:, bass.ds(4 * i + 2 * b, 2), t0:T] if not isinstance(i, int) else \
                    y_hi[:, 4 * i + 2 * b:4 * i + 2 * b + 2, t0:T]
                act.activation(dst, u_y[b][:, :, t0:T], ACTF.Copy).then_inc(yhi_made, 1)
                prep(c + 3, 1, i)

            def ffn_in(layer, first_in):
                prep(first_in + 2, 0)
                prep(first_in + 2, 1)
                for b in range(2):
                    ffn_chunk(layer, first_in, 0, b)
                with act.Fori(1, FFN_CHUNKS // 2) as i:
                    for b in range(2):
                        ffn_chunk(layer, first_in, i, b)

            ffn_in(0, FFN0_IN)
            for c in range(FFN0_OUT + 2, XR0 + 1):
                if c == ffn_out(0, 2 * FFN_OUT_K - 1):
                    out_squares(ffn_out(0, FFN_OUT_K - 1), 1, 0, 0)
                for q in range(SUB):
                    if (c, q) not in ((FFN0_OUT + 2, 0), (FFN0_OUT + 2, 1)):
                        prep(c, q)
            load_estimate_table()
            out_squares(ffn_out(0, 2 * FFN_OUT_K - 1), 1, 1, 0)
            estimate(STAT, 0, ms_up, MEAN[("post", 1)], ESTIMATE[("post", 1)])
            norm_input(2, 0)
            for q in range(SUB):
                prep(XR1, q)
                if q == 1:
                    estimate_input(2, 0)

            def gates(n):
                blk, d, s = n // 2, n % 2, GATE_SET[n]
                act.wait_ge(gates_up, n + 1)
                for to, base, first in ((lr, LBA, s), (li, LBI, s + 2)):
                    for m in range(2):
                        last = act.activation(to[blk][:, d, m, :], ps[:, first + m, 0:T], ACTF.Sigmoid,
                                              scale=UNSCALE, bias=lpar(base, d * DT + 2 * blk + m))
                last.then_inc(r_out, 1)

            def block_rates(blk):
                act.wait_ge(r_out, 2 * blk + 2)
                if blk == 3:
                    act.wait_ge(ix_made, 2)
                pairs = [(d, m, d * DT + 2 * blk + m) for d in range(2) for m in range(2)]
                for d, m, j in pairs:
                    last = act.activation(la[blk][:, d, m, :], lr[blk][:, d, m, :], ACTF.Exp,
                                          scale=spc[:, 1, j:j + 1])
                last.then_inc(exps, 1)
                act.wait_ge(exps, blk + 1)
                for d, m, j in pairs:
                    last = act.activation(lr[blk][:, d, m, :], lr[blk][:, d, m, :], ACTF.Tanh,
                                          scale=spc[:, 0, j:j + 1])
                last.then_inc(rates, 1)

            def block_root(blk):
                act.wait_ge(rates, blk + 1)
                act.activation(lq[blk], lr[blk], ACTF.Sqrt).then_inc(root, 1)

            def gate_gelu(k):
                act.wait_ge(gt_out, k + 1)
                act.activation(ggel[k], ggel[k], ACTF.Gelu_apprx_tanh, scale=-0.5 * UNSCALE).then_inc(gt_gelu, 1)

            def lru_y(blk):
                act.wait_ge(ly_raw, blk + 1)
                act.activation(y_hi[:, 2 * blk:2 * blk + 2, :], xc[:, 2 * blk:2 * blk + 2, :],
                               ACTF.Copy).then_inc(yhi_made, 1)

            def x_high(k):
                act.wait_ge(x_conv, k + 1)
                act.activation(xc_hi[k], xc[:, 4 * k:4 * k + 4, :], ACTF.Copy).then_inc(xhi_made, 1)

            for q in range(2):
                prep(GT0, q)
            x_high(0)
            for q in (2, 3):
                prep(GT0, q)
            prep(GT1, 0)
            prep(GT1, 1)
            gates(0)
            gates(1)
            x_high(1)
            prep(GT1, 2)
            prep(GT1, 3)
            gates(2)
            gates(3)
            for rates_or_root in (block_rates, block_root):
                for blk in (0, 1):
                    rates_or_root(blk)
            gate_gelu(0)
            for q in range(SUB):
                gates(4 + q)
                prep(LRU_OUT, q)
            lru_y(0)
            lru_y(1)
            for rates_or_root in (block_rates, block_root):
                for blk in (2, 3):
                    rates_or_root(blk)
            gate_gelu(1)
            lru_y(2)
            lru_y(3)
            for q in range(SUB):
                prep(LRU_OUT + 1, q)

            for q in range(SUB):
                prep(LRU_OUT + 2, q)
            out_squares(LRU_OUT, 2, 0, T0_LRU_OUT)
            load_estimate_table()
            out_squares(LRU_OUT + 1, 2, 1, T0_LRU_OUT)
            estimate(STAT, T0_LRU_OUT, ms_up, MEAN[("post", 2)], ESTIMATE[("post", 2)])
            norm_input(3, T0_LRU_OUT)
            for q in range(SUB):
                prep(LRU_OUT + 3, q)
                if q == 1:
                    estimate_input(3, T0_LRU_OUT)

            ffn_in(1, FFN1_IN)
            for n in range(2 * FFN_OUT_K):
                c = FFN1_OUT + n
                if c + 2 < CHUNKS:
                    for q in range(SUB):
                        if (n, q) not in ((0, 0), (0, 1)):
                            prep(c + 2, q)
                if n == 2 * FFN_OUT_K - 2:
                    load_estimate_table()
                if n in (FFN_OUT_K, 2 * FFN_OUT_K - 1):
                    half = n // FFN_OUT_K - (n == FFN_OUT_K)
                    act.wait_ge(w_used, used(FFN1_OUT + (half + 1) * FFN_OUT_K - 1))
                    for tt in range(2):
                        b = 2 * half + tt
                        if b:
                            act.wait_ge(fin_sum, b)
                        act.activation(fin_sq, ps[:, (X, Y)[half] + tt, :], ACTF.Square, scale=UNSCALE,
                                       accum_out=fin_s[:, half, tt:tt + 1]).then_inc(fin_sum, 1)
            act.wait_ge(fin_ms, 1)
            act.activation(fin_s[:, 3, :], fin_s[:, 2, :], ACTF.Abs_reciprocal_sqrt, scale=1.0 / D,
                           bias=eps_sb[:, 0:1]).then_inc(fin_est, 1)

        @block.vector
        def _(dve):
            step = [0]

            def mark(ins):
                step[0] += 1
                ins.then_inc(dve_step, 1)
                return step[0]

            def after(n):
                dve.wait_ge(dve_step, n)

            def link(ins):
                after(mark(ins))

            def prep(c, q, i=0):
                dve.wait_ge(whi_made, SUB * c + q + 1 + 2 * SUB * i)
                if c in (GW0, GW1):
                    dve.wait_ge(fylo_made, FFN_CHUNKS)
                elif c >= 2:
                    dve.wait_ge(w_used, used(before(c), q) + 2 * SUB * i)
                dve.scalar_tensor_tensor(out=part(w_lo, gw_lo, c, q), in0=flat(stage, c, q),
                                         scalar=W_SCALE, in1=part(w_hi, gw_hi, c, q), op0=ALU.mult,
                                         op1=ALU.subtract).then_inc(wlo_made, 1)

            def rsqrt(to, bank, t0, n):
                dve.wait_ge(rs_est, n)
                link(dve.tensor_tensor(rs1[:, t0:T], rs0[:, t0:T], rs0[:, t0:T], ALU.mult))
                link(dve.scalar_tensor_tensor(out=rs1[:, t0:T], in0=ps[:, bank, t0:T], scalar=EPS,
                                              in1=rs1[:, t0:T], op0=ALU.add, op1=ALU.mult))
                dve.scalar_tensor_tensor(out=to[:, t0:T], in0=rs1[:, t0:T], scalar=3.0, in1=rs0[:, t0:T],
                                         op0=ALU.subtract, op1=ALU.mult).then_inc(rs_made, 1)
                dve.wait_ge(rs_made, n)

            def rsqrt_input(i, t0):
                rsqrt(rs_in, STAT_IN, t0, ESTIMATE[("pre", i)])

            def norm_low(i, dt, t0):
                dve.wait_ge(ahi_made, i * DT + dt + 1)
                dve.scalar_tensor_tensor(out=a_lo[:, dt, t0:T], in0=hT[:, dt, t0:T], scalar=gain(2 * i, dt),
                                         in1=a_hi[:, dt, t0:T], op0=ALU.mult,
                                         op1=ALU.subtract).then_inc(alo_made, 1)

            def out_scale(i, half, t0):
                for n in range(4):
                    dt = half * 4 + n
                    dve.wait_ge(m_sq, i * DT + dt + 1)
                    last = dve.tensor_scalar(mT[:, dt, t0:T], ps[:, (X, Y)[half] + n, t0:T],
                                             gain(2 * i + 1, dt), None, ALU.mult)
                last.then_inc(m_scaled, 1)

            def residual(i, t0):
                rsqrt(rs, STAT, t0, ESTIMATE[("post", i)])
                dve.wait_ge(m_scaled, 2 * (i + 1))
                marks = []
                for dt in range(DT + 2):
                    if dt < DT:
                        marks.append(mark(dve.tensor_tensor(mT[:, dt, t0:T], mT[:, dt, t0:T], rs[:, t0:T],
                                                            ALU.mult)))
                    if 1 <= dt <= DT:
                        after(marks[dt - 1])
                        dve.tensor_tensor(hT[:, dt - 1, t0:T], hT[:, dt - 1, t0:T], mT[:, dt - 1, t0:T],
                                          ALU.add).then_inc(h_new, 1)
                    if dt >= 2:
                        norm_low(i + 1, dt - 2, t0)

            dve.memset(eps_sb[:], EPS).then_inc(eps_set, 1)
            dve.wait_ge(gain_up, 1)
            link(dve.tensor_copy(gains_sb[:], ps[:, GAINS, 0:8 * DT]))
            norms = gains_sb.rearrange("p (i w d) -> p i w d", w=2, d=DT)
            dve.tensor_scalar(norms[:, :, 0, :], norms[:, :, 0, :], A_SCALE, None, ALU.mult)
            dve.tensor_scalar(norms[:, :, 1, :], norms[:, :, 1, :], -UNSCALE / 2, None,
                              ALU.mult).then_inc(gain_ready, 1)
            for dt in range(DT):
                dve.wait_ge(xT_up, dt + 1)
                dve.tensor_copy(hT[:, dt, :], ps[:, dt, 0:T]).then_inc(h_in, 1)
                if dt:
                    norm_low(0, dt - 1, 0)
            norm_low(0, DT - 1, 0)
            for c in range(2):
                for q in range(SUB):
                    prep(c, q)
                    if (c, q) == (1, 1):
                        rsqrt_input(0, 0)
            dve.wait_ge(table_landed, 32)
            link(dve.tensor_tensor(rope_sb[:], rope_sb[:], rs_in[:].unsqueeze(1).to_broadcast([P, 2, T]),
                                   ALU.mult))

            def times_rs(dst, first, t0=0):
                return dve.tensor_tensor(dst[:, :, t0:T], ps[:, first:first + 4, t0:T],
                                         rs_in[:, t0:T].unsqueeze(1).to_broadcast([P, 4, T - t0]), ALU.mult)

            def head_y(h):
                dve.wait_ge(g_silu, h + 1)
                link(dve.scalar_tensor_tensor(out=oT, in0=oT, scalar=-A_SCALE / 2, in1=gT, op0=ALU.mult,
                                              op1=ALU.mult))
                dve.tensor_tensor(oT, oT, rs[:, 0:T].unsqueeze(1).to_broadcast([P, 4, T]),
                                  ALU.mult).then_inc(y_raw, 1)

            def head_low(h):
                dve.wait_ge(yhi_made, h + 1)
                dve.tensor_tensor(y_lo[:, 4 * h:4 * h + 4, :], oT, y_hi[:, 4 * h:4 * h + 4, :],
                                  ALU.subtract).then_inc(ylo_made, 1)

            def parameters():
                dve.wait_ge(par_up, 1)
                link(dve.tensor_copy(par[:], ps[:, PARAMS, 0:PAR_ROWS[1]]))
                for layer in range(2):
                    for tap in range(4):
                        col = PAR_COL[2 + 2 * layer + tap // 2] + tap % 2 * 2 * FT
                        for g in range(2):
                            scale = A_SCALE if g == 0 else 1.0
                            if tap < 3:
                                scale *= -UNSCALE / 2
                            last = dve.tensor_scalar(
                                cpar[:, layer, :, cpar_col(tap, 2 * g):cpar_col(tap, 2 * g) + 2],
                                ps[:, PARAMS, col + g * FT:col + (g + 1) * FT].rearrange("p (j n) -> p j n", n=2),
                                scale, None, ALU.mult)
                last.then_inc(par_raw, 1)
                link(dve.tensor_scalar(par[:, LC:LC + 32], par[:, LC:LC + 32], -0.5 * UNSCALE * A_SCALE, None,
                                       ALU.mult))
                dve.tensor_scalar(par[:, LB:LB + 8], par[:, LB:LB + 8], A_SCALE, None,
                                  ALU.mult).then_inc(par_ready, 1)

            def lru_rates():
                dve.wait_ge(lam_exp, 1)
                t_, z, z2, p_ = lam[:, 1, :], lam[:, 2, :], lam[:, 3, :], lam[:, 4, :]
                link(dve.tensor_scalar(z, t_, 2.0, None, ALU.add))
                link(dve.reciprocal(z2, z))
                link(dve.tensor_tensor(z, t_, z2, ALU.mult))
                link(dve.tensor_tensor(z2, z, z, ALU.mult))
                link(dve.tensor_scalar(p_, z2, 1.0 / 19, None, ALU.mult))
                for n in range(17, 1, -2):
                    link(dve.scalar_tensor_tensor(out=p_, in0=p_, scalar=1.0 / n, in1=z2, op0=ALU.add,
                                                  op1=ALU.mult))
                link(dve.scalar_tensor_tensor(out=p_, in0=p_, scalar=1.0, in1=z, op0=ALU.add, op1=ALU.mult))
                link(dve.tensor_scalar(z, par[:, LL:LL + 16], -1.0, 0.0, ALU.mult, ALU.max))
                link(dve.scalar_tensor_tensor(out=z2, in0=p_, scalar=2.0, in1=z, op0=ALU.mult, op1=ALU.add))
                dve.tensor_scalar(spc[:, 0, :], z2, 4.0, None, ALU.mult)
                dve.tensor_scalar(spc[:, 1, :], z2, -8.0, None, ALU.mult).then_inc(par_ready, 1)

            cos = rope_sb[:, 0:1, :].to_broadcast([P, 2, T])
            sin = rope_sb[:, 1:2, :].to_broadcast([P, 2, T])
            for h in range(HEADS):
                c = RET_IN[h]
                qk = ps[:, X:X + 4, 0:T].rearrange("p (g x) t -> p x g t", x=2)
                rot = rotq.rearrange("p (g x) t -> p x g t", x=2)
                dve.wait_ge(w_used, used(c))
                prods = [mark(dve.tensor_tensor(to, qk[:, x], by, ALU.mult)) for to, x, by in (
                    (rot[:, 0], 0, cos), (rotp[:, 0], 1, sin), (rot[:, 1], 1, cos), (rotp[:, 1], 0, sin))]
                after(prods[1])
                dve.tensor_tensor(rot[:, 0], rot[:, 0], rotp[:, 0], ALU.subtract)
                after(prods[3])
                dve.tensor_tensor(rot[:, 1], rot[:, 1], rotp[:, 1], ALU.add).then_inc(rot_done, 1)
                prep(c + 2, 0)
                dve.wait_ge(qkhi_made, h + 1)
                dve.tensor_tensor(qk_lo, rotq, qk_hi, ALU.subtract).then_inc(qklo_made, 1)
                prep(c + 2, 1)
                prep(c + 2, 2)
                dve.wait_ge(w_used, used(c + 1))
                times_rs(vT, Y).then_inc(v_out, 1)
                prep(c + 2, 3)
                if h:
                    rsqrt(rs, GN, 0, ESTIMATE[("head", h - 1)])
                dve.wait_ge(s_up, h + 1)
                for n, (m0, m) in enumerate(TOK_TILES):
                    last = dve.tensor_tensor(sT[0:m, n, :], ps[0:m, X + n, 0:T],
                                             decay_sb[0:m, h, 2 * P - m0:2 * P - m0 + T], ALU.mult)
                last.then_inc(s_dec, 1)
                dve.wait_ge(shi_made, h + 1)
                dve.tensor_tensor(s_lo[:, 0:2, :], sT[:, 0:2, :], s_hi[:, 0:2, :], ALU.subtract)
                dve.tensor_tensor(s_lo[0:META, 2, :], sT[0:META, 2, :], s_hi[0:META, 2, :],
                                  ALU.subtract).then_inc(slo_made, 1)
                for n, (_, m) in enumerate(TOK_TILES):
                    dve.wait_ge(vs_out, NTT * h + n + 1)
                    dve.tensor_scalar(vsum[0:m, n, 1:2], vsum[0:m, n, 0:1], -1.0 / HEAD_V, None,
                                      ALU.mult).then_inc(vmean, 1)
                for n, (_, m) in enumerate(TOK_TILES):
                    dve.wait_ge(vhi_made, NTT * h + n + 1)
                    last = dve.scalar_tensor_tensor(out=v_lo[0:m, n, :], in0=vs[0:m, n, :],
                                                    scalar=vsum[0:m, n, 1:2], in1=v_hi[0:m, n, :],
                                                    op0=ALU.add, op1=ALU.subtract)
                last.then_inc(vlo_made, 1)
                prep(c + 3, 0)
                if h:
                    head_y(h - 1)
                    head_low(h - 1)
                else:
                    parameters()
                prep(c + 3, 1)
                dve.wait_ge(w_used, used(c + 2))
                times_rs(gT, X).then_inc(g_out, 1)
                prep(c + 3, 2)
                prep(c + 3, 3)
                for q in range(SUB):
                    prep(c + 4, q)
                if h == 0:
                    lru_rates()

            c = RET_OUT
            rsqrt(rs, Y, 0, ESTIMATE[("head", HEADS - 1)])
            head_y(HEADS - 1)
            head_low(HEADS - 1)
            for q in range(SUB):
                prep(c + 2, q)
            out_scale(0, 0, 0)
            for n in (3, 4):
                for q in range(SUB):
                    prep(c + n, q)
            out_scale(0, 1, 0)
            residual(0, 0)
            for q in range(SUB):
                prep(c + 5, q)
                if q == 1:
                    rsqrt_input(1, 0)

            def ffn_chunk(layer, first_in, i, b):
                t0 = ffn_first(layer)
                c, s = first_in + b, (X, Y)[b]
                n0 = layer * FFN_CHUNKS + b + 2 * i
                dve.wait_ge(w_used, used(c) + 2 * SUB * i)
                times_rs(u_in[b], s, t0).then_inc(u_out, 1)
                prep(c + 2, 0, i)
                prep(c + 2, 1, i)
                dve.wait_ge(mid_tap, n0 + 1)
                order = (2, 3, 0, 1)
                for n in order:
                    dve.scalar_tensor_tensor(
                        out=u_cv[b][:, n, t0 + 1:T], in0=u_in[b][:, n, t0:T - 1],
                        scalar=cnow[b][:, cpar_col(0, n):cpar_col(0, n) + 1],
                        in1=u_cv[b][:, n, t0 + 1:T], op0=ALU.mult, op1=ALU.add).then_inc(left_tap, 1)
                for m, n in enumerate(order):
                    dve.wait_ge(left_tap, 4 * n0 + m + 1)
                    last = dve.scalar_tensor_tensor(
                        out=u_cv[b][:, n, t0:T - 1], in0=u_in[b][:, n, t0 + 1:T],
                        scalar=cnow[b][:, cpar_col(2, n):cpar_col(2, n) + 1],
                        in1=u_cv[b][:, n, t0:T - 1], op0=ALU.mult, op1=ALU.add)
                last.then_inc(conv_done, 1)
                prep(c + 2, 2, i)
                prep(c + 2, 3, i)

            def ffn_in(layer, first_in):
                for b in range(2):
                    ffn_chunk(layer, first_in, 0, b)
                with dve.Fori(1, FFN_CHUNKS // 2) as i:
                    for b in range(2):
                        ffn_chunk(layer, first_in, i, b)

            ffn_in(0, FFN0_IN)
            for c in range(FFN0_OUT + 2, XR0 + 1):
                if c == ffn_out(0, 2 * FFN_OUT_K - 1):
                    out_scale(1, 0, 0)
                for q in range(SUB):
                    prep(c, q)
            out_scale(1, 1, 0)
            residual(1, 0)
            prep(XR1, 0)
            prep(XR1, 1)
            rsqrt_input(2, 0)

            for k, c in ((0, XR0), (1, XR1)):
                dve.wait_ge(w_used, used(c))
                times_rs(x_raw[k], (X, Y)[k]).then_inc(x_out, 1)
                if k == 0:
                    prep(XR1, 2)
                    prep(XR1, 3)
                prep(c + 2, 0)
                prep(c + 2, 1)
                dve.wait_ge(x_mid, k + 1)
                taps = [t for t in range(LRU_TAPS) if t != LRU_LEFT]
                done = {}
                for t in taps:
                    sh = t - LRU_LEFT
                    a, b = max(0, -sh), T - max(0, sh)
                    for n in range(4):
                        j = 4 * k + n
                        if n in done:
                            after(done[n])
                        last = dve.scalar_tensor_tensor(
                            out=xc[:, j, a:b], in0=x_raw[k][:, n, a + sh:b + sh], scalar=lpar(LC, t * DT + j),
                            in1=xc[:, j, a:b], op0=ALU.mult, op1=ALU.add)
                        if t != taps[-1]:
                            done[n] = mark(last)
                last.then_inc(x_conv, 1)
                dve.wait_ge(xhi_made, k + 1)
                dve.tensor_tensor(xc_lo[k], xc[:, 4 * k:4 * k + 4, :], xc_hi[k],
                                  ALU.subtract).then_inc(xlo_made, 1)
                prep(c + 2, 2)
                prep(c + 2, 3)

            def lru_v(blk):
                dve.wait_ge(half_up, blk + 1)
                link(dve.scalar_tensor_tensor(out=l_prod, in0=lr[blk], scalar=1.0, in1=la[blk], op0=ALU.add,
                                              op1=ALU.mult))
                link(dve.scalar_tensor_tensor(out=la[blk], in0=l_prod, scalar=2.0, in1=la[blk],
                                              op0=ALU.subtract, op1=ALU.mult))

            def lru_scan(blk):
                dve.wait_ge(ix_made, blk + 1)
                mark(dve.tensor_scalar(lr[blk], la[blk], -2.0, -1.0, ALU.mult, ALU.add))
                link(dve.scalar_tensor_tensor(out=li[blk], in0=la[blk], scalar=-2.0, in1=li[blk],
                                              op0=ALU.mult, op1=ALU.mult))
                for d, h in ((0, hf), (1, hb)):
                    for m in range(2):
                        way = slice(None, None, 1 - 2 * d)
                        last = dve.tensor_tensor_scan(h[:, 2 * blk + m, way], lr[blk][:, d, m, way],
                                                      li[blk][:, d, m, way], 0.0, ALU.mult, ALU.add)
                last.then_inc(scanned, 1)

            def lru_y(blk):
                two = slice(2 * blk, 2 * blk + 2)
                gg = ggel[blk // 2][:, 2 * (blk % 2):2 * (blk % 2) + 2, :]
                dve.wait_ge(both, blk + 1)
                dve.wait_ge(gt_gelu, blk // 2 + 1)
                dve.tensor_tensor(xc[:, two, :], hf[:, two, :], gg, ALU.mult).then_inc(ly_raw, 1)

            def lru_y_low(blk):
                two = slice(2 * blk, 2 * blk + 2)
                dve.wait_ge(yhi_made, Y_LRU + blk + 1)
                dve.tensor_tensor(y_lo[:, two, :], xc[:, two, :], y_hi[:, two, :],
                                  ALU.subtract).then_inc(ylo_made, 1)

            lru_v(0)
            lru_v(1)
            dve.wait_ge(w_used, used(GT0))
            times_rs(ggel[0], X).then_inc(gt_out, 1)
            lru_scan(0)
            lru_scan(1)
            prep(LRU_OUT, 0)
            lru_y(0)
            lru_y(1)
            for q in range(1, SUB):
                prep(LRU_OUT, q)
            lru_y_low(0)
            lru_y_low(1)
            lru_v(2)
            lru_v(3)
            dve.wait_ge(w_used, used(GT1))
            times_rs(ggel[1], Y).then_inc(gt_out, 1)
            lru_scan(2)
            dve.wait_ge(root, 4)
            dve.tensor_tensor(li[3], li[3], lq[3], ALU.mult).then_inc(ix_made, 1)
            lru_scan(3)
            lru_y(2)
            dve.wait_ge(scanned, 4)
            dve.tensor_tensor(hf[:, 6:8, :], hf[:, 6:8, :], hb[:, 6:8, :], ALU.add).then_inc(both, 1)
            lru_y_low(2)
            lru_y(3)
            lru_y_low(3)
            for q in range(SUB):
                prep(LRU_OUT + 1, q)
            for q in range(SUB):
                prep(LRU_OUT + 2, q)
            out_scale(2, 0, T0_LRU_OUT)
            out_scale(2, 1, T0_LRU_OUT)
            residual(2, T0_LRU_OUT)
            for q in range(SUB):
                prep(LRU_OUT + 3, q)
                if q == 1:
                    rsqrt_input(3, T0_LRU_OUT)

            ffn_in(1, FFN1_IN)
            for n in range(2 * FFN_OUT_K):
                c = FFN1_OUT + n
                if c + 2 < CHUNKS:
                    for q in range(SUB):
                        prep(c + 2, q)
                if n in (FFN_OUT_K, 2 * FFN_OUT_K - 1):
                    half = n // FFN_OUT_K - (n == FFN_OUT_K)
                    if half == 0:
                        dve.wait_ge(g_row_landed, 16)
                    for tt in range(2):
                        b = 2 * half + tt
                        dve.wait_ge(fin_sum, b + 1)
                        if b == 3:
                            dve.tensor_tensor(fin_s[:, 2, :], fin_s[:, 0, :], fin_s[:, 1, :],
                                              ALU.add).then_inc(fin_ms, 1)
                        dve.scalar_tensor_tensor(out=fin[:, tt, half * BANK:(half + 1) * BANK],
                                                 in0=ps[:, (X, Y)[half] + tt, :], scalar=-UNSCALE / 2,
                                                 in1=g_row[:, half * BANK:(half + 1) * BANK],
                                                 op0=ALU.mult, op1=ALU.mult).then_inc(fin_m, 1)
            ms, r0, t_, r = fin_s[:, 2, :], fin_s[:, 3, :], fin_s[:, 4, :], fin_s[:, 5, :]
            dve.wait_ge(fin_est, 1)
            link(dve.tensor_scalar(ms, ms, 1.0 / D, EPS, ALU.mult, ALU.add))
            link(dve.tensor_tensor(t_, r0, r0, ALU.mult))
            link(dve.tensor_tensor(t_, t_, ms, ALU.mult))
            link(dve.scalar_tensor_tensor(out=r, in0=t_, scalar=3.0, in1=r0, op0=ALU.subtract, op1=ALU.mult))
            dve.wait_ge(fin_m, 4)
            dve.wait_ge(hrow_up, 1)
            for b in range(4):
                tt, cols = b // 2, slice(b % 2 * BANK, (b % 2 + 1) * BANK)
                dve.scalar_tensor_tensor(out=fin[:, tt, cols], in0=fin[:, tt, cols], scalar=r[:, tt:tt + 1],
                                         in1=ps[:, H_ROW[b], :], op0=ALU.mult,
                                         op1=ALU.add).then_inc(fin_out, 1)

        @block.gpsimd
        def _(pool):
            step = [0]

            def link(ins):
                step[0] += 1
                ins.then_inc(pool_step, 1)
                pool.wait_ge(pool_step, step[0])

            def sum_tiles(signal, n_tiles, t0, ready, n_ready):
                pool.wait_ge(ready, n_ready + 2)
                ins = pool.tensor_tensor(sq_sum[:, t0:T], sq[:, 0, t0:T], sq[:, 1, t0:T], ALU.add)
                for dt in range(2, n_tiles):
                    link(ins)
                    pool.wait_ge(ready, n_ready + dt + 1)
                    ins = pool.tensor_tensor(sq_sum[:, t0:T], sq_sum[:, t0:T], sq[:, dt, t0:T], ALU.add)
                ins.then_inc(signal, 1)

            def sum_output(i, t0):
                sum_tiles(sum_m, 4, t0, m_sq, i * DT)

            def sum_input(i, t0):
                if i:
                    pool.wait_ge(ms_up, MEAN[("post", i - 1)])
                sum_tiles(sum_h, DT, t0, h_sq, i * DT)

            def ffn_chunk(layer, i, b):
                t0 = ffn_first(layer)
                n0 = layer * FFN_CHUNKS + b + 2 * i
                dynamic = not isinstance(i, int)
                if layer or dynamic:
                    pool.wait_ge(conv_done, n0 - 1)
                here = cpar[:, layer, bass.ds(2 * i + b, 1), :] if dynamic else cpar[:, layer, 2 * i + b:2 * i + b + 1, :]
                pool.tensor_copy(cnow[b][:].unsqueeze(1), here).then_inc(cnow_set, 1)
                pool.wait_ge(gelu_done, n0 + 1)
                pool.tensor_tensor(u_y[b][:, :, t0:T], u_y[b][:, :, t0:T], u_cv[b][:, 0:2, t0:T],
                                   ALU.mult).then_inc(fy_raw, 1)
                pool.wait_ge(yhi_made, Y_FFN[layer] + b + 2 * i + 1)
                two = bass.ds(4 * i + 2 * b, 2) if dynamic else slice(4 * i + 2 * b, 4 * i + 2 * b + 2)
                pool.tensor_tensor(y_lo[:, two, t0:T], u_y[b][:, :, t0:T], y_hi[:, two, t0:T],
                                   ALU.subtract).then_inc(fylo_made, 1)

            def ffn_in(layer):
                for b in range(2):
                    ffn_chunk(layer, 0, b)
                with pool.Fori(1, FFN_CHUNKS // 2) as i:
                    for b in range(2):
                        ffn_chunk(layer, i, b)

            sum_input(0, 0)
            pool.wait_ge(ms_up, MEAN[("pre", 0)])
            sum_output(0, 0)
            sum_input(1, 0)
            pool.wait_ge(par_ready, 1)
            ffn_in(0)
            sum_output(1, 0)
            sum_input(2, 0)
            for k in range(2):
                pool.wait_ge(x_out, k + 1)
                for n in range(4):
                    j = 4 * k + n
                    last = pool.tensor_scalar(xc[:, j, :], x_raw[k][:, n, :], lpar(LC, LRU_LEFT * DT + j),
                                              lpar(LB, j), ALU.mult, ALU.add)
                last.then_inc(x_mid, 1)
            def gated_x(n):
                blk, d = n // 2, n % 2
                u = li[blk][:, d]
                pool.wait_ge(r_out, n + 1)
                link(pool.tensor_tensor(u, u, xc[:, 2 * blk:2 * blk + 2, :], ALU.mult))

            def half(blk):
                pool.wait_ge(rates, blk + 1)
                pool.tensor_scalar(la[blk], la[blk], 0.5, 0.5, ALU.mult, ALU.add).then_inc(half_up, 1)

            def times_root(blk):
                pool.wait_ge(root, blk + 1)
                pool.tensor_tensor(li[blk], li[blk], lq[blk], ALU.mult).then_inc(ix_made, 1)

            def add_scans(blk):
                two = slice(2 * blk, 2 * blk + 2)
                pool.wait_ge(scanned, blk + 1)
                pool.tensor_tensor(hf[:, two, :], hf[:, two, :], hb[:, two, :], ALU.add).then_inc(both, 1)

            for n in range(4):
                gated_x(n)
            for half_or_root in (half, times_root):
                for blk in (0, 1):
                    half_or_root(blk)
            gated_x(4)
            add_scans(0)
            gated_x(5)
            add_scans(1)
            gated_x(6)
            gated_x(7)
            half(2)
            half(3)
            times_root(2)
            add_scans(2)
            sum_output(2, T0_LRU_OUT)
            sum_input(3, T0_LRU_OUT)
            ffn_in(1)

        @block.tensor
        def _(pe):
            def three(o, w_h, w_l, x_h, x_l, start, stop):
                pe.matmul(o, w_h, x_h, start=start, stop=False)
                pe.matmul(o, w_h, x_l, start=False, stop=False)
                return pe.matmul(o, w_l, x_h, start=False, stop=stop)

            def chunk(c, banks, xh, xl, k0, t0, first=True, last=True, need=None, i=0, stat=None, bank3=None):
                s = c % 2
                for k in range(KC):
                    if k % 2 == 0:
                        pe.wait_ge(wlo_made, SUB * c + k // 2 + 1 + 2 * SUB * i)
                    if need:
                        need(k0 + k)
                    if stat and k == KC - 1:
                        stat()
                    for n in range(4):
                        if bank3 and k == 0 and n == 3:
                            bank3()
                        col = slice(n * P, (n + 1) * P)
                        mm = three(ps[:, banks + n, t0:T], w_hi[s][:, k, col], w_lo[s][:, k, col],
                                   xh[:, k0 + k, t0:T], xl[:, k0 + k, t0:T],
                                   first and k == 0, last and k == KC - 1)
                    if k % 2 == 1:
                        mm.then_inc(w_used, 1)

            def normed(i):
                return lambda k: pe.wait_ge(alo_made, i * DT + k + 1)

            def mean_input(i, t0):
                def issue():
                    pe.wait_ge(sum_h, i + 1)
                    pe.matmul(ps[:, STAT_IN, t0:T], ones_sb[:, 0, :], sq_sum[:, t0:T], start=True,
                              stop=True).then_inc(ms_up, 1)
                return issue

            def stat_in_read(i):
                return lambda: pe.wait_ge(rs_made, ESTIMATE[("pre", i)])

            def mean_output(i, t0):
                pe.wait_ge(m_scaled, 2 * i + 1)
                pe.wait_ge(sum_m, i + 1)
                pe.matmul(ps[:, STAT, t0:T], ones_sb[:, 0, :], sq_sum[:, t0:T], start=True, stop=False)
                for dt in range(4, DT):
                    pe.wait_ge(m_sq, i * DT + dt + 1)
                    mm = pe.matmul(ps[:, STAT, t0:T], ones_sb[:, 0, :], sq[:, dt, t0:T], start=False,
                                   stop=dt == DT - 1)
                mm.then_inc(ms_up, 1)

            pe.wait_ge(x_landed, 5 * 16)
            pe.wait_ge(gain_landed, 16)
            pe.transpose(ps[:, GAINS, 0:8 * DT], prow[0:8 * DT, 0, :],
                         ident_sb[0:8 * DT, 0:8 * DT]).then_inc(gain_up, 1)
            for dt in range(DT):
                if dt == GAINS:
                    pe.wait_ge(gain_ready, 1)
                for n, (t0, t) in enumerate(TOK_TILES):
                    mm = pe.transpose(ps[:, dt, t0:t0 + t], x_in[0:t, n, dt * P:(dt + 1) * P],
                                      ident_sb[0:t, 0:t])
                mm.then_inc(xT_up, 1)
            pe.wait_ge(const_landed, 16)

            def head_norm(h, bank):
                pe.wait_ge(o_sq, h + 1)
                for e in range(4):
                    mm = pe.matmul(ps[:, bank, 0:T], ones_sb[:, 1, :], osq[:, e, :], start=e == 0, stop=e == 3)
                mm.then_inc(gn_up, 1)

            for h in range(HEADS):
                c = RET_IN[h]
                if h:
                    pe.wait_ge(g_out, h)
                    chunk(c, X, a_hi, a_lo, 0, 0)
                    pe.wait_ge(o_sq, h)
                    chunk(c + 1, Y, a_hi, a_lo, 0, 0)
                else:
                    chunk(c, X, a_hi, a_lo, 0, 0, need=normed(0), stat=mean_input(0, 0))
                    chunk(c + 1, Y, a_hi, a_lo, 0, 0, bank3=stat_in_read(0))
                pe.wait_ge(rot_done, h + 1)
                if h:
                    head_norm(h - 1, GN)
                pe.wait_ge(qklo_made, h + 1)
                for n, (m0, m) in enumerate(TOK_TILES):
                    for k in range(2):
                        key = slice(m0, m0 + m)
                        mm = three(ps[0:m, X + n, 0:T], qk_hi[:, 2 + k, key], qk_lo[:, 2 + k, key],
                                   qk_hi[:, k, :], qk_lo[:, k, :], k == 0, k == 1)
                mm.then_inc(s_up, 1)
                pe.wait_ge(v_out, h + 1)
                for n, (m0, m) in enumerate(TOK_TILES):
                    for e in range(4):
                        mm = pe.transpose(ps[0:m, Y + n, e * P:(e + 1) * P], vT[:, e, m0:m0 + m], ident_sb[:])
                mm.then_inc(vt_up, 1)
                if h == 0:
                    pe.wait_ge(par_landed, 16 * len(param_loads))
                    for t in range(1, 6):
                        rows = PAR_ROWS[t]
                        mm = pe.transpose(ps[:, PARAMS, PAR_COL[t]:PAR_COL[t] + rows], prow[0:rows, t, :],
                                          ident_sb[0:rows, 0:rows])
                    mm.then_inc(par_up, 1)
                pe.wait_ge(s_dec, h + 1)
                if h:
                    pe.wait_ge(rs_made, ESTIMATE[("head", h - 1)])
                chunk(c + 2, X, a_hi, a_lo, 0, 0)
                pe.wait_ge(vs_out, NTT * (h + 1))
                pe.wait_ge(vlo_made, h + 1)
                pe.wait_ge(slo_made, h + 1)
                if h == 0:
                    pe.wait_ge(par_raw, 1)
                for e in range(4):
                    col = slice(e * P, (e + 1) * P)
                    for n, (m0, m) in enumerate(TOK_TILES):
                        mm = three(ps[:, Y + e, 0:T], v_hi[0:m, n, col], v_lo[0:m, n, col],
                                   s_hi[0:m, n, :], s_lo[0:m, n, :], n == 0, n == NTT - 1)
                mm.then_inc(o_up, 1)

            def heads(k):
                pe.wait_ge(ylo_made, k // 4 + 1)

            c = RET_OUT
            pe.wait_ge(g_out, HEADS)
            chunk(c, X, y_hi, y_lo, 0, 0, last=False, need=heads)
            head_norm(HEADS - 1, Y)
            chunk(c + 1, X, y_hi, y_lo, KC, 0, first=False, need=heads)
            chunk(c + 2, Y, y_hi, y_lo, 0, 0, last=False)
            chunk(c + 3, Y, y_hi, y_lo, KC, 0, first=False)
            mean_output(0, 0)

            def ffn_in(layer, first_in, i_sub):
                t0 = ffn_first(layer)
                chunk(first_in, X, a_hi, a_lo, 0, t0, need=normed(i_sub), stat=mean_input(i_sub, t0))
                chunk(first_in + 1, Y, a_hi, a_lo, 0, t0, bank3=stat_in_read(i_sub))
                with pe.Fori(1, FFN_CHUNKS // 2) as i:
                    for b in range(2):
                        pe.wait_ge(u_out, layer * FFN_CHUNKS + b - 1 + 2 * i)
                        chunk(first_in + b, (X, Y)[b], a_hi, a_lo, 0, t0, i=i)

            def gated(layer):
                return lambda k: pe.wait_ge(fylo_made, layer * FFN_CHUNKS + k // 2 + 1)

            ffn_in(0, FFN0_IN, 1)
            for n in range(2 * FFN_OUT_K):
                half, kg = divmod(n, FFN_OUT_K)
                if kg == 0:
                    pe.wait_ge(u_out, FFN_CHUNKS - 1 + half)
                chunk(ffn_out(0, n), (X, Y)[half], y_hi, y_lo, kg * KC, 0, kg == 0, kg == FFN_OUT_K - 1,
                      need=gated(0) if half == 0 else None)
            mean_output(1, 0)

            def lru_gates(k, free):
                wh, wl = [v[k].rearrange("p (q g k e) -> p q g k e", q=4, g=2, k=2) for v in (gw_hi, gw_lo)]
                for q in range(4):
                    b2 = 2 * (q // 2)
                    s = GATE_SET[4 * k + q]
                    signal, n = free[q]
                    pe.wait_ge(signal, n)
                    for g in range(2):
                        for m in range(2):
                            for kk in range(2):
                                col = slice(m * P, (m + 1) * P)
                                mm = three(ps[:, s + 2 * g + m, 0:T], wh[:, q, g, kk, col],
                                           wl[:, q, g, kk, col], xc_hi[k][:, b2 + kk, :],
                                           xc_lo[k][:, b2 + kk, :], kk == 0, kk == 1)
                    mm.then_inc(gates_up, 1)

            chunk(XR0, X, a_hi, a_lo, 0, 0, need=normed(2), stat=mean_input(2, 0))
            chunk(XR1, Y, a_hi, a_lo, 0, 0, bank3=stat_in_read(2))
            pe.wait_ge(xlo_made, 1)
            lru_gates(0, [(x_out, 1), (x_out, 2), (r_out, 1), (r_out, 2)])
            pe.wait_ge(r_out, 3)
            chunk(GT0, X, a_hi, a_lo, 0, 0)
            pe.wait_ge(xlo_made, 2)
            lru_gates(1, [(r_out, 4), (gt_out, 1), (r_out, 5), (r_out, 6)])
            pe.wait_ge(r_out, 7)
            chunk(GT1, Y, a_hi, a_lo, 0, 0)
            pe.wait_ge(r_out, 8)
            chunk(LRU_OUT, X, y_hi, y_lo, 0, T0_LRU_OUT,
                  need=lambda k: pe.wait_ge(ylo_made, HEADS + k // 2 + 1))
            pe.wait_ge(gt_out, 2)
            chunk(LRU_OUT + 1, Y, y_hi, y_lo, 0, T0_LRU_OUT)
            mean_output(2, T0_LRU_OUT)

            ffn_in(1, FFN1_IN, 3)
            pe.wait_ge(u_out, 2 * FFN_CHUNKS)
            for b in range(4):
                tt, half = b // 2, b % 2
                for n in range(4):
                    t0 = META + tt * P
                    mm = pe.transpose(ps[:, H_ROW[b], n * P:(n + 1) * P], hT[:, half * 4 + n, t0:t0 + P],
                                      ident_sb[:])
            mm.then_inc(hrow_up, 1)
            for n in range(2 * FFN_OUT_K):
                c, (half, kg) = FFN1_OUT + n, divmod(n, FFN_OUT_K)
                for k in range(KC):
                    if k % 2 == 0:
                        pe.wait_ge(wlo_made, SUB * c + k // 2 + 1)
                    if half == 0:
                        gated(1)(kg * KC + k)
                    wh, wl = w_hi[c % 2][:, k, :], w_lo[c % 2][:, k, :]
                    for tt in range(2):
                        tok = slice(META + tt * P, META + (tt + 1) * P)
                        yh, yl = y_hi[:, kg * KC + k, tok], y_lo[:, kg * KC + k, tok]
                        o = ps[:, (X, Y)[half] + tt, :]
                        start, stop = kg == 0 and k == 0, kg == FFN_OUT_K - 1 and k == KC - 1
                        pe.matmul(o, yh, wh, start=start, stop=False)
                        pe.matmul(o, yh, wl, start=False, stop=False)
                        mm = pe.matmul(o, yl, wh, start=False, stop=stop)
                    if k % 2 == 1:
                        mm.then_inc(w_used, 1)


_INS = ["x", "meta_tokens", "norm_gains", "ret_w_in", "ret_w_out", "lru_w_in", "lru_conv_w", "lru_conv_b",
        "lru_w_a", "lru_b_a", "lru_w_i", "lru_b_i", "lru_lambda", "lru_w_out", "ffn_w_in", "ffn_conv_w",
        "ffn_conv_b", "ffn_w_out"]


def constants():
    ident = np.eye(P, dtype=np.float32)
    ones = np.empty((P, 2, P), np.float32)
    ones[:, 0] = 1.0 / D
    ones[:, 1] = 1.0 / HEAD_V
    d = D // HEADS
    inv = np.float32(10000.0) ** (-np.arange(0, d, 2, dtype=np.float32) / np.float32(d))
    ang = np.arange(T, dtype=np.float32)[None, :] * inv[:, None]
    rope = np.stack([np.cos(ang), np.sin(ang)], 1).astype(np.float32) * np.float32(-0.5 * UNSCALE * A_SCALE)
    away = np.abs(np.arange(DECAY_W)[None, :] - 2 * P - np.arange(P)[:, None]).astype(np.float64)
    log_gamma = np.log1p(-np.exp2(-5.0 - np.arange(HEADS)))
    decay = np.exp(log_gamma[None, :, None] * away[:, None, :]) * d ** -0.5 / A_SCALE
    return {"ident": ident, "ones": ones, "rope": rope, "decay": decay.astype(np.float32)}


def kernel(**inputs):
    import concourse.bacc as bacc
    from concourse.bass_utils import run_bass_kernel_spmd

    nc = bacc.Bacc("TRN2", target_bir_lowering=False, num_devices=1)
    arrays, args = {}, []
    named = {name: np.ascontiguousarray(inputs[name]) for name in _INS} | constants()
    for name, a in named.items():
        arrays[f"in_{name}"] = a
        args.append(nc.dram_tensor(f"in_{name}", a.shape, mybir.dt.from_np(a.dtype), kind="ExternalInput").ap())
    args.append(nc.dram_tensor("out", (1, SEQ, D), F32, kind="ExternalOutput").ap())
    build(nc, *args)
    r = run_bass_kernel_spmd(nc, [arrays], core_ids=[0])
    return r.results[0]["out"]
```

```python
from contextlib import ExitStack

import concourse.bass as bass
from concourse import mybir
import numpy as np

F32 = mybir.dt.float32
F16 = mybir.dt.float16
ALU = mybir.AluOpType
ACTF = mybir.ActivationFunctionType
AX_X = mybir.AxisListType.X

P = 128
BANK = 512
EPS = 1e-6
W_SCALE = 2.0 ** 6
A_SCALE = 2.0 ** 4
UNSCALE = 1.0 / (W_SCALE * A_SCALE)

D = 1024
SEQ = 256
META = 16
T = SEQ + META
DT = D // P
HEADS = 4
FFN = 3 * D
FT = FFN // P
LRU_TAPS, LRU_LEFT = 4, 2
LRU_BLOCKS = 4
TOK_TILES = [(0, P), (P, P), (2 * P, T - 2 * P)]
NTT = len(TOK_TILES)
HEAD_V = 2 * D // HEADS
DECAY_W = 2 * P + T

KC = 8
CW = 512
SUB = 4
RET_IN = [3 * h for h in range(HEADS)]
RET_OUT = 3 * HEADS
FFN_CHUNKS = 2 * FFN // CW
FFN_OUT_K = FFN // (KC * P)
FFN0_IN = RET_OUT + 4
FFN0_OUT = FFN0_IN + FFN_CHUNKS
GW0, GW1 = FFN0_OUT + FFN_OUT_K, FFN0_OUT + FFN_OUT_K + 1
XR0, XR1, GT0, GT1, LRU_OUT = range(FFN0_OUT + 2 * FFN_OUT_K + 2, FFN0_OUT + 2 * FFN_OUT_K + 7)
FFN1_IN = LRU_OUT + 2
FFN1_OUT = FFN1_IN + FFN_CHUNKS
CHUNKS = FFN1_OUT + 2 * FFN_OUT_K

def ffn_out(layer, n):
    return FFN1_OUT + n if layer else FFN0_OUT + n + (2 if n >= FFN_OUT_K else 0)


def used(c, q=SUB - 1):
    return SUB * (c - (2 if c > GW1 else 0)) + q + 1


def before(c):
    return c - (4 if c in (GW1 + 1, GW1 + 2) else 2)


STAGGERED = (RET_OUT + 3, ffn_out(0, 2 * FFN_OUT_K - 1))


def freed(c, q):
    return used(before(c), SUB - 1 if before(c) in STAGGERED else q)


RET_OUT_ORDER = [(0, 0), (0, 1), (1, 0), (1, 1)]

_order = ([("pre", 0)] + [("head", h) for h in range(HEADS)] + [("post", 0)]
          + [(w, i) for i in (1, 2) for w in ("pre", "post")] + [("pre", 3)])
ESTIMATE = {which: n + 1 for n, which in enumerate(_order)}
MEAN = {which: n + 1 for n, which in enumerate(w for w in _order if w[0] != "head")}

Y_FFN = [HEADS, HEADS + FFN_CHUNKS + 4]
Y_LRU = HEADS + FFN_CHUNKS

PAR_ROWS = [8 * DT, 88, 4 * FT, 4 * FT, 4 * FT, 4 * FT]
PAR_COL = [0, 0, 88, 88 + 4 * FT, 88 + 8 * FT, 88 + 12 * FT]

T0_LRU_OUT = META - 2
T0_OUT = META


def ffn_first(layer):
    return 0 if layer == 0 else T0_LRU_OUT


def build(nc, x, meta, gains, ret_w_in, ret_w_out, lru_w_in, lru_conv_w, lru_conv_b, lru_w_a, lru_b_a,
          lru_w_i, lru_b_i, lru_lambda, lru_w_out, ffn_w_in, ffn_conv_w, ffn_conv_b, ffn_w_out,
          ident, ones, rope, decay, out):
    ctx = ExitStack()
    with ctx:
        def sb(name, shape, dt=F32):
            return ctx.enter_context(nc.sbuf_tensor(name, shape, dt))

        def sem(name):
            return ctx.enter_context(nc.semaphore(name))

        stage = [sb(f"stage{s}", [P, KC, CW]) for s in range(2)]
        w_hi = [sb(f"w_hi{s}", [P, KC, CW], F16) for s in range(2)]
        w_lo = [sb(f"w_lo{s}", [P, KC, CW], F16) for s in range(2)]
        hT = sb("hT", [P, DT, T])
        mT = sb("mT", [P, DT, T])
        sq = sb("sq", [P, DT, T])
        a_hi = sb("a_hi", [P, DT, T], F16)
        a_lo = sb("a_lo", [P, DT, T], F16)
        y_hi = sb("y_hi", [P, FT, T], F16)
        y_lo = sb("y_lo", [P, FT, T], F16)
        ident_sb = sb("ident_sb", [P, P])
        ones_sb = sb("ones_sb", [P, 2, P])
        rope_sb = sb("rope_sb", [P, 2, T])
        decay_all = sb("decay_all", [P, 8 * T])
        decay_sb = decay_all[:, 0:HEADS * DECAY_W].rearrange("p (h j) -> p h j", j=DECAY_W)
        prow = sb("prow", [P, 6, P])
        gains_sb = sb("gains_sb", [P, 8 * DT])
        par = sb("par", [P, PAR_ROWS[1]])
        eps_sb = sb("eps_sb", [P, 1])
        est_warm = sb("est_warm", [P, 1])
        rs0 = sb("rs0", [P, T])
        rs1 = sb("rs1", [P, T])
        rs = sb("rs", [P, T])
        rs_in = sb("rs_in", [P, T])
        sq_sum = sb("sq_sum", [P, T])
        cpar = sb("cpar", [P, 2, FFN_CHUNKS, 16])
        cnow = [sb(f"cnow{b}", [P, 16]) for b in range(2)]
        fin_s = sb("fin_s", [P, 8, 2])
        lam = sb("lam", [P, 8, 16])
        spc = sb("spc", [P, 2, 16])
        work = sb("work", [P, 10 * 4 * T])
        work16 = sb("work16", [P, 14 * T + 6 * BANK], F16)

        off = 0

        def carve(*shape):
            nonlocal off
            n = int(np.prod(shape))
            v = work[:, off:off + n]
            off += n
            if len(shape) == 2:
                v = v.rearrange("p (a b) -> p a b", b=shape[1])
            if len(shape) == 3:
                v = v.rearrange("p (a b c) -> p a b c", b=shape[1], c=shape[2])
            return v
        x_in = work[:, 0:3 * D].rearrange("p (a b) -> p a b", b=D)
        rotp = carve(2, 2, T)
        rotq = carve(4, T)
        vs = carve(3, BANK)
        sT = rotq[:, 0:3, :]
        oT, gT = mT[:, 0:4, :], mT[:, 4:8, :]
        osq, vT = sq[:, 0:4, :], sq[:, 4:8, :]
        vsum = sb("vsum", [P, 3, 2])
        qk_hi = work16[:, 0:4 * T].rearrange("p (a b) -> p a b", b=T)
        qk_lo = work16[:, 4 * T:8 * T].rearrange("p (a b) -> p a b", b=T)
        v_hi = work16[:, 8 * T:8 * T + 3 * BANK].rearrange("p (a b) -> p a b", b=BANK)
        v_lo = work16[:, 8 * T + 3 * BANK:8 * T + 6 * BANK].rearrange("p (a b) -> p a b", b=BANK)
        s_hi = work16[:, 8 * T + 6 * BANK:11 * T + 6 * BANK].rearrange("p (a b) -> p a b", b=T)
        s_lo = work16[:, 11 * T + 6 * BANK:14 * T + 6 * BANK].rearrange("p (a b) -> p a b", b=T)
        R_HI, R_LO = 32, 64
        off = 0
        u_in = [carve(4, T) for _ in range(2)]
        u_cv = [carve(4, T) for _ in range(2)]
        u_y = [carve(2, T) for _ in range(2)]
        n_parts = KC * CW // 2
        gw_hi, gw_lo = [[work[:, (2 * k + part) * n_parts:(2 * k + part + 1) * n_parts].bitcast(F16)
                         for k in range(2)] for part in range(2)]
        off = 4 * n_parts
        xc = carve(DT, T)
        assert off <= 10 * 4 * T
        hf, hb = sq, mT

        def quad(v, n):
            return v[:, 4 * T * n:4 * T * (n + 1)].rearrange("p (d m t) -> p d m t", d=2, t=T)
        y_hi_rest, y_lo_rest = [v.rearrange("p a b -> p (a b)")[:, DT * T:3 * DT * T].bitcast(F32)
                                for v in (y_hi, y_lo)]
        g0_place, g1_place = work[:, 0:2 * n_parts], work[:, 2 * n_parts:4 * n_parts]
        hf_flat, hb_flat = [v.rearrange("p a b -> p (a b)") for v in (hf, hb)]
        lr = [quad(decay_all, 0), quad(y_lo_rest, 0), quad(y_hi_rest, 0), quad(g0_place, 0)]
        li = [quad(decay_all, 1), quad(y_lo_rest, 1), quad(y_hi_rest, 1), quad(g0_place, 1)]
        la = [quad(hb_flat, 0), quad(hf_flat, 1), quad(hb_flat, 1), quad(g0_place, 2)]
        lq = [quad(hf_flat, 0), la[3], quad(g1_place, 0), quad(g1_place, 1)]
        x_raw = [y_hi_rest[:, 4 * T * k:4 * T * (k + 1)].rearrange("p (a b) -> p a b", b=T) for k in range(2)]
        regions = [work16[:, k * DT * T:(k + 1) * DT * T] for k in range(2)]
        xc_hi = [v[:, 0:4 * T].rearrange("p (a b) -> p a b", b=T) for v in regions]
        xc_lo = [v[:, 4 * T:8 * T].rearrange("p (a b) -> p a b", b=T) for v in regions]
        ggel = [v.bitcast(F32).rearrange("p (a b) -> p a b", b=T) for v in regions]
        l_prod = quad(work16[:, 2 * DT * T:3 * DT * T].bitcast(F32), 0)
        g_row = mT.rearrange("p a b -> p (a b)")[:, 0:D]
        fin = sq.rearrange("p a b -> p (a b)")[:, 0:2 * D].rearrange("p (a b) -> p a b", b=D)
        fin_sq = work[:, 0:BANK]

        ps = ctx.enter_context(nc.psum_tensor("ps", [P, 8, BANK], F32))
        X, Y = 0, 4
        GATE_SET = [X, Y, X, Y, Y, X, Y, X]
        STAT = X
        STAT_IN = Y + 3
        GAINS = Y + 3
        PARAMS = Y + 3
        H_ROW = [X + 2, X + 3, Y + 2, Y + 3]
        GN = X + 3

        def gain(norm, dt):
            return gains_sb[:, norm * DT + dt:norm * DT + dt + 1]

        LC, LB, LBA, LBI, LL = 0, 32, 40, 56, 72

        def lpar(base, i):
            return par[:, base + i:base + i + 1]

        def cpar_col(tap, n):
            return tap * 4 + n

        def tiles(v):
            return v.rearrange("n (t p) -> (n t) p", p=P)

        gain_load = (prow[0:8 * DT, 0, :], gains.rearrange("l n (t p) -> (l n t) p", p=P))
        param_loads = [(prow[LC:LB, 1, :], tiles(lru_conv_w[0])), (prow[LB:LBA, 1, :], tiles(lru_conv_b)),
                       (prow[LBA:LBI, 1, :], tiles(lru_b_a[0])), (prow[LBI:LL, 1, :], tiles(lru_b_i[0])),
                       (prow[LL:LL + 16, 1, :], tiles(lru_lambda[0]))]
        for layer in range(2):
            param_loads += [(prow[0:4 * FT, 2 + 2 * layer, :], tiles(ffn_conv_w[layer, 0:2])),
                            (prow[0:2 * FT, 3 + 2 * layer, :], tiles(ffn_conv_w[layer, 2:3])),
                            (prow[2 * FT:4 * FT, 3 + 2 * layer, :], tiles(ffn_conv_b[layer:layer + 1]))]

        x_landed = sem("x_landed")
        const_landed = sem("const_landed")
        gain_landed = sem("gain_landed")
        par_landed = sem("par_landed")
        table_landed = sem("table_landed")
        first_landed = sem("first_landed")
        w_landed = [[sem(f"w_landed{s}_{j}") for j in range(2)] for s in range(2)]
        whi_made = sem("whi_made")
        wlo_made = sem("wlo_made")
        w_used = sem("w_used")
        bank_up = sem("bank_up")
        xT_up = sem("xT_up")
        h_in = sem("h_in")
        gain_up = sem("gain_up")
        gain_ready = sem("gain_ready")
        par_up = sem("par_up")
        par_raw = sem("par_raw")
        par_ready = sem("par_ready")
        lam_abs = sem("lam_abs")
        lam_exp = sem("lam_exp")
        eps_set = sem("eps_set")
        m_sq = sem("m_sq")
        m_scaled = sem("m_scaled")
        h_new = sem("h_new")
        h_sq = sem("h_sq")
        sum_h = sem("sum_h")
        sum_m = sem("sum_m")
        ms_up = sem("ms_up")
        rs_est = sem("rs_est")
        rs_made = sem("rs_made")
        ahi_made = sem("ahi_made")
        alo_made = sem("alo_made")
        rope_scaled = sem("rope_scaled")
        rot_done = sem("rot_done")
        qkhi_made = sem("qkhi_made")
        qklo_made = sem("qklo_made")
        v_out = sem("v_out")
        s_up = sem("s_up")
        vt_up = sem("vt_up")
        s_dec = sem("s_dec")
        zeroed = sem("zeroed")
        shi_made = sem("shi_made")
        slo_made = sem("slo_made")
        vs_out = sem("vs_out")
        vmean = sem("vmean")
        vhi_made = sem("vhi_made")
        vlo_made = sem("vlo_made")
        g_out = sem("g_out")
        g_silu = sem("g_silu")
        o_up = sem("o_up")
        o_sq = sem("o_sq")
        sum_o = sem("sum_o")
        gn_up = sem("gn_up")
        y_raw = sem("y_raw")
        yhi_made = sem("yhi_made")
        ylo_made = sem("ylo_made")
        cnow_set = sem("cnow_set")
        u_out = sem("u_out")
        mid_tap = sem("mid_tap")
        left_tap = sem("left_tap")
        conv_done = sem("conv_done")
        gelu_done = sem("gelu_done")
        fy_raw = sem("fy_raw")
        fylo_made = sem("fylo_made")
        x_out = sem("x_out")
        x_mid = sem("x_mid")
        x_conv = sem("x_conv")
        xhi_made = sem("xhi_made")
        xlo_made = sem("xlo_made")
        gates_up = sem("gates_up")
        r_out = sem("r_out")
        exps = sem("exps")
        rates = sem("rates")
        half_up = sem("half_up")
        root = sem("root")
        ix_made = sem("ix_made")
        scanned = sem("scanned")
        gt_out = sem("gt_out")
        gt_gelu = sem("gt_gelu")
        both = sem("both")
        ly_raw = sem("ly_raw")
        hrow_up = sem("hrow_up")
        g_row_landed = sem("g_row_landed")
        fin_sum = sem("fin_sum")
        fin_m = sem("fin_m")
        fin_ms = sem("fin_ms")
        fin_est = sem("fin_est")
        fin_out = sem("fin_out")
        stored = sem("stored")
        dve_step = sem("dve_step")
        pool_step = sem("pool_step")

        def landed(c):
            gates = sum(g <= c and g % 2 == c % 2 for g in (GW0, GW1))
            return 32 * (c // 2 + 1) + 32 * gates

        def flat(w, c, q):
            return w[c % 2][:, 2 * q:2 * q + 2, :].rearrange("p a b -> p (a b)")

        def part(w, gw, c, q):
            return gw[c - GW0][:, 2 * CW * q:2 * CW * (q + 1)] if c in (GW0, GW1) else flat(w, c, q)

        block = ctx.enter_context(nc.Block())

        @block.sync
        def _(sp):
            sp.dma_start(ident_sb[:], ident).then_inc(x_landed, 16)
            sp.dma_start(x_in[0:META, 0, :], meta).then_inc(x_landed, 16)
            sp.dma_start(x_in[META:P, 0, :], x[0, 0:P - META, :]).then_inc(x_landed, 16)
            sp.dma_start(x_in[:, 1, :], x[0, P - META:2 * P - META, :]).then_inc(x_landed, 16)
            sp.dma_start(x_in[0:META, 2, :], x[0, 2 * P - META:SEQ, :]).then_inc(x_landed, 16)
            sp.dma_start(*gain_load).then_inc(gain_landed, 16)

            def load(c, pieces, i=0, halves=(0, 1)):
                s = c % 2
                for half in halves:
                    if c >= 2:
                        sp.wait_ge(wlo_made, SUB * (c - 2) + 2 * half + 2 + 2 * SUB * i)
                    views = pieces(half)
                    for dst, src in views:
                        sp.dma_start(dst, src).then_inc(w_landed[s][half], max(16, 32 // len(views)))

            def rows(w, k0, half):
                k = k0 + half * KC // 2
                return w.rearrange("(k p) n -> p k n", p=P)[:, k:k + KC // 2, :]

            def half_slot(c, half):
                return stage[c % 2][:, half * KC // 2:(half + 1) * KC // 2, :]

            def load_plain(c, w, k0, n0):
                load(c, lambda half: [(half_slot(c, half), rows(w, k0, half)[:, :, n0:n0 + CW])])

            def load_pair(c, w, n0, n1, i=0, halves=(0, 1)):
                def columns(half, n):
                    return rows(w, 0, half)[:, :, n:n + CW // 2] if isinstance(i, int) and i == 0 else \
                        rows(w, 0, half)[:, :, bass.ds(i * CW + n, CW // 2)]
                load(c, lambda half: [(half_slot(c, half)[:, :, 0:CW // 2], columns(half, n0)),
                                      (half_slot(c, half)[:, :, CW // 2:CW], columns(half, n1))], i, halves)

            def load_gates(c, block0):
                def pieces(half):
                    n = block0 + half
                    to = half_slot(c, half).rearrange("p a b -> p (a b)").rearrange(
                        "p (d g k e) -> p d g k e", d=2, g=2, k=2)
                    return [(to[:, d, g, :, :], w[0, d, n].rearrange("(k p) e -> p k e", p=P))
                            for g, w in enumerate((lru_w_a, lru_w_i)) for d in range(2)]
                load(c, pieces)

            wi, wo = ret_w_in[0], ret_w_out[0]
            for k0, signal in ((0, first_landed), (2, w_landed[0][0])):
                for side in range(2):
                    sp.dma_start(stage[0][:, k0:k0 + 2, side * 2 * P:(side + 1) * 2 * P],
                                 rows(wi, k0, 0)[:, 0:2, side * D:side * D + 2 * P]).then_inc(signal, 16)
            for h in range(HEADS):
                load_pair(RET_IN[h], wi, h * 2 * P, D + h * 2 * P, halves=(0, 1) if h else (1,))
                if h == 0:
                    sp.dma_start(ones_sb[:], ones).then_inc(const_landed, 16)
                    sp.dma_start(rope_sb[:], rope).then_inc(table_landed, 16)
                load_plain(RET_IN[h] + 1, wi, 0, 2 * D + h * HEAD_V)
                if h == 0:
                    for dst, src in param_loads:
                        sp.dma_start(dst, src).then_inc(par_landed, 16)
                    sp.dma_start(decay_sb, decay).then_inc(table_landed, 16)
                load_plain(RET_IN[h] + 2, wi, 0, 4 * D + h * HEAD_V)
            for n, (half, kg) in enumerate(RET_OUT_ORDER):
                load_plain(RET_OUT + n, wo, kg * KC, half * CW)

            def load_ffn(layer, first_in):
                with sp.Fori(0, FFN_CHUNKS // 2) as i:
                    for b in range(2):
                        load_pair(first_in + b, ffn_w_in[layer], b * 2 * P, FFN + b * 2 * P, i)
                for n in range(2 * FFN_OUT_K):
                    if (layer, n) == (0, FFN_OUT_K):
                        load_gates(GW0, 0)
                        load_gates(GW1, 2)
                    load_plain(ffn_out(layer, n), ffn_w_out[layer], (n % FFN_OUT_K) * KC,
                               n // FFN_OUT_K * CW)

            load_ffn(0, FFN0_IN)
            for c, n0 in ((XR0, D), (XR1, D + CW), (GT0, 0), (GT1, CW)):
                load_plain(c, lru_w_in[0], 0, n0)
            for n in range(2):
                def pieces(half):
                    k = 4 * n + 2 * half
                    rows_k = lru_w_out[0].rearrange("(k p) n -> p k n", p=P)[:, k:k + 2, :]
                    to = half_slot(LRU_OUT + n, half)
                    return [(to[:, 2 * m:2 * m + 2, :], rows_k[:, :, m * CW:(m + 1) * CW]) for m in range(2)]
                load(LRU_OUT + n, pieces)
            load_ffn(1, FFN1_IN)
            sp.wait_ge(h_new, 3 * DT)
            sp.dma_start(g_row, gains[1, 3, :].partition_broadcast(P)).then_inc(g_row_landed, 16)
            for b in range(4):
                sp.wait_ge(fin_out, b + 1)
                tt, half = b // 2, b % 2
                sp.dma_start(out[0, tt * P:(tt + 1) * P, half * BANK:(half + 1) * BANK],
                             fin[:, tt, half * BANK:(half + 1) * BANK]).then_inc(stored, 16)
            sp.wait_ge(stored, 64)

        @block.scalar
        def _(act):
            def prep(c, q, i=0):
                if (c, q) == (0, 0):
                    act.wait_ge(first_landed, 32)
                else:
                    act.wait_ge(w_landed[c % 2][q // 2], landed(c) + 32 * i)
                if c in (GW0, GW1):
                    act.wait_ge(fylo_made, FFN_CHUNKS)
                elif c >= 2:
                    act.wait_ge(w_used, freed(c, q) + 2 * SUB * i)
                act.activation(part(w_hi, gw_hi, c, q), flat(stage, c, q), ACTF.Copy,
                               scale=W_SCALE).then_inc(whi_made, 1)

            def estimate(bank, t0, up, n_up, n):
                act.wait_ge(up, n_up)
                if n > 1:
                    act.wait_ge(rs_made, n - 1)
                act.activation(rs0[:, t0:T], ps[:, bank, t0:T], ACTF.Abs_reciprocal_sqrt,
                               bias=eps_sb[:, 0:1]).then_inc(rs_est, 1)

            def load_estimate_table():
                act.activation(est_warm[:], eps_sb[:], ACTF.Abs_reciprocal_sqrt)

            def norm_input(i, t0, preps={}):
                for dt in range(DT):
                    if i == 0:
                        act.wait_ge(h_in, dt + 1)
                    else:
                        act.wait_ge(h_new, (i - 1) * DT + dt + 1)
                    act.activation(a_hi[:, dt, t0:T], hT[:, dt, t0:T], ACTF.Copy,
                                   scale=gain(2 * i, dt)).then_inc(ahi_made, 1)
                    if i:
                        act.activation(sq[:, dt, t0:T], hT[:, dt, t0:T], ACTF.Square).then_inc(h_sq, 1)
                    if dt in preps:
                        prep(0, preps[dt])

            def estimate_input(i, t0):
                estimate(STAT_IN, t0, ms_up, MEAN[("pre", i)], ESTIMATE[("pre", i)])

            def out_squares(c, i, half, t0, q=SUB - 1):
                for n in range(4):
                    if half == 1 and c == LRU_OUT + 1 and n < 3:
                        act.wait_ge(bank_up, n + 1)
                    elif n == 0 or half == 1:
                        act.wait_ge(w_used, used(c, n if c in STAGGERED else q))
                    act.activation(sq[:, half * 4 + n, t0:T], ps[:, (X, Y)[half] + n, t0:T], ACTF.Square,
                                   scale=UNSCALE).then_inc(m_sq, 1)

            act.wait_ge(eps_set, 1)
            load_estimate_table()
            act.wait_ge(gain_ready, 1)
            norm_input(0, 0, {1: 0, 4: 1})
            for c, q in ((0, 2), (0, 3), (1, 0), (1, 1)):
                prep(c, q)
            estimate_input(0, 0)
            prep(1, 2)
            prep(1, 3)

            def head_y(h):
                act.wait_ge(y_raw, h + 1)
                act.activation(y_hi[:, 4 * h:4 * h + 4, :], oT, ACTF.Copy).then_inc(yhi_made, 1)

            for h in range(HEADS):
                c = RET_IN[h]
                prep(c + 2, 0)
                prep(c + 2, 1)
                act.wait_ge(rot_done, h + 1)
                if h:
                    act.wait_ge(s_up, h)
                act.activation(qk_hi, rotq, ACTF.Copy).then_inc(qkhi_made, 1)
                prep(c + 2, 2)
                prep(c + 2, 3)
                if h:
                    estimate(GN, 0, gn_up, h, ESTIMATE[("head", h - 1)])
                prep(c + 3, 0)
                act.wait_ge(s_dec, h + 1)
                if h:
                    act.wait_ge(o_up, h)
                act.activation(s_hi[:, 0:2, :], sT[:, 0:2, :], ACTF.Copy)
                if h == 0:
                    act.wait_ge(zeroed, 2)
                act.activation(s_hi[R_LO:R_LO + META, 2, :], sT[0:META, 2, :], ACTF.Copy)
                act.activation(s_hi[0:META, 2, :], sT[0:META, 2, :], ACTF.Copy).then_inc(shi_made, 1)
                act.wait_ge(vt_up, h + 1)
                if h:
                    act.wait_ge(vlo_made, h)
                for n, (_, m) in enumerate(TOK_TILES):
                    act.activation(vs[0:m, n, :], ps[0:m, Y + n, :], ACTF.Copy, scale=-0.5 * UNSCALE * A_SCALE,
                                   accum_out=vsum[0:m, n, 0:1]).then_inc(vs_out, 1)
                for n, (_, m) in enumerate(TOK_TILES):
                    act.wait_ge(vmean, NTT * h + n + 1)
                    if n == 2:
                        act.activation(v_hi[R_HI:R_HI + m, n, :], vs[0:m, n, :], ACTF.Identity,
                                       bias=vsum[0:m, n, 1:2])
                    act.activation(v_hi[0:m, n, :], vs[0:m, n, :], ACTF.Identity,
                                   bias=vsum[0:m, n, 1:2]).then_inc(vhi_made, 1)
                if h:
                    head_y(h - 1)
                for q in range(1, SUB):
                    prep(c + 3, q)
                act.wait_ge(g_out, h + 1)
                act.activation(gT, gT, ACTF.Silu, scale=-0.5 * UNSCALE).then_inc(g_silu, 1)
                for q in range(SUB - 1):
                    prep(c + 4, q)
                act.wait_ge(o_up, h + 1)
                if h:
                    act.wait_ge(yhi_made, h)
                    act.wait_ge(ylo_made, h)
                for n in range(4):
                    act.activation(oT[:, n, :], ps[:, Y + n, 0:T], ACTF.Copy, scale=1.0 / A_SCALE ** 2)
                for n in range(4):
                    last = act.activation(osq[:, n, :], ps[:, Y + n, 0:T], ACTF.Square,
                                          scale=1.0 / A_SCALE ** 2)
                last.then_inc(o_sq, 1)
                prep(c + 4, 3)
                if h == 0:
                    act.wait_ge(par_raw, 1)
                    act.activation(lam[:, 0, :], par[:, LL:LL + 16], ACTF.Abs).then_inc(lam_abs, 1)
                    act.wait_ge(lam_abs, 1)
                    act.activation(lam[:, 1, :], lam[:, 0, :], ACTF.Exp, scale=-1.0).then_inc(lam_exp, 1)

            c = RET_OUT
            estimate(Y, 0, gn_up, HEADS, ESTIMATE[("head", HEADS - 1)])
            head_y(HEADS - 1)
            for q in range(SUB):
                prep(c + 2, q)
            out_squares(c + 1, 0, 0, 0)
            for n in (3, 4):
                for q in range(SUB):
                    prep(c + n, q)
            load_estimate_table()
            out_squares(c + 3, 0, 1, 0)
            estimate(STAT, 0, ms_up, MEAN[("post", 0)], ESTIMATE[("post", 0)])
            norm_input(1, 0)
            for q in range(SUB):
                prep(c + 5, q)
                if q == 1:
                    estimate_input(1, 0)

            def ffn_chunk(layer, first_in, i, b):
                t0 = ffn_first(layer)
                c = first_in + b
                n0 = layer * FFN_CHUNKS + b + 2 * i
                behind = layer > 0 or not (isinstance(i, int) and i == 0)
                act.wait_ge(u_out, n0 + 1)
                act.wait_ge(cnow_set, n0 + 1)
                if behind:
                    act.wait_ge(fy_raw, n0 - 1)
                for n in range(4):
                    last = act.activation(u_cv[b][:, n, t0:T], u_in[b][:, n, t0:T], ACTF.Identity,
                                          scale=cnow[b][:, cpar_col(1, n):cpar_col(1, n) + 1],
                                          bias=cnow[b][:, cpar_col(3, n):cpar_col(3, n) + 1])
                last.then_inc(mid_tap, 1)
                prep(c + 2, 2, i)
                prep(c + 2, 3, i)
                act.wait_ge(conv_done, n0 + 1)
                if behind:
                    act.wait_ge(fylo_made, n0 - 1)
                act.activation(u_y[b][:, :, t0:T], u_cv[b][:, 2:4, t0:T],
                               ACTF.Gelu_apprx_tanh).then_inc(gelu_done, 1)
                prep(c + 3, 0, i)
                act.wait_ge(fy_raw, n0 + 1)
                dst = y_hi[:, bass.ds(4 * i + 2 * b, 2), t0:T] if not isinstance(i, int) else \
                    y_hi[:, 4 * i + 2 * b:4 * i + 2 * b + 2, t0:T]
                act.activation(dst, u_y[b][:, :, t0:T], ACTF.Copy).then_inc(yhi_made, 1)
                prep(c + 3, 1, i)

            def ffn_in(layer, first_in):
                prep(first_in + 2, 0)
                prep(first_in + 2, 1)
                for b in range(2):
                    ffn_chunk(layer, first_in, 0, b)
                with act.Fori(1, FFN_CHUNKS // 2) as i:
                    for b in range(2):
                        ffn_chunk(layer, first_in, i, b)

            ffn_in(0, FFN0_IN)
            for c in range(FFN0_OUT + 2, XR0 + 1):
                if c == ffn_out(0, 2 * FFN_OUT_K - 1):
                    out_squares(ffn_out(0, FFN_OUT_K - 1), 1, 0, 0)
                for q in range(SUB):
                    if (c, q) not in ((FFN0_OUT + 2, 0), (FFN0_OUT + 2, 1)):
                        prep(c, q)
            load_estimate_table()
            out_squares(ffn_out(0, 2 * FFN_OUT_K - 1), 1, 1, 0)
            estimate(STAT, 0, ms_up, MEAN[("post", 1)], ESTIMATE[("post", 1)])
            norm_input(2, 0)
            for q in range(SUB):
                prep(XR1, q)
                if q == 1:
                    estimate_input(2, 0)

            def gates(n):
                blk, d, s = n // 2, n % 2, GATE_SET[n]
                act.wait_ge(gates_up, n + 1)
                for to, base, first in ((lr, LBA, s), (li, LBI, s + 2)):
                    for m in range(2):
                        last = act.activation(to[blk][:, d, m, :], ps[:, first + m, 0:T], ACTF.Sigmoid,
                                              scale=UNSCALE, bias=lpar(base, d * DT + 2 * blk + m))
                last.then_inc(r_out, 1)

            def block_rates(blk):
                act.wait_ge(r_out, 2 * blk + 2)
                if blk == 3:
                    act.wait_ge(ix_made, 2)
                pairs = [(d, m, d * DT + 2 * blk + m) for d in range(2) for m in range(2)]
                for d, m, j in pairs:
                    last = act.activation(la[blk][:, d, m, :], lr[blk][:, d, m, :], ACTF.Exp,
                                          scale=spc[:, 1, j:j + 1])
                last.then_inc(exps, 1)
                act.wait_ge(exps, blk + 1)
                for d, m, j in pairs:
                    last = act.activation(lr[blk][:, d, m, :], lr[blk][:, d, m, :], ACTF.Tanh,
                                          scale=spc[:, 0, j:j + 1])
                last.then_inc(rates, 1)

            def block_root(blk):
                act.wait_ge(rates, blk + 1)
                act.activation(lq[blk], lr[blk], ACTF.Sqrt).then_inc(root, 1)

            def gate_gelu(k):
                act.wait_ge(gt_out, k + 1)
                act.activation(ggel[k][:, :, T0_LRU_OUT:T], ggel[k][:, :, T0_LRU_OUT:T], ACTF.Gelu_apprx_tanh,
                               scale=-0.5 * UNSCALE).then_inc(gt_gelu, 1)

            def lru_y(blk):
                act.wait_ge(ly_raw, blk + 1)
                act.activation(y_hi[:, 2 * blk:2 * blk + 2, T0_LRU_OUT:T],
                               xc[:, 2 * blk:2 * blk + 2, T0_LRU_OUT:T], ACTF.Copy).then_inc(yhi_made, 1)

            def x_high(k):
                act.wait_ge(x_conv, k + 1)
                act.activation(xc_hi[k], xc[:, 4 * k:4 * k + 4, :], ACTF.Copy).then_inc(xhi_made, 1)

            for q in range(2):
                prep(GT0, q)
            x_high(0)
            for q in (2, 3):
                prep(GT0, q)
            prep(GT1, 0)
            prep(GT1, 1)
            gates(0)
            gates(1)
            gates(2)
            x_high(1)
            gates(3)
            for rates_or_root in (block_rates, block_root):
                for blk in (0, 1):
                    rates_or_root(blk)
            gate_gelu(0)
            act.wait_ge(wlo_made, SUB * (GT1 + 1))
            for q in range(SUB):
                gates(4 + q)
                if q < 2:
                    prep(LRU_OUT, q)
            lru_y(0)
            lru_y(1)
            for rates_or_root in (block_rates, block_root):
                for blk in (2, 3):
                    rates_or_root(blk)
            act.wait_ge(wlo_made, SUB * (LRU_OUT + 1) + 1)
            prep(LRU_OUT + 1, 1)
            gate_gelu(1)
            prep(LRU_OUT + 1, 2)
            lru_y(2)
            prep(LRU_OUT + 1, 3)
            lru_y(3)

            prep(LRU_OUT + 2, 0)
            prep(LRU_OUT + 2, 1)
            load_estimate_table()
            out_squares(LRU_OUT + 1, 2, 0, T0_LRU_OUT, 2)
            out_squares(LRU_OUT + 1, 2, 1, T0_LRU_OUT)
            prep(LRU_OUT + 2, 2)
            prep(LRU_OUT + 2, 3)
            estimate(STAT, T0_LRU_OUT, ms_up, MEAN[("post", 2)], ESTIMATE[("post", 2)])
            norm_input(3, T0_LRU_OUT)
            for q in range(SUB):
                prep(LRU_OUT + 3, q)
                if q == 1:
                    estimate_input(3, T0_LRU_OUT)

            ffn_in(1, FFN1_IN)
            for n in range(2 * FFN_OUT_K):
                c = FFN1_OUT + n
                if c + 2 < CHUNKS:
                    for q in range(SUB):
                        if (n, q) not in ((0, 0), (0, 1)):
                            prep(c + 2, q)
                if n == 2 * FFN_OUT_K - 2:
                    load_estimate_table()
                if n in (FFN_OUT_K, 2 * FFN_OUT_K - 1):
                    half = n // FFN_OUT_K - (n == FFN_OUT_K)
                    for tt in range(2):
                        last_c = FFN1_OUT + (half + 1) * FFN_OUT_K - 1
                        act.wait_ge(w_used, used(last_c, 0 if (half, tt) == (1, 0) else SUB - 1))
                        b = 2 * half + tt
                        if b:
                            act.wait_ge(fin_sum, b)
                        act.activation(fin_sq, ps[:, (X, Y)[half] + tt, :], ACTF.Square, scale=UNSCALE,
                                       accum_out=fin_s[:, half, tt:tt + 1]).then_inc(fin_sum, 1)
                        if half:
                            act.wait_ge(fin_ms, tt + 1)
                            act.activation(fin_s[:, 3, tt:tt + 1], fin_s[:, 2, tt:tt + 1],
                                           ACTF.Abs_reciprocal_sqrt, scale=1.0 / D,
                                           bias=eps_sb[:, 0:1]).then_inc(fin_est, 1)

        @block.vector
        def _(dve):
            step = [0]

            def mark(ins):
                step[0] += 1
                ins.then_inc(dve_step, 1)
                return step[0]

            def after(n):
                dve.wait_ge(dve_step, n)

            def link(ins):
                after(mark(ins))

            def prep(c, q, i=0):
                dve.wait_ge(whi_made, SUB * c + q + 1 + 2 * SUB * i)
                if c in (GW0, GW1):
                    dve.wait_ge(fylo_made, FFN_CHUNKS)
                elif c >= 2:
                    dve.wait_ge(w_used, freed(c, q) + 2 * SUB * i)
                dve.scalar_tensor_tensor(out=part(w_lo, gw_lo, c, q), in0=flat(stage, c, q),
                                         scalar=W_SCALE, in1=part(w_hi, gw_hi, c, q), op0=ALU.mult,
                                         op1=ALU.subtract).then_inc(wlo_made, 1)

            def prep_both(c, q):
                dve.wait_ge(w_landed[c % 2][q // 2], landed(c))
                dve.wait_ge(w_used, freed(c, q))
                dve.tensor_scalar(flat(w_hi, c, q), flat(stage, c, q), W_SCALE, None,
                                  ALU.mult).then_inc(whi_made, 1)
                prep(c, q)

            def rsqrt(to, bank, t0, n):
                dve.wait_ge(rs_est, n)
                link(dve.tensor_tensor(rs1[:, t0:T], rs0[:, t0:T], rs0[:, t0:T], ALU.mult))
                link(dve.scalar_tensor_tensor(out=rs1[:, t0:T], in0=ps[:, bank, t0:T], scalar=EPS,
                                              in1=rs1[:, t0:T], op0=ALU.add, op1=ALU.mult))
                dve.scalar_tensor_tensor(out=to[:, t0:T], in0=rs1[:, t0:T], scalar=3.0, in1=rs0[:, t0:T],
                                         op0=ALU.subtract, op1=ALU.mult).then_inc(rs_made, 1)
                dve.wait_ge(rs_made, n)

            def rsqrt_input(i, t0):
                rsqrt(rs_in, STAT_IN, t0, ESTIMATE[("pre", i)])

            def norm_low(i, dt, t0):
                dve.wait_ge(ahi_made, i * DT + dt + 1)
                dve.scalar_tensor_tensor(out=a_lo[:, dt, t0:T], in0=hT[:, dt, t0:T], scalar=gain(2 * i, dt),
                                         in1=a_hi[:, dt, t0:T], op0=ALU.mult,
                                         op1=ALU.subtract).then_inc(alo_made, 1)

            def out_scale(i, half, t0):
                for n in range(4):
                    dt = half * 4 + n
                    dve.wait_ge(m_sq, i * DT + dt + 1)
                    last = dve.tensor_scalar(mT[:, dt, t0:T], ps[:, (X, Y)[half] + n, t0:T],
                                             gain(2 * i + 1, dt), None, ALU.mult)
                last.then_inc(m_scaled, 1)

            def residual(i, t0):
                rsqrt(rs, STAT, t0, ESTIMATE[("post", i)])
                dve.wait_ge(m_scaled, 2 * (i + 1))
                marks = []
                for dt in range(DT + 2):
                    if dt < DT:
                        marks.append(mark(dve.tensor_tensor(mT[:, dt, t0:T], mT[:, dt, t0:T], rs[:, t0:T],
                                                            ALU.mult)))
                    if 1 <= dt <= DT:
                        after(marks[dt - 1])
                        dve.tensor_tensor(hT[:, dt - 1, t0:T], hT[:, dt - 1, t0:T], mT[:, dt - 1, t0:T],
                                          ALU.add).then_inc(h_new, 1)
                    if dt >= 2:
                        norm_low(i + 1, dt - 2, t0)

            dve.memset(eps_sb[:], EPS).then_inc(eps_set, 1)
            dve.wait_ge(gain_up, 1)
            link(dve.tensor_copy(gains_sb[:], ps[:, GAINS, 0:8 * DT]))
            norms = gains_sb.rearrange("p (i w d) -> p i w d", w=2, d=DT)
            dve.tensor_scalar(norms[:, :, 0, :], norms[:, :, 0, :], A_SCALE, None, ALU.mult)
            dve.tensor_scalar(norms[:, :, 1, :], norms[:, :, 1, :], -UNSCALE / 2, None,
                              ALU.mult).then_inc(gain_ready, 1)
            for dt in range(DT):
                dve.wait_ge(xT_up, dt + 1)
                dve.tensor_copy(hT[:, dt, :], ps[:, dt, 0:T]).then_inc(h_in, 1)
                if dt:
                    norm_low(0, dt - 1, 0)
                if dt in (3, 5):
                    prep(0, (dt - 3) // 2)
            norm_low(0, DT - 1, 0)
            for c, q in ((0, 2), (0, 3), (1, 0), (1, 1)):
                prep(c, q)
            rsqrt_input(0, 0)
            prep(1, 2)
            prep(1, 3)
            dve.wait_ge(table_landed, 32)
            link(dve.tensor_tensor(rope_sb[:], rope_sb[:], rs_in[:].unsqueeze(1).to_broadcast([P, 2, T]),
                                   ALU.mult))

            def times_rs(dst, first, t0=0):
                return dve.tensor_tensor(dst[:, :, t0:T], ps[:, first:first + 4, t0:T],
                                         rs_in[:, t0:T].unsqueeze(1).to_broadcast([P, 4, T - t0]), ALU.mult)

            def head_y(h):
                dve.wait_ge(g_silu, h + 1)
                link(dve.scalar_tensor_tensor(out=oT, in0=oT, scalar=-A_SCALE / 2, in1=gT, op0=ALU.mult,
                                              op1=ALU.mult))
                dve.tensor_tensor(oT, oT, rs[:, 0:T].unsqueeze(1).to_broadcast([P, 4, T]),
                                  ALU.mult).then_inc(y_raw, 1)

            def head_low(h):
                dve.wait_ge(yhi_made, h + 1)
                dve.tensor_tensor(y_lo[:, 4 * h:4 * h + 4, :], oT, y_hi[:, 4 * h:4 * h + 4, :],
                                  ALU.subtract).then_inc(ylo_made, 1)

            def parameters():
                dve.wait_ge(par_up, 1)
                link(dve.tensor_copy(par[:], ps[:, PARAMS, 0:PAR_ROWS[1]]))
                for layer in range(2):
                    for tap in range(4):
                        col = PAR_COL[2 + 2 * layer + tap // 2] + tap % 2 * 2 * FT
                        for g in range(2):
                            scale = A_SCALE if g == 0 else 1.0
                            if tap < 3:
                                scale *= -UNSCALE / 2
                            last = dve.tensor_scalar(
                                cpar[:, layer, :, cpar_col(tap, 2 * g):cpar_col(tap, 2 * g) + 2],
                                ps[:, PARAMS, col + g * FT:col + (g + 1) * FT].rearrange("p (j n) -> p j n", n=2),
                                scale, None, ALU.mult)
                last.then_inc(par_raw, 1)
                link(dve.tensor_scalar(par[:, LC:LC + 32], par[:, LC:LC + 32], -0.5 * UNSCALE * A_SCALE, None,
                                       ALU.mult))
                dve.tensor_scalar(par[:, LB:LB + 8], par[:, LB:LB + 8], A_SCALE, None,
                                  ALU.mult).then_inc(par_ready, 1)

            def lru_rates():
                dve.wait_ge(lam_exp, 1)
                t_, z, z2, p_ = lam[:, 1, :], lam[:, 2, :], lam[:, 3, :], lam[:, 4, :]
                link(dve.tensor_scalar(z, t_, 2.0, None, ALU.add))
                link(dve.reciprocal(z2, z))
                link(dve.tensor_tensor(z, t_, z2, ALU.mult))
                link(dve.tensor_tensor(z2, z, z, ALU.mult))
                link(dve.tensor_scalar(p_, z2, 1.0 / 19, None, ALU.mult))
                for n in range(17, 1, -2):
                    link(dve.scalar_tensor_tensor(out=p_, in0=p_, scalar=1.0 / n, in1=z2, op0=ALU.add,
                                                  op1=ALU.mult))
                link(dve.scalar_tensor_tensor(out=p_, in0=p_, scalar=1.0, in1=z, op0=ALU.add, op1=ALU.mult))
                link(dve.tensor_scalar(z, par[:, LL:LL + 16], -1.0, 0.0, ALU.mult, ALU.max))
                link(dve.scalar_tensor_tensor(out=z2, in0=p_, scalar=2.0, in1=z, op0=ALU.mult, op1=ALU.add))
                dve.tensor_scalar(spc[:, 0, :], z2, 4.0, None, ALU.mult)
                dve.tensor_scalar(spc[:, 1, :], z2, -8.0, None, ALU.mult).then_inc(par_ready, 1)

            cos = rope_sb[:, 0:1, :].to_broadcast([P, 2, T])
            sin = rope_sb[:, 1:2, :].to_broadcast([P, 2, T])
            for h in range(HEADS):
                c = RET_IN[h]
                qk = ps[:, X:X + 4, 0:T].rearrange("p (g x) t -> p x g t", x=2)
                rot = rotq.rearrange("p (g x) t -> p x g t", x=2)
                dve.wait_ge(w_used, used(c))
                prods = [mark(dve.tensor_tensor(to, qk[:, x], by, ALU.mult)) for to, x, by in (
                    (rot[:, 0], 0, cos), (rotp[:, 0], 1, sin), (rot[:, 1], 1, cos), (rotp[:, 1], 0, sin))]
                after(prods[1])
                dve.tensor_tensor(rot[:, 0], rot[:, 0], rotp[:, 0], ALU.subtract)
                after(prods[3])
                dve.tensor_tensor(rot[:, 1], rot[:, 1], rotp[:, 1], ALU.add).then_inc(rot_done, 1)
                prep(c + 2, 0)
                dve.wait_ge(qkhi_made, h + 1)
                dve.tensor_tensor(qk_lo, rotq, qk_hi, ALU.subtract).then_inc(qklo_made, 1)
                prep(c + 2, 1)
                prep(c + 2, 2)
                dve.wait_ge(w_used, used(c + 1))
                times_rs(vT, Y).then_inc(v_out, 1)
                prep(c + 2, 3)
                dve.wait_ge(s_up, h + 1)
                for n, (m0, m) in enumerate(TOK_TILES):
                    last = dve.tensor_tensor(sT[0:m, n, :], ps[0:m, X + n, 0:T],
                                             decay_sb[0:m, h, 2 * P - m0:2 * P - m0 + T], ALU.mult)
                last.then_inc(s_dec, 1)
                if h:
                    rsqrt(rs, GN, 0, ESTIMATE[("head", h - 1)])
                dve.wait_ge(shi_made, h + 1)
                dve.tensor_tensor(s_lo[:, 0:2, :], sT[:, 0:2, :], s_hi[:, 0:2, :], ALU.subtract)
                dve.tensor_tensor(s_hi[R_HI:R_HI + META, 2, :], sT[0:META, 2, :], s_hi[0:META, 2, :],
                                  ALU.subtract).then_inc(slo_made, 1)
                for n, (_, m) in enumerate(TOK_TILES):
                    dve.wait_ge(vs_out, NTT * h + n + 1)
                    dve.tensor_scalar(vsum[0:m, n, 1:2], vsum[0:m, n, 0:1], -1.0 / HEAD_V, None,
                                      ALU.mult).then_inc(vmean, 1)
                for n, (_, m) in enumerate(TOK_TILES):
                    dve.wait_ge(vhi_made, NTT * h + n + 1)
                    to = v_lo[0:m, n, :] if n < 2 else v_hi[R_LO:R_LO + m, n, :]
                    last = dve.scalar_tensor_tensor(out=to, in0=vs[0:m, n, :],
                                                    scalar=vsum[0:m, n, 1:2], in1=v_hi[0:m, n, :],
                                                    op0=ALU.add, op1=ALU.subtract)
                last.then_inc(vlo_made, 1)
                prep(c + 3, 0)
                if h:
                    head_y(h - 1)
                    head_low(h - 1)
                else:
                    parameters()
                prep(c + 3, 1)
                dve.wait_ge(w_used, used(c + 2))
                times_rs(gT, X).then_inc(g_out, 1)
                prep(c + 3, 2)
                prep(c + 3, 3)
                for q in range(SUB):
                    prep(c + 4, q)
                if h == 0:
                    lru_rates()

            c = RET_OUT
            rsqrt(rs, Y, 0, ESTIMATE[("head", HEADS - 1)])
            head_y(HEADS - 1)
            head_low(HEADS - 1)
            for q in range(SUB):
                prep(c + 2, q)
            out_scale(0, 0, 0)
            for n in (3, 4):
                for q in range(SUB):
                    prep(c + n, q)
            out_scale(0, 1, 0)
            residual(0, 0)
            for q in range(SUB):
                prep(c + 5, q)
                if q == 1:
                    rsqrt_input(1, 0)

            def ffn_chunk(layer, first_in, i, b):
                t0 = ffn_first(layer)
                c, s = first_in + b, (X, Y)[b]
                n0 = layer * FFN_CHUNKS + b + 2 * i
                dve.wait_ge(w_used, used(c) + 2 * SUB * i)
                times_rs(u_in[b], s, t0).then_inc(u_out, 1)
                prep(c + 2, 0, i)
                prep(c + 2, 1, i)
                dve.wait_ge(mid_tap, n0 + 1)
                order = (2, 3, 0, 1)
                for n in order:
                    dve.scalar_tensor_tensor(
                        out=u_cv[b][:, n, t0 + 1:T], in0=u_in[b][:, n, t0:T - 1],
                        scalar=cnow[b][:, cpar_col(0, n):cpar_col(0, n) + 1],
                        in1=u_cv[b][:, n, t0 + 1:T], op0=ALU.mult, op1=ALU.add).then_inc(left_tap, 1)
                for m, n in enumerate(order):
                    dve.wait_ge(left_tap, 4 * n0 + m + 1)
                    last = dve.scalar_tensor_tensor(
                        out=u_cv[b][:, n, t0:T - 1], in0=u_in[b][:, n, t0 + 1:T],
                        scalar=cnow[b][:, cpar_col(2, n):cpar_col(2, n) + 1],
                        in1=u_cv[b][:, n, t0:T - 1], op0=ALU.mult, op1=ALU.add)
                last.then_inc(conv_done, 1)
                prep(c + 2, 2, i)
                prep(c + 2, 3, i)

            def ffn_in(layer, first_in):
                for b in range(2):
                    ffn_chunk(layer, first_in, 0, b)
                with dve.Fori(1, FFN_CHUNKS // 2) as i:
                    for b in range(2):
                        ffn_chunk(layer, first_in, i, b)

            ffn_in(0, FFN0_IN)
            for c in range(FFN0_OUT + 2, XR0 + 1):
                if c == ffn_out(0, 2 * FFN_OUT_K - 1):
                    out_scale(1, 0, 0)
                for q in range(SUB):
                    prep(c, q)
            out_scale(1, 1, 0)
            residual(1, 0)
            prep(XR1, 0)
            prep(XR1, 1)
            rsqrt_input(2, 0)

            for k, c in ((0, XR0), (1, XR1)):
                dve.wait_ge(w_used, used(c))
                times_rs(x_raw[k], (X, Y)[k]).then_inc(x_out, 1)
                if k == 0:
                    prep(XR1, 2)
                    prep(XR1, 3)
                else:
                    prep(GT0, 0)
                    prep(GT0, 1)
                dve.wait_ge(x_mid, k + 1)
                taps = [t for t in range(LRU_TAPS) if t != LRU_LEFT]
                done = {}
                for t in taps:
                    sh = t - LRU_LEFT
                    a, b = max(0, -sh), T - max(0, sh)
                    for n in range(4):
                        j = 4 * k + n
                        if n in done:
                            after(done[n])
                        last = dve.scalar_tensor_tensor(
                            out=xc[:, j, a:b], in0=x_raw[k][:, n, a + sh:b + sh], scalar=lpar(LC, t * DT + j),
                            in1=xc[:, j, a:b], op0=ALU.mult, op1=ALU.add)
                        if t != taps[-1]:
                            done[n] = mark(last)
                last.then_inc(x_conv, 1)
                dve.wait_ge(xhi_made, k + 1)
                dve.tensor_tensor(xc_lo[k], xc[:, 4 * k:4 * k + 4, :], xc_hi[k],
                                  ALU.subtract).then_inc(xlo_made, 1)
            for c, q in ((GT0, 2), (GT0, 3), (GT1, 0), (GT1, 1)):
                prep(c, q)
            prep_both(GT1, 2)
            prep_both(GT1, 3)

            def lru_v(blk):
                dve.wait_ge(half_up, blk + 1)
                link(dve.scalar_tensor_tensor(out=l_prod, in0=lr[blk], scalar=1.0, in1=la[blk], op0=ALU.add,
                                              op1=ALU.mult))
                link(dve.scalar_tensor_tensor(out=la[blk], in0=l_prod, scalar=2.0, in1=la[blk],
                                              op0=ALU.subtract, op1=ALU.mult))

            def lru_a(blk):
                dve.wait_ge(root, blk + 1)
                return mark(dve.tensor_scalar(lr[blk], la[blk], -2.0, -1.0, ALU.mult, ALU.add))

            def lru_scan(blk):
                lru_a(blk)
                dve.wait_ge(ix_made, blk + 1)
                link(dve.scalar_tensor_tensor(out=li[blk], in0=la[blk], scalar=-2.0, in1=li[blk],
                                              op0=ALU.mult, op1=ALU.mult))
                for d, h in ((0, hf), (1, hb)):
                    for m in range(2):
                        way = slice(None, None, 1 - 2 * d)
                        last = dve.tensor_tensor_scan(h[:, 2 * blk + m, way], lr[blk][:, d, m, way],
                                                      li[blk][:, d, m, way], 0.0, ALU.mult, ALU.add)
                last.then_inc(scanned, 1)

            def lru_y(blk):
                two = slice(2 * blk, 2 * blk + 2)
                gg = ggel[blk // 2][:, 2 * (blk % 2):2 * (blk % 2) + 2, T0_LRU_OUT:T]
                dve.wait_ge(both, blk + 1)
                dve.wait_ge(gt_gelu, blk // 2 + 1)
                dve.tensor_tensor(xc[:, two, T0_LRU_OUT:T], hf[:, two, T0_LRU_OUT:T], gg,
                                  ALU.mult).then_inc(ly_raw, 1)

            def lru_y_low(blk):
                two = slice(2 * blk, 2 * blk + 2)
                dve.wait_ge(yhi_made, Y_LRU + blk + 1)
                dve.tensor_tensor(y_lo[:, two, T0_LRU_OUT:T], xc[:, two, T0_LRU_OUT:T],
                                  y_hi[:, two, T0_LRU_OUT:T], ALU.subtract).then_inc(ylo_made, 1)

            lru_v(0)
            dve.wait_ge(w_used, used(GT0))
            times_rs(ggel[0], X, T0_LRU_OUT).then_inc(gt_out, 1)
            lru_v(1)
            lru_scan(0)
            lru_scan(1)
            prep(LRU_OUT, 0)
            lru_y(0)
            lru_y(1)
            prep(LRU_OUT, 1)
            prep_both(LRU_OUT, 2)
            prep_both(LRU_OUT, 3)
            lru_y_low(0)
            lru_y_low(1)
            prep_both(LRU_OUT + 1, 0)
            lru_v(2)
            dve.wait_ge(w_used, used(GT1))
            times_rs(ggel[1], Y, T0_LRU_OUT).then_inc(gt_out, 1)
            lru_v(3)

            def add_scans(blk):
                two = slice(2 * blk, 2 * blk + 2)
                dve.wait_ge(scanned, blk + 1)
                dve.tensor_tensor(hf[:, two, T0_LRU_OUT:T], hf[:, two, T0_LRU_OUT:T], hb[:, two, T0_LRU_OUT:T],
                                  ALU.add).then_inc(both, 1)

            lru_scan(2)
            add_scans(2)
            lru_y(2)
            prep(LRU_OUT + 1, 1)
            lru_y_low(2)
            lru_scan(3)
            add_scans(3)
            lru_y(3)
            prep(LRU_OUT + 1, 2)
            lru_y_low(3)
            prep(LRU_OUT + 1, 3)
            prep(LRU_OUT + 2, 0)
            prep(LRU_OUT + 2, 1)
            out_scale(2, 0, T0_LRU_OUT)
            out_scale(2, 1, T0_LRU_OUT)
            prep(LRU_OUT + 2, 2)
            residual(2, T0_LRU_OUT)
            prep(LRU_OUT + 2, 3)
            for q in range(SUB):
                prep(LRU_OUT + 3, q)
                if q == 1:
                    rsqrt_input(3, T0_LRU_OUT)

            ffn_in(1, FFN1_IN)

            def final(tt):
                ms, r0, t_, r = [fin_s[:, n, tt:tt + 1] for n in (2, 3, 4, 5)]
                dve.wait_ge(fin_est, tt + 1)
                link(dve.tensor_scalar(ms, ms, 1.0 / D, EPS, ALU.mult, ALU.add))
                link(dve.tensor_tensor(t_, r0, r0, ALU.mult))
                link(dve.tensor_tensor(t_, t_, ms, ALU.mult))
                link(dve.scalar_tensor_tensor(out=r, in0=t_, scalar=3.0, in1=r0, op0=ALU.subtract,
                                              op1=ALU.mult))
                dve.wait_ge(fin_m, 3 + tt)
                dve.wait_ge(hrow_up, 2)
                for half in range(2):
                    cols = slice(half * BANK, (half + 1) * BANK)
                    dve.scalar_tensor_tensor(out=fin[:, tt, cols], in0=fin[:, tt, cols], scalar=r,
                                             in1=ps[:, H_ROW[2 * tt + half], :], op0=ALU.mult,
                                             op1=ALU.add).then_inc(fin_out, 1)

            for n in range(2 * FFN_OUT_K):
                c = FFN1_OUT + n
                if c + 2 < CHUNKS:
                    for q in range(SUB):
                        prep(c + 2, q)
                if n in (FFN_OUT_K, 2 * FFN_OUT_K - 1):
                    half = n // FFN_OUT_K - (n == FFN_OUT_K)
                    if half == 0:
                        dve.wait_ge(g_row_landed, 16)
                    for tt in range(2):
                        b = 2 * half + tt
                        dve.wait_ge(fin_sum, b + 1)
                        if half:
                            dve.tensor_tensor(fin_s[:, 2, tt:tt + 1], fin_s[:, 0, tt:tt + 1],
                                              fin_s[:, 1, tt:tt + 1], ALU.add).then_inc(fin_ms, 1)
                        dve.scalar_tensor_tensor(out=fin[:, tt, half * BANK:(half + 1) * BANK],
                                                 in0=ps[:, (X, Y)[half] + tt, :], scalar=-UNSCALE / 2,
                                                 in1=g_row[:, half * BANK:(half + 1) * BANK],
                                                 op0=ALU.mult, op1=ALU.mult).then_inc(fin_m, 1)
                        if half:
                            final(tt)

        @block.gpsimd
        def _(pool):
            step = [0]

            def link(ins):
                step[0] += 1
                ins.then_inc(pool_step, 1)
                pool.wait_ge(pool_step, step[0])

            def sum_tiles(signal, n_tiles, t0, ready, n_ready):
                pool.wait_ge(ready, n_ready + 2)
                ins = pool.tensor_tensor(sq_sum[:, t0:T], sq[:, 0, t0:T], sq[:, 1, t0:T], ALU.add)
                for dt in range(2, n_tiles):
                    link(ins)
                    pool.wait_ge(ready, n_ready + dt + 1)
                    ins = pool.tensor_tensor(sq_sum[:, t0:T], sq_sum[:, t0:T], sq[:, dt, t0:T], ALU.add)
                ins.then_inc(signal, 1)

            def sum_output(i, t0):
                sum_tiles(sum_m, 4, t0, m_sq, i * DT)

            def sum_input(i, t0):
                if i:
                    pool.wait_ge(ms_up, MEAN[("post", i - 1)])
                sum_tiles(sum_h, DT, t0, h_sq, i * DT)

            def ffn_chunk(layer, i, b):
                t0 = ffn_first(layer)
                n0 = layer * FFN_CHUNKS + b + 2 * i
                dynamic = not isinstance(i, int)
                if layer or dynamic:
                    pool.wait_ge(conv_done, n0 - 1)
                one = bass.ds(2 * i + b, 1) if dynamic else slice(2 * i + b, 2 * i + b + 1)
                pool.tensor_copy(cnow[b][:].unsqueeze(1), cpar[:, layer, one, :]).then_inc(cnow_set, 1)
                pool.wait_ge(gelu_done, n0 + 1)
                pool.tensor_tensor(u_y[b][:, :, t0:T], u_y[b][:, :, t0:T], u_cv[b][:, 0:2, t0:T],
                                   ALU.mult).then_inc(fy_raw, 1)
                pool.wait_ge(yhi_made, Y_FFN[layer] + b + 2 * i + 1)
                two = bass.ds(4 * i + 2 * b, 2) if dynamic else slice(4 * i + 2 * b, 4 * i + 2 * b + 2)
                pool.tensor_tensor(y_lo[:, two, t0:T], u_y[b][:, :, t0:T], y_hi[:, two, t0:T],
                                   ALU.subtract).then_inc(fylo_made, 1)

            def ffn_in(layer):
                for b in range(2):
                    ffn_chunk(layer, 0, b)
                with pool.Fori(1, FFN_CHUNKS // 2) as i:
                    for b in range(2):
                        ffn_chunk(layer, i, b)

            pool.memset(v_hi[:, 2, :], 0.0).then_inc(zeroed, 1)
            pool.memset(s_hi[:, 2, :], 0.0).then_inc(zeroed, 1)
            for dt in range(DT + 1):
                if dt < DT:
                    pool.wait_ge(h_in, dt + 1)
                    pool.tensor_tensor(sq[:, dt, :], hT[:, dt, :], hT[:, dt, :], ALU.mult).then_inc(h_sq, 1)
                if dt >= 2:
                    pool.wait_ge(h_sq, dt)
                    last = pool.tensor_tensor(sq_sum[:], sq[:, 0, :] if dt == 2 else sq_sum[:], sq[:, dt - 1, :],
                                              ALU.add)
                    if dt < DT:
                        link(last)
            last.then_inc(sum_h, 1)
            for h in range(HEADS):
                pool.wait_ge(o_sq, h + 1)
                link(pool.tensor_tensor(osq[:, 0:2, :], osq[:, 0:2, :], osq[:, 2:4, :], ALU.add))
                pool.tensor_tensor(osq[:, 0, :], osq[:, 0, :], osq[:, 1, :], ALU.add).then_inc(sum_o, 1)
            pool.wait_ge(ms_up, MEAN[("pre", 0)])
            sum_output(0, 0)
            sum_input(1, 0)
            pool.wait_ge(par_ready, 1)
            ffn_in(0)
            sum_output(1, 0)
            sum_input(2, 0)
            for k in range(2):
                pool.wait_ge(x_out, k + 1)
                for n in range(4):
                    j = 4 * k + n
                    last = pool.tensor_scalar(xc[:, j, :], x_raw[k][:, n, :], lpar(LC, LRU_LEFT * DT + j),
                                              lpar(LB, j), ALU.mult, ALU.add)
                last.then_inc(x_mid, 1)
            def gated_x(n):
                blk, d = n // 2, n % 2
                u = li[blk][:, d]
                pool.wait_ge(r_out, n + 1)
                link(pool.tensor_tensor(u, u, xc[:, 2 * blk:2 * blk + 2, :], ALU.mult))

            def half(blk):
                pool.wait_ge(rates, blk + 1)
                pool.tensor_scalar(la[blk], la[blk], 0.5, 0.5, ALU.mult, ALU.add).then_inc(half_up, 1)

            def times_root(blk):
                pool.wait_ge(root, blk + 1)
                pool.tensor_tensor(li[blk], li[blk], lq[blk], ALU.mult).then_inc(ix_made, 1)

            def add_scans(blk):
                two = slice(2 * blk, 2 * blk + 2)
                pool.wait_ge(scanned, blk + 1)
                pool.tensor_tensor(hf[:, two, T0_LRU_OUT:T], hf[:, two, T0_LRU_OUT:T], hb[:, two, T0_LRU_OUT:T],
                                  ALU.add).then_inc(both, 1)

            for n in range(4):
                gated_x(n)
            for half_or_root in (half, times_root):
                for blk in (0, 1):
                    half_or_root(blk)
            gated_x(4)
            add_scans(0)
            gated_x(5)
            add_scans(1)
            gated_x(6)
            gated_x(7)
            half(2)
            half(3)
            times_root(2)
            times_root(3)
            sum_output(2, T0_LRU_OUT)
            sum_input(3, T0_LRU_OUT)
            ffn_in(1)

        @block.tensor
        def _(pe):
            def three(o, w_h, w_l, x_h, x_l, start, stop):
                pe.matmul(o, w_h, x_h, start=start, stop=False)
                pe.matmul(o, w_h, x_l, start=False, stop=False)
                return pe.matmul(o, w_l, x_h, start=False, stop=stop)

            def chunk(c, banks, xh, xl, k0, t0, first=True, last=True, need=None, i=0, stat=None, stat_k=KC - 1,
                      bank3=None):
                s = c % 2
                for k in range(KC):
                    if k % 2 == 0:
                        pe.wait_ge(wlo_made, SUB * c + k // 2 + 1 + 2 * SUB * i)
                    if need:
                        need(k0 + k)
                    if stat and k == stat_k:
                        stat()
                    for n in range(4):
                        if bank3 and k == 0 and n == 3:
                            bank3()
                        col = slice(n * P, (n + 1) * P)
                        mm = three(ps[:, banks + n, t0:T], w_hi[s][:, k, col], w_lo[s][:, k, col],
                                   xh[:, k0 + k, t0:T], xl[:, k0 + k, t0:T],
                                   first and k == 0, last and k == KC - 1)
                    if k % 2 == 1:
                        mm.then_inc(w_used, 1)

            def normed(i):
                return lambda k: pe.wait_ge(alo_made, i * DT + k + 1)

            def mean_input(i, t0):
                def issue():
                    pe.wait_ge(sum_h, i + 1)
                    pe.matmul(ps[:, STAT_IN, t0:T], ones_sb[:, 0, :], sq_sum[:, t0:T], start=True,
                              stop=True).then_inc(ms_up, 1)
                return issue

            def stat_in_read(i):
                return lambda: pe.wait_ge(rs_made, ESTIMATE[("pre", i)])

            def mean_part(i, t0, dt, start=False):
                if start:
                    pe.wait_ge(m_scaled, 2 * i + 1)
                if dt is None:
                    pe.wait_ge(sum_m, i + 1)
                else:
                    pe.wait_ge(m_sq, i * DT + dt + 1)
                mm = pe.matmul(ps[:, STAT, t0:T], ones_sb[:, 0, :],
                               sq_sum[:, t0:T] if dt is None else sq[:, dt, t0:T], start=start, stop=dt == DT - 1)
                if dt == DT - 1:
                    mm.then_inc(ms_up, 1)

            def keep_clock():
                for _ in range(30):
                    pe.matmul(ps[:, STAT + 1, 0:T], y_hi[:, 0, 0:P], y_hi[:, 1, :], start=True, stop=True)

            def staggered(c, i, k0):
                pe.wait_ge(wlo_made, SUB * (c + 1))
                for n in range(4):
                    col = slice(n * P, (n + 1) * P)
                    for k in range(KC):
                        mm = three(ps[:, Y + n, 0:T], w_hi[c % 2][:, k, col], w_lo[c % 2][:, k, col],
                                   y_hi[:, k0 + k, 0:T], y_lo[:, k0 + k, 0:T], False, k == KC - 1)
                    mm.then_inc(w_used, 1)
                    if n == 1:
                        mean_part(i, 0, None, start=True)
                    if n:
                        mean_part(i, 0, 4 + n - 1)
                mean_part(i, 0, DT - 1)
                keep_clock()

            pe.wait_ge(x_landed, 5 * 16)
            pe.wait_ge(gain_landed, 16)
            pe.transpose(ps[:, GAINS, 0:8 * DT], prow[0:8 * DT, 0, :],
                         ident_sb[0:8 * DT, 0:8 * DT]).then_inc(gain_up, 1)
            for dt in range(DT):
                if dt == GAINS:
                    pe.wait_ge(gain_ready, 1)
                for n, (t0, t) in enumerate(TOK_TILES):
                    mm = pe.transpose(ps[:, dt, t0:t0 + t], x_in[0:t, n, dt * P:(dt + 1) * P],
                                      ident_sb[0:t, 0:t])
                mm.then_inc(xT_up, 1)
            pe.wait_ge(h_in, 1)
            for _ in range(6):
                pe.transpose(ps[:, 0, 0:P], ident_sb[:], ident_sb[:])
            pe.wait_ge(const_landed, 16)

            def head_norm(h, bank):
                pe.wait_ge(sum_o, h + 1)
                pe.matmul(ps[:, bank, 0:T], ones_sb[:, 1, :], osq[:, 0, :], start=True,
                          stop=True).then_inc(gn_up, 1)

            def head_norm_read(h):
                return lambda: pe.wait_ge(rs_made, ESTIMATE[("head", h)])

            for h in range(HEADS):
                c = RET_IN[h]
                if h:
                    pe.wait_ge(g_out, h)
                    chunk(c, X, a_hi, a_lo, 0, 0)
                    pe.wait_ge(o_sq, h)
                    chunk(c + 1, Y, a_hi, a_lo, 0, 0)
                else:
                    chunk(c, X, a_hi, a_lo, 0, 0, need=normed(0), stat=mean_input(0, 0))
                    chunk(c + 1, Y, a_hi, a_lo, 0, 0, bank3=stat_in_read(0))
                pe.wait_ge(rot_done, h + 1)
                if h:
                    head_norm(h - 1, GN)
                pe.wait_ge(qklo_made, h + 1)
                for n, (m0, m) in enumerate(TOK_TILES):
                    for k in range(2):
                        key = slice(m0, m0 + m)
                        mm = three(ps[0:m, X + n, 0:T], qk_hi[:, 2 + k, key], qk_lo[:, 2 + k, key],
                                   qk_hi[:, k, :], qk_lo[:, k, :], k == 0, k == 1)
                mm.then_inc(s_up, 1)
                pe.wait_ge(v_out, h + 1)
                for n, (m0, m) in enumerate(TOK_TILES):
                    for e in range(4):
                        mm = pe.transpose(ps[0:m, Y + n, e * P:(e + 1) * P], vT[:, e, m0:m0 + m], ident_sb[:])
                mm.then_inc(vt_up, 1)
                if h == 0:
                    pe.wait_ge(par_landed, 16 * len(param_loads))
                    for t in range(1, 6):
                        rows = PAR_ROWS[t]
                        mm = pe.transpose(ps[:, PARAMS, PAR_COL[t]:PAR_COL[t] + rows], prow[0:rows, t, :],
                                          ident_sb[0:rows, 0:rows])
                    mm.then_inc(par_up, 1)
                pe.wait_ge(s_dec, h + 1)
                chunk(c + 2, X, a_hi, a_lo, 0, 0, bank3=head_norm_read(h - 1) if h else None)
                pe.wait_ge(vs_out, NTT * (h + 1))
                pe.wait_ge(vlo_made, h + 1)
                pe.wait_ge(slo_made, h + 1)
                if h == 0:
                    pe.wait_ge(par_raw, 1)
                for e in range(4):
                    col = slice(e * P, (e + 1) * P)
                    for n in range(2):
                        three(ps[:, Y + e, 0:T], v_hi[:, n, col], v_lo[:, n, col], s_hi[:, n, :], s_lo[:, n, :],
                              n == 0, False)
                    mm = pe.matmul(ps[:, Y + e, 0:T], v_hi[0:R_LO + META, 2, col], s_hi[0:R_LO + META, 2, :],
                                   start=False, stop=True)
                mm.then_inc(o_up, 1)

            def heads(k):
                pe.wait_ge(ylo_made, k // 4 + 1)

            c = RET_OUT
            pe.wait_ge(g_out, HEADS)
            chunk(c, X, y_hi, y_lo, 0, 0, last=False, need=heads, stat=lambda: head_norm(HEADS - 1, Y),
                  stat_k=6)
            chunk(c + 1, X, y_hi, y_lo, KC, 0, first=False, need=heads)
            chunk(c + 2, Y, y_hi, y_lo, 0, 0, last=False)
            staggered(c + 3, 0, KC)

            def ffn_in(layer, first_in, i_sub):
                t0 = ffn_first(layer)
                chunk(first_in, X, a_hi, a_lo, 0, t0, need=normed(i_sub), stat=mean_input(i_sub, t0))
                chunk(first_in + 1, Y, a_hi, a_lo, 0, t0, bank3=stat_in_read(i_sub))
                with pe.Fori(1, FFN_CHUNKS // 2) as i:
                    for b in range(2):
                        pe.wait_ge(u_out, layer * FFN_CHUNKS + b - 1 + 2 * i)
                        chunk(first_in + b, (X, Y)[b], a_hi, a_lo, 0, t0, i=i)

            def gated(layer):
                return lambda k: pe.wait_ge(fylo_made, layer * FFN_CHUNKS + k // 2 + 1)

            ffn_in(0, FFN0_IN, 1)
            for n in range(2 * FFN_OUT_K - 1):
                half, kg = divmod(n, FFN_OUT_K)
                if kg == 0:
                    pe.wait_ge(u_out, FFN_CHUNKS - 1 + half)
                chunk(ffn_out(0, n), (X, Y)[half], y_hi, y_lo, kg * KC, 0, kg == 0, kg == FFN_OUT_K - 1,
                      need=gated(0) if half == 0 else None)
            staggered(ffn_out(0, 2 * FFN_OUT_K - 1), 1, (FFN_OUT_K - 1) * KC)

            def lru_gates(k, free):
                wh, wl = [v[k].rearrange("p (q g k e) -> p q g k e", q=4, g=2, k=2) for v in (gw_hi, gw_lo)]
                for q in range(4):
                    b2 = 2 * (q // 2)
                    s = GATE_SET[4 * k + q]
                    signal, n = free[q]
                    pe.wait_ge(signal, n)
                    for g in range(2):
                        for m in range(2):
                            for kk in range(2):
                                col = slice(m * P, (m + 1) * P)
                                mm = three(ps[:, s + 2 * g + m, 0:T], wh[:, q, g, kk, col],
                                           wl[:, q, g, kk, col], xc_hi[k][:, b2 + kk, :],
                                           xc_lo[k][:, b2 + kk, :], kk == 0, kk == 1)
                    mm.then_inc(gates_up, 1)

            chunk(XR0, X, a_hi, a_lo, 0, 0, need=normed(2), stat=mean_input(2, 0))
            chunk(XR1, Y, a_hi, a_lo, 0, 0, bank3=stat_in_read(2))
            pe.wait_ge(xlo_made, 1)
            lru_gates(0, [(x_out, 1), (x_out, 2), (r_out, 1), (r_out, 2)])
            pe.wait_ge(r_out, 3)
            chunk(GT0, X, a_hi, a_lo, 0, T0_LRU_OUT)
            pe.wait_ge(xlo_made, 2)
            lru_gates(1, [(r_out, 4), (gt_out, 1), (r_out, 5), (r_out, 6)])
            pe.wait_ge(r_out, 7)
            chunk(GT1, Y, a_hi, a_lo, 0, T0_LRU_OUT)
            pe.wait_ge(r_out, 8)
            for blk in range(LRU_BLOCKS):
                c = LRU_OUT + blk // 2
                pe.wait_ge(ylo_made, HEADS + blk + 1)
                for half in range(2):
                    q = 2 * (blk % 2) + half
                    if (blk, half) == (0, 1):
                        pe.wait_ge(gt_out, 2)
                    pe.wait_ge(wlo_made, SUB * c + q + 1)
                    for m in range(4):
                        col = slice(m * P, (m + 1) * P)
                        for kk in range(2):
                            k = 2 * blk + kk
                            mm = three(ps[:, (X, Y)[half] + m, T0_LRU_OUT:T], w_hi[c % 2][:, 2 * q + kk, col],
                                       w_lo[c % 2][:, 2 * q + kk, col], y_hi[:, k, T0_LRU_OUT:T],
                                       y_lo[:, k, T0_LRU_OUT:T], k == 0, k == DT - 1)
                        if (blk, half) == (LRU_BLOCKS - 1, 1) and m < 3:
                            mm.then_inc(bank_up, 1)
                    mm.then_inc(w_used, 1)
            for dt in (4, 5, 6, None, 7):
                mean_part(2, T0_LRU_OUT, dt, start=dt == 4)
            keep_clock()

            ffn_in(1, FFN1_IN, 3)
            def residual_rows(half_set):
                for b in (2 * half_set, 2 * half_set + 1):
                    tt, half = b // 2, b % 2
                    for n in range(4):
                        t0 = META + tt * P
                        mm = pe.transpose(ps[:, H_ROW[b], n * P:(n + 1) * P], hT[:, half * 4 + n, t0:t0 + P],
                                          ident_sb[:])
                mm.then_inc(hrow_up, 1)

            pe.wait_ge(u_out, 2 * FFN_CHUNKS - 1)
            residual_rows(0)
            def tokens(tt, half, k, wh, wl):
                tok = slice(META + tt * P, META + (tt + 1) * P)
                yh, yl, o = y_hi[:, k, tok], y_lo[:, k, tok], ps[:, (X, Y)[half] + tt, :]
                pe.matmul(o, yh, wh, start=k == 0, stop=False)
                pe.matmul(o, yh, wl, start=False, stop=False)
                return pe.matmul(o, yl, wh, start=False, stop=k == FT - 1)

            for n in range(2 * FFN_OUT_K - 1):
                c, (half, kg) = FFN1_OUT + n, divmod(n, FFN_OUT_K)
                for k in range(KC):
                    if k % 2 == 0:
                        pe.wait_ge(wlo_made, SUB * c + k // 2 + 1)
                    if half == 0:
                        gated(1)(kg * KC + k)
                    wh, wl = w_hi[c % 2][:, k, :], w_lo[c % 2][:, k, :]
                    for tt in range(2):
                        mm = tokens(tt, half, kg * KC + k, wh, wl)
                    if k % 2 == 1:
                        mm.then_inc(w_used, 1)
                if n == 0:
                    pe.wait_ge(u_out, 2 * FFN_CHUNKS)
                    residual_rows(1)
            c = CHUNKS - 1
            pe.wait_ge(wlo_made, SUB * CHUNKS)
            for tt in range(2):
                for k in range(KC):
                    mm = tokens(tt, 1, (FFN_OUT_K - 1) * KC + k, w_hi[c % 2][:, k, :], w_lo[c % 2][:, k, :])
                    if (tt, k) in ((0, 7), (1, 3), (1, 5), (1, 7)):
                        mm.then_inc(w_used, 1)


_INS = ["x", "meta_tokens", "norm_gains", "ret_w_in", "ret_w_out", "lru_w_in", "lru_conv_w", "lru_conv_b",
        "lru_w_a", "lru_b_a", "lru_w_i", "lru_b_i", "lru_lambda", "lru_w_out", "ffn_w_in", "ffn_conv_w",
        "ffn_conv_b", "ffn_w_out"]


def constants():
    ident = np.eye(P, dtype=np.float32)
    ones = np.empty((P, 2, P), np.float32)
    ones[:, 0] = 1.0 / D
    ones[:, 1] = 1.0 / HEAD_V
    d = D // HEADS
    inv = np.float32(10000.0) ** (-np.arange(0, d, 2, dtype=np.float32) / np.float32(d))
    ang = np.arange(T, dtype=np.float32)[None, :] * inv[:, None]
    rope = np.stack([np.cos(ang), np.sin(ang)], 1).astype(np.float32) * np.float32(-0.5 * UNSCALE * A_SCALE)
    away = np.abs(np.arange(DECAY_W)[None, :] - 2 * P - np.arange(P)[:, None]).astype(np.float64)
    log_gamma = np.log1p(-np.exp2(-5.0 - np.arange(HEADS)))
    decay = np.exp(log_gamma[None, :, None] * away[:, None, :]) * d ** -0.5 / A_SCALE
    return {"ident": ident, "ones": ones, "rope": rope, "decay": decay.astype(np.float32)}


def kernel(**inputs):
    import concourse.bacc as bacc
    from concourse.bass_utils import run_bass_kernel_spmd

    nc = bacc.Bacc("TRN2", target_bir_lowering=False, num_devices=1)
    arrays, args = {}, []
    named = {name: np.ascontiguousarray(inputs[name]) for name in _INS} | constants()
    for name, a in named.items():
        arrays[f"in_{name}"] = a
        args.append(nc.dram_tensor(f"in_{name}", a.shape, mybir.dt.from_np(a.dtype), kind="ExternalInput").ap())
    args.append(nc.dram_tensor("out", (1, SEQ, D), F32, kind="ExternalOutput").ap())
    build(nc, *args)
    r = run_bass_kernel_spmd(nc, [arrays], core_ids=[0])
    return r.results[0]["out"]
```
